# Optimizing a Trainium2 kernel written in Bass

```python
import math
import jax
import jax.numpy as jnp
from jax import lax
import numpy as np

D_MODEL = 1024
BATCH = 1
SEQ = 256
DEPTH = 2
DEC_BATCH = 8
DEC_SEQ = 8
PAST_LEN = 1024
PAGE_SIZE = 128

H_A = 4
DK_A = 64
DV_A = 128
RET_CHUNK = 128
H_B = 4
DH_B = 64
DIL_PATTERNS = ((128, 1), (512, 4), (2048, 16))
WIN_MAX = 2048
H_C = 4
DQK_C = 32
DV_C = 64
H_X = 4
DH_X = D_MODEL // H_X
N_MEM = 256
D_FF = 2816
N_BUCKETS = 32
MAX_DISTANCE = 128
BLOCK = 128
ROPE_BASE = 10000.0
LN_EPS = 1e-5
RMS_EPS = 1e-6
NEG_INF = -1e30
DEEPNORM_ALPHA = (2 * DEPTH) ** 0.25
DEEPNORM_BETA = (8 * DEPTH) ** -0.25
IN_SPLITS = (H_A * DK_A, H_A * DK_A, H_A * DV_A, H_A * DV_A, H_B * DH_B, H_B * DH_B, H_B * DH_B, H_C * 2 * DQK_C, H_C * 2 * DQK_C, H_C * DV_C)
D_IN = sum(IN_SPLITS)
D_MIX = H_A * DV_A + H_B * DH_B + H_C * DV_C

kernel_name = "hybrid_ret_dilated_diff_step"

def layer_norm(x, g, b):
    xf = x.astype(jnp.float32)
    mu = jnp.mean(xf, -1, keepdims=True)
    var = jnp.mean(jnp.square(xf - mu), -1, keepdims=True)
    y = (xf - mu) * lax.rsqrt(var + LN_EPS)
    return (y * g.astype(jnp.float32) + b.astype(jnp.float32)).astype(x.dtype)

def rms_norm(x, g=None):
    xf = x.astype(jnp.float32)
    y = xf * lax.rsqrt(jnp.mean(jnp.square(xf), -1, keepdims=True) + RMS_EPS)
    if g is not None:
        y = y * g.astype(jnp.float32)
    return y

def t5_bucket(dist):
    n = jnp.maximum(dist, 0)
    max_exact = N_BUCKETS // 2
    nf = jnp.maximum(n, 1).astype(jnp.float32)
    large = max_exact + (jnp.log(nf / max_exact) / math.log(MAX_DISTANCE / max_exact) * (N_BUCKETS - max_exact)).astype(jnp.int32)
    large = jnp.minimum(large, N_BUCKETS - 1)
    return jnp.where(n < max_exact, n, large)

def rope(x, pos):
    half = x.shape[-1] // 2
    inv = ROPE_BASE ** (-jnp.arange(half, dtype=jnp.float32) / half)
    ang = pos.astype(jnp.float32)[:, None] * inv[None]
    cos = jnp.cos(ang)[None, :, None, :]
    sin = jnp.sin(ang)[None, :, None, :]
    xf = x.astype(jnp.float32)
    x1, x2 = xf[..., :half], xf[..., half:]
    return jnp.concatenate([x1 * cos - x2 * sin, x1 * sin + x2 * cos], -1)

def softmax_stats(s):
    m = jnp.max(s, -1, keepdims=True)
    p = jnp.exp(s - m)
    den = jnp.sum(p, -1, keepdims=True)
    return p / den, (m + jnp.log(den))[..., 0]

def swiglu(h, w_in, w_out):
    a, b = jnp.split(h @ w_in, 2, axis=-1)
    return (jax.nn.silu(a) * b) @ w_out

def ffn_sublayer(x, w_in, w_out, g, b):
    return layer_norm(DEEPNORM_ALPHA * x + 0.5 * swiglu(x, w_in, w_out), g, b)

def project_mixers(h, w):
    B, T, _ = h.shape
    pts, acc = [], 0
    for wd in IN_SPLITS[:-1]:
        acc += wd
        pts.append(acc)
    aq, ak, av, ag, bq, bk, bv, cq, ck, cv = jnp.split(h @ w, pts, axis=-1)
    return (aq.reshape(B, T, H_A, DK_A), ak.reshape(B, T, H_A, DK_A), av.reshape(B, T, H_A, DV_A), ag,
            bq.reshape(B, T, H_B, DH_B), bk.reshape(B, T, H_B, DH_B), bv.reshape(B, T, H_B, DH_B),
            cq.reshape(B, T, H_C, 2, DQK_C), ck.reshape(B, T, H_C, 2, DQK_C), cv.reshape(B, T, H_C, DV_C))

def retention(q, k, v, state0, pos, chunk):
    B, T = q.shape[:2]
    qf = rope(q, pos)
    kf = rope(k, pos) * DK_A ** -0.5
    vf = v.astype(jnp.float32)
    log_g = jnp.log1p(-jnp.exp2(-5.0 - jnp.arange(H_A, dtype=jnp.float32)))
    idx = jnp.arange(chunk, dtype=jnp.float32)
    rel = idx[:, None] - idx[None, :]
    decay_mask = jnp.where(rel >= 0, jnp.exp(log_g[:, None, None] * jnp.maximum(rel, 0.0)), 0.0)
    q_decay = jnp.exp(log_g[None, :] * (idx + 1.0)[:, None])[None, :, :, None]
    k_decay = jnp.exp(log_g[None, :] * (chunk - 1.0 - idx)[:, None])[None, :, :, None]
    chunk_decay = jnp.exp(log_g * chunk)[None, :, None, None]
    n = T // chunk

    def to_chunks(a):
        return a.reshape(B, n, chunk, *a.shape[2:]).swapaxes(0, 1)

    def step(S, inp):
        qc, kc, vc = inp
        scores = jnp.einsum('bihd,bjhd->bhij', qc, kc) * decay_mask[None]
        inner = jnp.einsum('bhij,bjhe->bihe', scores, vc)
        cross = jnp.einsum('bihd,bhde->bihe', qc, S) * q_decay
        S_new = S * chunk_decay + jnp.einsum('bjhd,bjhe->bhde', kc * k_decay, vc)
        return S_new, inner + cross

    S_fin, outs = lax.scan(step, state0.astype(jnp.float32), (to_chunks(qf), to_chunks(kf), to_chunks(vf)))
    o = outs.swapaxes(0, 1).reshape(B, T, H_A, DV_A)
    return o, S_fin.astype(state0.dtype)

def banded_attention(q, k, v, wl, dil, bias_tab):
    N, n, H, dh = q.shape
    nb = -(-n // BLOCK)
    pad = nb * BLOCK - n

    def blocks(a):
        return jnp.pad(a, ((0, 0), (0, pad), (0, 0), (0, 0))).reshape(N, nb, BLOCK, H, dh)

    def with_prev(a):
        prev = jnp.pad(a, ((0, 0), (1, 0), (0, 0), (0, 0), (0, 0)))[:, :-1]
        return jnp.concatenate([prev, a], axis=2)

    qb = blocks(q)
    kk = with_prev(blocks(k))
    vv = with_prev(blocks(v))
    s = jnp.einsum('nbihd,nbjhd->nbhij', qb, kk).astype(jnp.float32) * dh ** -0.5
    qi = jnp.arange(BLOCK)[:, None] + BLOCK
    kj = jnp.arange(2 * BLOCK)[None, :]
    local = qi - kj
    bias = jnp.moveaxis(bias_tab[t5_bucket(local * dil)].astype(jnp.float32), -1, 0)
    kpos = jnp.arange(nb)[:, None] * BLOCK + kj - BLOCK
    valid = ((local >= 0) & (local <= wl))[None] & (kpos >= 0)[:, None, :]
    s = jnp.where(valid[None, :, None], s + bias[None, None], NEG_INF)
    p, lse = softmax_stats(s)
    o = jnp.einsum('nbhij,nbjhd->nbihd', p, vv.astype(jnp.float32)).reshape(N, nb * BLOCK, H, dh)[:, :n]
    lse = jnp.swapaxes(lse, 2, 3).reshape(N, nb * BLOCK, H)[:, :n]
    return o, lse

def res_split(a, dil):
    B, S = a.shape[:2]
    rest = a.shape[2:]
    return a.reshape(B, S // dil, dil, *rest).swapaxes(1, 2).reshape(B * dil, S // dil, *rest)

def res_merge(a, B, dil):
    n = a.shape[1]
    rest = a.shape[2:]
    return a.reshape(B, dil, n, *rest).swapaxes(1, 2).reshape(B, n * dil, *rest)

def combine_by_denominator(outs, lses):
    w = jax.nn.softmax(jnp.stack(lses, 0), axis=0)
    return jnp.sum(w[..., None] * jnp.stack(outs, 0), axis=0)

def dilated_prompt(q, k, v, bias_b):
    B = q.shape[0]
    outs, lses = [], []
    for win, dil in DIL_PATTERNS:
        o, lse = banded_attention(res_split(q, dil), res_split(k, dil), res_split(v, dil), win // dil, dil, bias_b)
        outs.append(res_merge(o, B, dil))
        lses.append(res_merge(lse, B, dil))
    return combine_by_denominator(outs, lses)

def dilated_sample(q, k_new, v_new, k_buf, v_buf, bias_b):
    T = q.shape[1]
    dh = q.shape[-1]
    L = k_buf.shape[1]
    k_all = jnp.concatenate([k_buf, k_new], 1)
    v_all = jnp.concatenate([v_buf, v_new], 1)
    qi = jnp.arange(T)
    outs, lses = [], []
    for win, dil in DIL_PATTERNS:
        dist = jnp.arange(win // dil + 1) * dil
        rows = L + qi[:, None] - dist[None]
        valid = rows >= 0
        rows_c = jnp.maximum(rows, 0)
        kg = k_all[:, rows_c]
        vg = v_all[:, rows_c]
        s = jnp.einsum('bthd,btjhd->bthj', q, kg).astype(jnp.float32) * dh ** -0.5
        s = s + bias_b[t5_bucket(dist)].astype(jnp.float32).T[None, None]
        s = jnp.where(valid[None, :, None, :], s, NEG_INF)
        p, lse = softmax_stats(s)
        outs.append(jnp.einsum('bthj,btjhd->bthd', p, vg.astype(jnp.float32)))
        lses.append(lse)
    return combine_by_denominator(outs, lses)

def diff_lambda_value(lp, lam_init):
    lpf = lp.astype(jnp.float32)
    return jnp.exp(jnp.sum(lpf[0] * lpf[1])) - jnp.exp(jnp.sum(lpf[2] * lpf[3])) + lam_init

def diff_attend(q, k, v, qpos, kpos, bias_c, lam):
    s = jnp.einsum('bqhmd,bkhmd->bhmqk', q, k).astype(jnp.float32) * DQK_C ** -0.5
    dist = qpos[:, None] - kpos[None, :]
    bias = jnp.moveaxis(bias_c[t5_bucket(dist)].astype(jnp.float32), -1, 0)
    s = jnp.where((dist >= 0)[None, None, None], s + bias[None, :, None], NEG_INF)
    p = jax.nn.softmax(s, axis=-1)
    attn = p[:, :, 0] - lam * p[:, :, 1]
    return jnp.einsum('bhqk,bkhe->bqhe', attn, v.astype(jnp.float32))

def diff_prompt(q, k, v, bias_c, lam):
    B, S = q.shape[:2]
    nb = S // BLOCK
    qb = q.reshape(B, nb, BLOCK, H_C, 2, DQK_C).swapaxes(0, 1)
    starts = jnp.arange(nb) * BLOCK
    kpos = jnp.arange(S)

    def one_block(args):
        qblk, s0 = args
        return diff_attend(qblk, k, v, s0 + jnp.arange(BLOCK), kpos, bias_c, lam)

    o = lax.map(one_block, (qb, starts))
    return o.swapaxes(0, 1).reshape(B, S, H_C, DV_C)

def mixer_merge(x, o_a, g_a, o_b, o_c, lam_init, subln_g, w_out, g, b):
    B, T = x.shape[:2]
    ya = rms_norm(o_a).reshape(B, T, H_A * DV_A) * jax.nn.silu(g_a.astype(jnp.float32))
    yc = rms_norm(o_c, subln_g) * (1.0 - lam_init)
    y = jnp.concatenate([ya, o_b.reshape(B, T, H_B * DH_B), yc.reshape(B, T, H_C * DV_C)], -1).astype(x.dtype)
    return layer_norm(DEEPNORM_ALPHA * x + y @ w_out, g, b)

def cross_sublayer(x, mk, mv, w_q, w_o, g, b):
    B, T, _ = x.shape
    q = (x @ w_q).reshape(B, T, H_X, DH_X)
    s = jnp.einsum('bthd,bmhd->bhtm', q, mk).astype(jnp.float32) * DH_X ** -0.5
    p = jax.nn.softmax(s, axis=-1)
    o = jnp.einsum('bhtm,bmhd->bthd', p, mv.astype(jnp.float32)).reshape(B, T, D_MODEL).astype(x.dtype)
    return layer_norm(DEEPNORM_ALPHA * x + o @ w_o, g, b)

def prompt_trunk(x, mem, w_in, w_out, diff_lambda, diff_subln_g, rel_bias, w_xq, w_xk, w_xv, w_xo, ffn1_in, ffn1_out, ffn2_in, ffn2_out, ln_g, ln_b):
    B, S, _ = x.shape
    pos = jnp.arange(S)
    lw = min(WIN_MAX, S)
    dk_l, dv_l, wk_l, wv_l, ret_l, mk_l, mv_l = [], [], [], [], [], [], []
    for l in range(DEPTH):
        lam_init = 0.8 - 0.6 * math.exp(-0.3 * l)
        x = ffn_sublayer(x, ffn1_in[l], ffn1_out[l], ln_g[l, 0], ln_b[l, 0])
        aq, ak, av, ag, bq, bk, bv, cq, ck, cv = project_mixers(x, w_in[l])
        o_a, st = retention(aq, ak, av, jnp.zeros((B, H_A, DK_A, DV_A), x.dtype), pos, min(RET_CHUNK, S))
        o_b = dilated_prompt(bq, bk, bv, rel_bias[:, :H_B])
        lam = diff_lambda_value(diff_lambda[l], lam_init)
        o_c = diff_prompt(cq, ck, cv, rel_bias[:, H_B:], lam)
        x = mixer_merge(x, o_a, ag, o_b, o_c, lam_init, diff_subln_g[l], w_out[l], ln_g[l, 1], ln_b[l, 1])
        mk = (mem @ w_xk[l]).reshape(B, N_MEM, H_X, DH_X)
        mv = (mem @ w_xv[l]).reshape(B, N_MEM, H_X, DH_X)
        x = cross_sublayer(x, mk, mv, w_xq[l], w_xo[l], ln_g[l, 2], ln_b[l, 2])
        x = ffn_sublayer(x, ffn2_in[l], ffn2_out[l], ln_g[l, 3], ln_b[l, 3])
        dk_l.append(ck.reshape(B, S, H_C, 2 * DQK_C))
        dv_l.append(cv)
        wk_l.append(bk[:, S - lw:])
        wv_l.append(bv[:, S - lw:])
        ret_l.append(st)
        mk_l.append(mk)
        mv_l.append(mv)
    st = lambda a: jnp.stack(a, axis=1)
    return x, st(dk_l), st(dv_l), st(wk_l), st(wv_l), st(ret_l), st(mk_l), st(mv_l)

def sample_trunk(x, cache_diff_k, cache_diff_v, cache_win_k, cache_win_v, state_ret, cache_mem_k, cache_mem_v, page_table, w_in, w_out, diff_lambda, diff_subln_g, rel_bias, w_xq, w_xo, ffn1_in, ffn1_out, ffn2_in, ffn2_out, ln_g, ln_b):
    Bd, T, _ = x.shape
    past_len = page_table.shape[1] * cache_diff_k.shape[2]
    pos = past_len + jnp.arange(T)
    kpos = jnp.arange(past_len + T)
    dk_l, dv_l, wk_l, wv_l, ret_l = [], [], [], [], []
    for l in range(DEPTH):
        lam_init = 0.8 - 0.6 * math.exp(-0.3 * l)
        x = ffn_sublayer(x, ffn1_in[l], ffn1_out[l], ln_g[l, 0], ln_b[l, 0])
        aq, ak, av, ag, bq, bk, bv, cq, ck, cv = project_mixers(x, w_in[l])
        o_a, st = retention(aq, ak, av, state_ret[:, l], pos, T)
        o_b = dilated_sample(bq, bk, bv, cache_win_k[:, l], cache_win_v[:, l], rel_bias[:, :H_B])
        past_k = cache_diff_k[page_table, l].reshape(Bd, past_len, H_C, 2, DQK_C)
        past_v = cache_diff_v[page_table, l].reshape(Bd, past_len, H_C, DV_C)
        k_all = jnp.concatenate([past_k, ck.astype(past_k.dtype)], 1)
        v_all = jnp.concatenate([past_v, cv.astype(past_v.dtype)], 1)
        lam = diff_lambda_value(diff_lambda[l], lam_init)
        o_c = diff_attend(cq, k_all, v_all, pos, kpos, rel_bias[:, H_B:], lam)
        x = mixer_merge(x, o_a, ag, o_b, o_c, lam_init, diff_subln_g[l], w_out[l], ln_g[l, 1], ln_b[l, 1])
        x = cross_sublayer(x, cache_mem_k[:, l], cache_mem_v[:, l], w_xq[l], w_xo[l], ln_g[l, 2], ln_b[l, 2])
        x = ffn_sublayer(x, ffn2_in[l], ffn2_out[l], ln_g[l, 3], ln_b[l, 3])
        dk_l.append(ck.reshape(Bd, T, H_C, 2 * DQK_C))
        dv_l.append(cv)
        wk_l.append(bk)
        wv_l.append(bv)
        ret_l.append(st)
    st = lambda a: jnp.stack(a, axis=1)
    return x, st(dk_l), st(dv_l), st(wk_l), st(wv_l), st(ret_l)

def setup_inputs(seed: int = 0) -> dict:
    key = jax.random.key(seed)
    ks = jax.random.split(key, 28)
    f32 = jnp.float32
    n_pages = PAST_LEN // PAGE_SIZE
    n_used = DEC_BATCH * n_pages
    n_phys = n_used + max(1, n_used // 4)
    l_win = min(WIN_MAX, PAST_LEN)

    def nrm(k, shape, scale=1.0):
        return jax.random.normal(k, shape, f32) * scale

    page_table = jax.random.permutation(ks[0], n_phys)[:n_used].reshape(DEC_BATCH, n_pages).astype(jnp.int32)
    return {
        "x_prompt": nrm(ks[1], (BATCH, SEQ, D_MODEL)),
        "x_sample": nrm(ks[2], (DEC_BATCH, DEC_SEQ, D_MODEL)),
        "mem_prompt": nrm(ks[3], (BATCH, N_MEM, D_MODEL)),
        "cache_diff_k": nrm(ks[4], (n_phys, DEPTH, PAGE_SIZE, H_C, 2 * DQK_C)),
        "cache_diff_v": nrm(ks[5], (n_phys, DEPTH, PAGE_SIZE, H_C, DV_C)),
        "cache_win_k": nrm(ks[6], (DEC_BATCH, DEPTH, l_win, H_B, DH_B)),
        "cache_win_v": nrm(ks[7], (DEC_BATCH, DEPTH, l_win, H_B, DH_B)),
        "state_ret": nrm(ks[8], (DEC_BATCH, DEPTH, H_A, DK_A, DV_A)),
        "cache_mem_k": nrm(ks[9], (DEC_BATCH, DEPTH, N_MEM, H_X, DH_X)),
        "cache_mem_v": nrm(ks[10], (DEC_BATCH, DEPTH, N_MEM, H_X, DH_X)),
        "page_table": page_table,
        "w_in": nrm(ks[11], (DEPTH, D_MODEL, D_IN), D_MODEL ** -0.5),
        "w_out": nrm(ks[12], (DEPTH, D_MIX, D_MODEL), D_MIX ** -0.5 * DEEPNORM_BETA),
        "diff_lambda": nrm(ks[13], (DEPTH, 4, DQK_C), 0.1),
        "diff_subln_g": 1.0 + nrm(ks[14], (DEPTH, DV_C), 0.02),
        "rel_bias": nrm(ks[15], (N_BUCKETS, H_B + H_C), 0.5),
        "w_xq": nrm(ks[16], (DEPTH, D_MODEL, D_MODEL), D_MODEL ** -0.5),
        "w_xk": nrm(ks[17], (DEPTH, D_MODEL, D_MODEL), D_MODEL ** -0.5),
        "w_xv": nrm(ks[18], (DEPTH, D_MODEL, D_MODEL), D_MODEL ** -0.5),
        "w_xo": nrm(ks[19], (DEPTH, D_MODEL, D_MODEL), D_MODEL ** -0.5 * DEEPNORM_BETA),
        "ffn1_in": nrm(ks[20], (DEPTH, D_MODEL, 2 * D_FF), D_MODEL ** -0.5),
        "ffn1_out": nrm(ks[21], (DEPTH, D_FF, D_MODEL), D_FF ** -0.5 * DEEPNORM_BETA),
        "ffn2_in": nrm(ks[22], (DEPTH, D_MODEL, 2 * D_FF), D_MODEL ** -0.5),
        "ffn2_out": nrm(ks[23], (DEPTH, D_FF, D_MODEL), D_FF ** -0.5 * DEEPNORM_BETA),
        "ln_g": 1.0 + nrm(ks[24], (DEPTH, 4, D_MODEL), 0.02),
        "ln_b": nrm(ks[25], (DEPTH, 4, D_MODEL), 0.02),
    }

def reference(x_prompt, x_sample, mem_prompt, cache_diff_k, cache_diff_v, cache_win_k, cache_win_v, state_ret, cache_mem_k, cache_mem_v, page_table, w_in, w_out, diff_lambda, diff_subln_g, rel_bias, w_xq, w_xk, w_xv, w_xo, ffn1_in, ffn1_out, ffn2_in, ffn2_out, ln_g, ln_b):
    y_prompt, p_diff_k, p_diff_v, p_win_k, p_win_v, p_ret, p_mem_k, p_mem_v = prompt_trunk(
        x_prompt, mem_prompt, w_in, w_out, diff_lambda, diff_subln_g, rel_bias, w_xq, w_xk, w_xv, w_xo,
        ffn1_in, ffn1_out, ffn2_in, ffn2_out, ln_g, ln_b)
    y_sample, s_diff_k, s_diff_v, s_win_k, s_win_v, s_ret = sample_trunk(
        x_sample, cache_diff_k, cache_diff_v, cache_win_k, cache_win_v, state_ret, cache_mem_k, cache_mem_v,
        page_table, w_in, w_out, diff_lambda, diff_subln_g, rel_bias, w_xq, w_xo,
        ffn1_in, ffn1_out, ffn2_in, ffn2_out, ln_g, ln_b)
    return (y_prompt, y_sample, p_diff_k, p_diff_v, p_win_k, p_win_v, p_ret, p_mem_k, p_mem_v, s_diff_k, s_diff_v, s_win_k, s_win_v, s_ret)


_drawn_inputs = setup_inputs


def setup_inputs(seed=0):
    import zlib

    import numpy as np

    out = dict(_drawn_inputs(seed))
    spreads = {}
    factors = {'diff_lambda': 8.0, 'diff_subln_g': 8.0, 'cache_win_k': 3.247}
    for name, (base, spread) in spreads.items():
        noise = np.random.default_rng([zlib.crc32(name.encode()), seed]).standard_normal(out[name].shape)
        drawn = base * np.exp(spread * noise) if base else spread * noise
        out[name] = jnp.asarray(drawn.astype(out[name].dtype))
    for name, factor in factors.items():
        out[name] = (out[name] * factor).astype(out[name].dtype)
    return out
```

```python
import math
from contextlib import ExitStack

import numpy as np

import concourse.bass as bass
from concourse import mybir

F32 = mybir.dt.float32
I32 = mybir.dt.int32
ALU = mybir.AluOpType
ACT = mybir.ActivationFunctionType
AX = mybir.AxisListType

P = 128
D = 1024
KD = D // P
SEQ, DB, DT = 256, 8, 8
NS = DB * DT
T = SEQ + NS
L = 2
PAST, PAGE = 1024, 128
NPG = PAST // PAGE
F = 2816
NF = F // P
HX = 4
NH = 2 * HX
NBUCKET = 32
WK = 768
OFF = PAST + DT - 1
NU = 1288
ALPHA = (2 * L) ** 0.25
LN_EPS, RMS_EPS = 1e-5, 1e-6
NEG = -1e30
LOW = -3.0e38
XSCALE = 256.0 ** -0.5

RING = 4
SEGMENTS = [("w16", 22), ("w11", 16), ("w16", 32), ("w16", 22), ("w11", 16)]
SLOTS = sum(n for _, n in SEGMENTS)
POS_FFN1, POS_MIX, POS_FFN2 = 0, 38, 70
assert SLOTS % RING == 0

MIXER = [(k, i) for k in ("diff_dec", "win_dec", "win_pro", "diff_pro") for i in range(4)]
CROSS = [(k, i) for k in ("cross_dec", "cross_pro") for i in range(4)]
ITEMS = MIXER + CROSS
NI = len(ITEMS)
BATCHES = [3 if k == "diff_dec" else 1 for k, _ in ITEMS]
BEFORE = [sum(BATCHES[:i]) for i in range(NI)]
NB = sum(BATCHES)
LEAD = 1 + NI - (len(MIXER) + 4)


DVE_STEPS = 79
CHUNK_DECAY = [float(np.float32(np.exp(DT * np.log1p(-2.0 ** (-5.0 - h))))) for h in range(HX)]


class Signal:

    def __init__(self, sem, per_layer, first=0):
        self.sem, self.per_layer, self.first = sem, per_layer, first

    def upto(self, layer, n):
        return layer * self.per_layer + (self.first + n)


def view(ap, dims):
    ap = ap[:]
    return bass.AP(ap.tensor, ap.offset, [list(ap.ap[0])] + [list(d) for d in dims])


def build(nc, a, o):
    ctx = ExitStack()
    with ctx:
        def sb(name, shape, dt=F32):
            return ctx.enter_context(nc.sbuf_tensor(name, shape, dt))

        def sem(name):
            return ctx.enter_context(nc.semaphore(name))

        def signal(name, per_layer, first=0):
            return Signal(sem(name), per_layer, first)

        ring = sb("ring", [P, RING, 2048])
        cache = sb("cache", [P, 4, 2048])
        xT = sb("xT", [P, KD, T])
        yT = sb("yT", [P, KD, T])
        tok = sb("tok", [P, 3, 1024])
        hid = sb("hid", [P, NF, T])
        fm = sb("fm", [P, 8, T])
        arena = sb("arena", [P, 4480])
        qd = sb("qd", [P, 2, DB, 64])
        qw = sb("qw", [P, 2, DB, 32])
        s_dec = sb("s_dec", [P, 4, HX, P])
        s_pro = sb("s_pro", [64, HX, P])
        bias_pro = sb("bias_pro", [P, NH, 256])
        bias_dd = sb("bias_dd", [P, PAST])
        bias_dn = sb("bias_dn", [P, 4, NS])
        bias_wd = sb("bias_wd", [64, WK])
        bias_wn = sb("bias_wn", [64, 4, NS])
        decay = sb("decay", [P, HX, 256])
        decay_s = sb("decay_s", [NS, HX, NS])
        qdec = sb("qdec", [P, HX, 4, NS])
        kmask = sb("kmask", [NS, HX, DB])
        kdec = sb("kdec", [P, 2, HX])
        cos = sb("cos", [P, 3, 32])
        sin = sb("sin", [P, 3, 32])
        ident = sb("ident", [P, P])
        gate = sb("gate", [P, 2, T])
        params = sb("params", [P, L, 130])
        cur = sb("cur", [P, 130])
        subg = sb("subg", [P, L, 64])
        curg = sb("curg", [P, 64])
        stat = sb("stat", [P, 2, 16])
        small = sb("small", [P, 64])
        bn = sb("bn", [P, 3, 2, 6])
        mean_var = sb("mean_var", [P, 3, 2])
        lnst = sb("lnst", [P, 3, 3])
        pt = sb("pt", [1, DB * NPG], I32)
        ps = ctx.enter_context(nc.psum_tensor("ps", [P, 8, 512], F32))

        hflat = hid[:, :, :].rearrange("p a b -> p (a b)")
        def tmat(r0, r1, g, c, n):
            return hflat[r0:r1, 2048 * g + c:2048 * g + c + n]

        memT = hflat[:, 0:2048].rearrange("p (a b) -> p a b", a=KD)
        mkT = hflat[:, 2048:4096].rearrange("p (a b) -> p a b", a=KD)
        mvt = hflat[:, 4096:6144].rearrange("p (a b) -> p a b", a=2)
        tflat = tok[:, :, :].rearrange("p a b -> p (a b)")
        rp = [tflat[:, 768 * i:768 * (i + 1)].rearrange("p (g h d) -> p g h d", g=3, h=8) for i in range(4)]
        ytok = tflat[:, 0:2304].rearrange("p (g c) -> p g c", g=3)
        qc = tflat[:, 0:2048].rearrange("p (c b r) -> p c b r", c=KD, b=DB)
        prob = [arena[:, 0:1088], arena[:, 1088:2176]]
        pT = [arena[:, 2176:3328], arena[:, 3328:4480]]
        kd = arena[:, 0:512].rearrange("p (g h d) -> p g h d", g=2, h=HX)
        qTp = arena[:, 512:1024].rearrange("p (c t) -> p c t", c=2)
        kTp = arena[:, 1024:1536].rearrange("p (c t) -> p c t", c=2)
        qTs = arena[0:64, 1536:1792].rearrange("p (h t) -> p h t", h=HX)
        kTs = arena[0:64, 1792:2048].rearrange("p (h t) -> p h t", h=HX)
        qx = arena[:, 2048:3072].rearrange("p (h g t) -> p h g t", h=HX, g=4)
        aT = [arena[:, 3072:3456], arena[:, 3456:3840]]
        aTs = arena[0:NS, 3840:4096].rearrange("p (h t) -> p h t", h=HX)
        kx = fm[:, :, :].rearrange("p a b -> p (a b)")[0:NS, 0:2048].rearrange("p (h g d) -> p h g d", h=HX, g=DB)
        sq = fm[:, :, :].rearrange("p a b -> p (a b)")[:, 0:768]
        ocT = sb("ocT", [P, 2, NS])
        qxT = fm[:, :, 0:256]
        onehot = hflat[0:NBUCKET, 0:NU]
        counts = hflat[0:NH, 1288:1288 + NU]
        brow = hflat[0:NH, 2576:2576 + NU]
        hank_d = hflat[0:32, 3864:3864 + 1032]
        hank_w = hflat[0:32, 4896:4896 + 1032]
        rel = hflat[0:NBUCKET, 5928:5936]
        selJ = hflat[:, 5936:6064]
        sel_d = hflat[0:32, 6064:6192]
        sel_w = hflat[0:32, 6192:6256]
        mask_d = hflat[:, 6256:6288].rearrange("p (g b) -> p g b", g=4)
        mask_w = hflat[0:64, 6288:6320].rearrange("p (g b) -> p g b", g=4)
        lamv = hflat[:, 6320:6320 + 256].rearrange("p (l v d) -> p l v d", l=L, v=4)
        lamt = hflat[:, 6576:6576 + 128]
        lconst = hflat[:, 6704:6704 + 8]
        hank = tflat[:, 0:2048].rearrange("p (h c) -> p h c", h=NH)

        w_ready = [signal(f"w_ready{i}", 16 * SLOTS // RING) for i in range(RING)]
        w_used = signal("w_used", SLOTS, RING)
        k_ready = [signal(f"k_ready{i}", 16 * (4 * NPG + 8)) for i in range(2)]
        v_ready = [signal(f"v_ready{i}", 16 * (4 * NPG + 8)) for i in range(2)]
        const_in = sem("const_in")
        hank_in = sem("hank_in")
        brow_out = sem("brow_out")
        set_pe, set_act, set_dve = sem("set_pe"), sem("set_act"), sem("set_dve")
        dve_step = signal("dve_step", DVE_STEPS)
        own_set = sem("own_set")
        cur_done = signal("cur_done", 1)
        a_psum = signal("a_psum", 2 * NF)
        silu_done = signal("silu_done", 2 * NF)
        gate_done = signal("gate_done", 2 * NF, 2)
        out_psum = signal("out_psum", 8)
        res_done = signal("res_done", 32)
        tok_psum = signal("tok_psum", 8)
        var_done = signal("var_done", 4)
        sd_done = signal("sd_done", 4)
        par_done = signal("par_done", 4)
        norm_dve = signal("norm_dve", 4)
        norm_act = signal("norm_act", 4)
        xt_psum = signal("xt_psum", 32)
        x_act = signal("x_act", 16, 1)
        x_dve = signal("x_dve", 16, 1)
        fm_psum = signal("fm_psum", 4)
        fm_done = signal("fm_done", 8)
        tm_psum = signal("tm_psum", 8)
        tm_act = signal("tm_act", 3)
        tm_dve = signal("tm_dve", 9)
        q_built = signal("q_built", 1)
        s_psum = signal("s_psum", NI, LEAD)
        m_done = signal("m_done", NI)
        e_done = signal("e_done", NI)
        p_done = signal("p_done", NI)
        t_psum = signal("t_psum", NB)
        t_done = signal("t_done", NB)
        o_psum = signal("o_psum", NI, LEAD)
        o_done = signal("o_done", NI)
        rt_psum = signal("rt_psum", 4)
        rt_act = signal("rt_act", 2)
        rt_dve = signal("rt_dve", 2)
        k_decayed = signal("k_decayed", 1)
        ra_psum = signal("ra_psum", 5)
        ra_done = signal("ra_done", 5)
        ro_psum = signal("ro_psum", 2)
        st_in = signal("st_in", 16)
        st_psum = signal("st_psum", 5)
        st_act = signal("st_act", 1)
        st_dve = signal("st_dve", 4)
        oc_psum = signal("oc_psum", 1)
        rsq_done = signal("rsq_done", 1)
        rss_done = signal("rss_done", 1)
        rsd_done = signal("rsd_done", 1)
        y_done = signal("y_done", 1)
        y_psum = signal("y_psum", 6)
        y_act = signal("y_act", 6)
        mem_in = signal("mem_in", 16)
        mk_psum = signal("mk_psum", 4)
        mk_act = signal("mk_act", 8)
        mv_psum = signal("mv_psum", 2)
        mv_dve = signal("mv_dve", 4)
        qx_psum = signal("qx_psum", 4)
        qx_act = signal("qx_act", 8)
        qc_zero = signal("qc_zero", 1)
        out_prj = signal("out_prj", 32)
        out_st = signal("out_st", 32)
        out_mem = signal("out_mem", 32)
        out_x = sem("out_x")

        def banks(b, r0, r1, n):
            return view(ps[r0:r1, b, 0:1], [[1, n]])

        def layer_of(ap, l):
            return ap[bass.ds(l, 1)].rearrange("a p c -> (a p) c")

        passed = {e: sem(f"passed_{e}") for e in ("sp", "pe", "dve")}

        def wait_apart(eng, name, awaited, value):
            eng.wait_ge(awaited, value)
            eng.sem_inc(passed[name], 1)

        block = ctx.enter_context(nc.Block())

        CONSTS = [(xT[:], "x"), (decay[:], "decay"), (decay_s[:], "decay_s"), (qdec[:], "qdec"),
                  (kmask[:], "kmask"), (kdec[:], "kdec"), (cos[:], "cos"), (sin[:], "sin"), (ident[:], "ident"),
                  (onehot, "onehot"), (counts, "counts"), (rel, "rel_bias"), (selJ, "selJ"), (sel_d, "sel_d"),
                  (sel_w, "sel_w"), (mask_d, "mask_d"), (mask_w, "mask_w"), (lconst, "lconst"),
                  (pt[:], "page_table"), (params[:, :, 0:128], "ln")]

        @block.sync
        def _(sp):
            for dst, name in CONSTS:
                sp.dma_start(dst, a[name]).then_inc(const_in, 16)
            for dst, name, n in ((lamv, "diff_lambda", L * 128), (subg, "diff_subln_g", L * 64)):
                sp.dma_start(view(dst, [[1, n]]), bass.AP(a[name].tensor, 0, [[0, P], [1, n]])).then_inc(const_in, 16)
            sp.wait_ge(set_dve, 1)
            sp.dma_start(a["brow"], brow).then_inc(brow_out, 16)
            sp.wait_ge(brow_out, 16)
            for h in range(NH):
                src = bass.AP(a["brow"].tensor, h * NU + OFF - 255, [[1, P], [1, 256]])
                sp.dma_start(hank[:, h, :], src).then_inc(hank_in, 16)
            for h in range(HX):
                for dst, h0 in ((hank_w, 0), (hank_d, HX)):
                    src = bass.AP(a["brow"].tensor, (h0 + h) * NU, [[1, DT], [1, 1032]])
                    sp.dma_start(dst[DT * h:DT * h + DT, :], src).then_inc(hank_in, 16)
            sp.wait_ge(const_in, 16 * (len(CONSTS) + 2))
            with sp.Fori(0, L) as l:
                def page_numbers(g):
                    return [nc.values_load_multi_w_load_instructions(
                        pt[0:1, bass.ds(g * (2 * NPG) + b2 * NPG, NPG)], [mybir.EngineType.SP],
                        min_val=0, max_val=a["dk"].shape[0] - 1)[1] for b2 in range(2)]

                def pages(numbers, what, ready, slot0):
                    for b2 in range(2):
                        for pg in range(NPG):
                            src = a[what][bass.ds(numbers[b2][pg], 1), bass.ds(l, 1)].rearrange("a b p c -> (a b p) c")
                            sp.dma_start(cache[:, slot0 + b2, 256 * pg:256 * pg + 256], src).then_inc(ready[b2].sem, 16)

                def diff_keys(numbers, before):
                    wait_apart(sp, "sp", s_psum.sem, s_psum.upto(l, before))
                    pages(numbers, "dk", k_ready, 0)

                def diff_values(numbers, before):
                    wait_apart(sp, "sp", o_psum.sem, o_psum.upto(l, before))
                    pages(numbers, "dv", v_ready, 2)

                def pair(name, used, before, g, ready, slot0, n):
                    sp.wait_ge(used.sem, used.upto(l, before) + g)
                    for b2 in range(2):
                        src = a[name][bass.ds(l, 1), bass.ds(g * 2 + b2, 1)].rearrange("a b p c -> (a b p) c")
                        sp.dma_start(cache[:, slot0 + b2, 0:n], src).then_inc(ready[b2].sem, 16)

                def win_keys(g):
                    pair("wk", s_psum, 4, g, k_ready, 0, 2 * WK)

                def win_values(g):
                    pair("wv", o_psum, 4, g, v_ready, 2, 2 * WK)

                def cross_keys(g, before):
                    pair("ck", s_psum, before, g, k_ready, 0, 2048)

                def cross_values(g, before):
                    pair("cv", o_psum, before, g, v_ready, 2, 2048)

                sp.dma_start(view(s_dec, [[1, 2048]]), layer_of(a["state"], l)).then_inc(st_in.sem, 16)
                numbers = [page_numbers(0)]
                diff_keys(numbers[0], len(MIXER) + 4 - NI)
                diff_values(numbers[0], len(MIXER) + 4 - NI)
                sp.wait_ge(fm_done.sem, fm_done.upto(l, 8))
                sp.wait_ge(tm_dve.sem, tm_dve.upto(l, 9))
                sp.dma_start(o["fm"][bass.ds(l, 1)].rearrange("a p c t -> (a p) c t"),
                             view(fm[:, 2, 0:1], [[4 * T, 2], [1, 2 * T]])).then_inc(out_prj.sem, 16)
                sp.dma_start(o["tm"][bass.ds(l, 1)].rearrange("a p g c -> (a p) g c"),
                             view(tmat(0, P, 0, 1536, 1), [[2048, 3], [1, 512]])).then_inc(out_prj.sem, 16)
                for g in range(1, 4):
                    numbers.append(page_numbers(g))
                    diff_keys(numbers[g], g)
                    if g > 1:
                        diff_values(numbers[g - 1], g - 1)
                win_keys(0)
                diff_values(numbers[3], 3)
                with sp.Fori(1, 4) as g:
                    win_keys(g)
                    win_values(g - 1)
                cross_keys(0, 8)
                win_values(3)
                cross_values(0, 8)
                wait_apart(sp, "sp", st_act.sem, st_act.upto(l, 1))
                sp.dma_start(layer_of(o["s_pro"], l), view(s_pro, [[1, 512]])).then_inc(out_st.sem, 16)
                sp.wait_ge(st_dve.sem, st_dve.upto(l, 4))
                sp.dma_start(layer_of(o["s_dec"], l), view(s_dec, [[1, 2048]])).then_inc(out_st.sem, 16)
                sp.wait_ge(y_done.sem, y_done.upto(l, 1))
                sp.wait_ge(out_prj.sem, out_prj.upto(l, 32))
                sp.dma_start(memT, a["memT"]).then_inc(mem_in.sem, 16)
                cross_keys(1, len(MIXER))
                with sp.Fori(2, 4) as g:
                    cross_keys(g, len(MIXER))
                    cross_values(g - 1, len(MIXER))
                cross_values(3, len(MIXER))
                sp.wait_ge(mk_act.sem, mk_act.upto(l, 8))
                sp.dma_start(layer_of(o["mk"], l), view(mkT, [[1, 2048]])).then_inc(out_mem.sem, 16)
                sp.wait_ge(mv_dve.sem, mv_dve.upto(l, 4))
                sp.dma_start(layer_of(o["mv"], l), view(mvt, [[1, 2048]])).then_inc(out_mem.sem, 16)
                wait_apart(sp, "sp", out_st.sem, out_st.upto(l, 32))
            sp.wait_ge(x_act.sem, x_act.upto(L - 1, 16))
            sp.wait_ge(x_dve.sem, x_dve.upto(L - 1, 16))
            sp.dma_start(o["x"], xT[:]).then_inc(out_x, 16)
            sp.wait_ge(out_prj.sem, out_prj.upto(L - 1, 32))
            sp.wait_ge(out_mem.sem, out_mem.upto(L - 1, 32))
            sp.wait_ge(out_x, 16)

        @block.gpsimd
        def _(pool):
            with pool.Fori(0, L) as l:
                def load(name, r, at, idx):
                    n = a[name].shape[2]
                    pool.wait_ge(w_used.sem, w_used.upto(l, 1 - RING) + at)
                    pool.dma_start(ring[:, r, 0:n],
                                   a[name][bass.ds(l * (a[name].shape[0] // L) + idx, 1)].rearrange("a p c -> (a p) c")
                                   ).then_inc(w_ready[r].sem, 16)

                pos, index = 0, {"w16": 0, "w11": 0}
                for name, count in SEGMENTS:
                    whole = count // RING * RING
                    with pool.Fori(0, whole // RING) as turn:
                        i = turn * RING
                        for j in range(RING):
                            load(name, (pos + j) % RING, i + (pos + j), i + (index[name] + j))
                    for j in range(whole, count):
                        load(name, (pos + j) % RING, pos + j, index[name] + j)
                    pos += count
                    index[name] += count

        @block.tensor
        def _(pe):
            mm = nc.tensor.matmul

            def tr(out, in_):
                return nc.tensor.transpose(out, in_, ident[0:in_.shape[0], 0:in_.shape[0]])

            pe.sem_inc(w_used.sem, RING)
            pe.sem_inc(s_psum.sem, LEAD)
            pe.sem_inc(o_psum.sem, LEAD)
            pe.wait_ge(const_in, 16 * (len(CONSTS) + 2))
            for i in range(3):
                w = min(512, NU - 512 * i)
                last = mm(ps[0:NH, i, 0:w], rel, onehot[:, 512 * i:512 * i + w], start=True, stop=True)
            last.then_inc(set_pe, 1)
            pe.wait_ge(hank_in, 16 * (NH + 2 * HX))
            for h in range(NH):
                last = mm(ps[:, 3 + h // 2, 256 * (h % 2):256 * (h % 2) + 256], selJ, hank[:, h, :],
                          start=True, stop=True)
            last.then_inc(set_pe, 1)
            mm(ps[:, 0, :], sel_d, hank_d[:, 0:512], start=True, stop=True)
            mm(ps[:, 1, :], sel_d, hank_d[:, 512:1024], start=True, stop=True)
            mm(ps[:, 2, 0:DT], sel_d, hank_d[:, 1024:1032], start=True, stop=True).then_inc(set_pe, 1)
            pe.wait_ge(set_dve, 4)
            mm(ps[0:64, 0, 0:256], sel_w, hank_w[:, 0:512].rearrange("p (a c) -> p a c", c=16)[:, :, 0:8],
               start=True, stop=True)
            mm(ps[0:64, 1, :], sel_w, hank_w[:, 512:1024], start=True, stop=True)
            mm(ps[0:64, 2, 0:DT], sel_w, hank_w[:, 1024:1032], start=True, stop=True).then_inc(set_pe, 1)
            pe.wait_ge(set_dve, 5)

            with pe.Fori(0, L) as l:
                def slot(pos, add=0):
                    r = w_ready[pos % RING]
                    pe.wait_ge(r.sem, r.upto(l, 16 * (pos // RING + 1)) + add)
                    return ring[:, pos % RING, :]

                def x_ready(u):
                    pe.wait_ge(x_dve.sem, x_dve.upto(l, 4 * u))
                    wait_apart(pe, "pe", x_act.sem, x_act.upto(l, 4 * u))

                def ffn_in(u, pos0):
                    def chunk(j, i):
                        w = slot(pos0 + j, 4 * i)
                        pe.wait_ge(gate_done.sem, gate_done.upto(l, NF * u + j - 1) + i)
                        for half, done in ((0, a_psum), (1, w_used)):
                            for k in range(KD):
                                last = mm(ps[:, 2 * (j % 2) + half, 0:T], w[:, (half * KD + k) * P:(half * KD + k + 1) * P],
                                          xT[:, k, :], start=(k == 0), stop=(k == KD - 1))
                            last.then_inc(done.sem, 1)

                    whole = NF // RING * RING
                    with pe.Fori(0, whole // RING) as turn:
                        i = turn * RING
                        for j in range(RING):
                            chunk(j, i)
                    for j in range(whole, NF):
                        chunk(j, 0)
                    pe.wait_ge(gate_done.sem, gate_done.upto(l, NF * (u + 1)))

                def back_to_tokens(u, m):
                    pe.wait_ge(res_done.sem, res_done.upto(l, 8 * u + m + 1))
                    for g in range(3):
                        w = min(P, T - P * g)
                        last = tr(ps[0:w, 2 + 2 * g + m // 4, P * (m % 4):P * (m % 4) + P], yT[:, m, P * g:P * g + w])
                    if m % 4 == 3:
                        last.then_inc(tok_psum.sem, 1)

                def project_ffn(u, pos0):
                    for m in range(KD):
                        if m >= 2:
                            pe.wait_ge(res_done.sem, res_done.upto(l, 8 * u + m - 1))
                        for half in range(2):
                            w = slot(pos0 + 2 * m + half)
                            for k in range(11):
                                last = mm(ps[:, m % 2, 0:T], w[:, k * P:(k + 1) * P], hid[:, 11 * half + k, :],
                                          start=(half == 0 and k == 0), stop=(half == 1 and k == 10))
                            last.then_inc(w_used.sem, 1)
                        if m:
                            back_to_tokens(u, m - 1)
                    back_to_tokens(u, KD - 1)

                def chunks(pos0, src, n, free, even):
                    for m in range(KD):
                        if m % 2 == 0:
                            w = slot(pos0 + m // 2)
                        free(m)
                        for k in range(KD):
                            last = mm(ps[:, m % 2, 0:n], w[:, ((m % 2) * KD + k) * P:((m % 2) * KD + k + 1) * P],
                                      src[:, k, :], start=(k == 0), stop=(k == KD - 1))
                        last.then_inc((w_used if m % 2 else even).sem, 1)
                        yield m

                def project(u, pos0):
                    def free(m):
                        if m >= 2:
                            pe.wait_ge(res_done.sem, res_done.upto(l, 8 * u + m - 1))
                    for m in chunks(pos0, xT, T, free, out_psum):
                        if m:
                            back_to_tokens(u, m - 1)
                    back_to_tokens(u, KD - 1)

                def back_to_features(u):
                    pe.wait_ge(norm_dve.sem, norm_dve.upto(l, u + 1))
                    pe.wait_ge(norm_act.sem, norm_act.upto(l, u + 1))
                    for m in range(KD):
                        if m >= 2:
                            x = x_dve if m % 2 else x_act
                            pe.wait_ge(x.sem, x.upto(l, 4 * u + m // 2))
                        for g in range(3):
                            w = min(P, T - P * g)
                            last = tr(ps[:, m % 2, P * g:P * g + w], tok[0:w, g, P * m:P * m + P])
                        last.then_inc(xt_psum.sem, 1)

                def projections():
                    def free(m):
                        if m >= 2:
                            pe.wait_ge(fm_done.sem, fm_done.upto(l, m - 1))
                    for _ in chunks(POS_MIX, xT, T, free, fm_psum):
                        pass
                    for n in range(4):
                        for g in range(3):
                            i = 3 * n + g
                            if i >= 2:
                                nb, gb = divmod(i - 2, 3)
                                if nb == 2:
                                    pe.wait_ge(tm_act.sem, tm_act.upto(l, gb + 1))
                                else:
                                    pe.wait_ge(tm_dve.sem, tm_dve.upto(l, 3 * min(nb, 2) + gb + 1))
                            w = min(P, T - P * g)
                            for k in range(KD):
                                if g == 0 and k % 4 == 0:
                                    slot(POS_MIX + 4 + 2 * n + k // 4)
                                last = mm(ps[0:w, 2 + i % 2, :], xT[:, k, P * g:P * g + w],
                                          ring[:, (POS_MIX + 4 + 2 * n + k // 4) % RING, 512 * (k % 4):512 * (k % 4) + 512],
                                          start=(k == 0), stop=(k == KD - 1))
                                if g == 2 and k % 4 == 3:
                                    last.then_inc(w_used.sem, 1)
                            if g < 2:
                                last.then_inc(tm_psum.sem, 1)

                def memory():
                    pe.wait_ge(mem_in.sem, mem_in.upto(l, 16))
                    def free(m):
                        if m >= 2:
                            pe.wait_ge(mk_act.sem, mk_act.upto(l, m - 1))
                    for _ in chunks(POS_MIX + 16, memT, 256, free, mk_psum):
                        pass
                    for n in range(2):
                        for g in range(2):
                            if n == 0:
                                pe.wait_ge(mk_act.sem, mk_act.upto(l, 7 + g))
                            else:
                                pe.wait_ge(mv_dve.sem, mv_dve.upto(l, g + 1))
                            for k in range(KD):
                                if g == 0 and k % 4 == 0:
                                    slot(POS_MIX + 20 + 2 * n + k // 4)
                                last = mm(ps[:, g, :], memT[:, k, P * g:P * g + P],
                                          ring[:, (POS_MIX + 20 + 2 * n + k // 4) % RING, 512 * (k % 4):512 * (k % 4) + 512],
                                          start=(k == 0), stop=(k == KD - 1))
                                if g == 1 and k % 4 == 3:
                                    last.then_inc(w_used.sem, 1)
                            if g == 0:
                                last.then_inc(mv_psum.sem, 1)
                    pe.wait_ge(mv_dve.sem, mv_dve.upto(l, 4))

                def cache_in(ready, s):
                    for b2 in range(2):
                        r = ready[b2]
                        pe.wait_ge(r.sem, r.upto(l, 16 * (NPG * min(s + 1, 4) + max(s - 3, 0))))

                def scores(i, first):
                    kind, n = ITEMS[i]
                    b0 = 3 * (i % 2)
                    if i - 2 >= first:
                        s = m_done if kind[:5] != "cross" else e_done
                        pe.wait_ge(s.sem, s.upto(l, i - 1))
                    if kind == "diff_dec":
                        cache_in(k_ready, n)
                        for b2 in range(2):
                            r = 64 * b2
                            for c in range(3):
                                for hp in range(2):
                                    rhs = (view(cache[:, b2, 1024 * c + 128 * hp:1024 * c + 128 * hp + 1], [[256, 4], [1, 128]])
                                           if c < 2 else fm[:, 6 + hp, SEQ:T])
                                    last = mm(ps[r:r + 64, b0 + c, 0:(512 if c < 2 else NS)], qd[:, hp, 2 * n + b2, :], rhs,
                                              start=(hp == 0), stop=(hp == 1))
                    elif kind == "win_dec":
                        cache_in(k_ready, 4 + n)
                        for b2 in range(2):
                            r = 32 * b2
                            for c, (at, w, bank, col) in enumerate(((0, 512, 0, 0), (512, 256, 1, 0), (0, NS, 1, 256))):
                                for hp in range(2):
                                    rhs = cache[:, b2, WK * hp + at:WK * hp + at + w] if c < 2 else fm[:, 2 + hp, SEQ:T]
                                    last = mm(ps[r:r + 32, b0 + bank, col:col + w], qw[:, hp, 2 * n + b2, :], rhs,
                                              start=(hp == 0), stop=(hp == 1))
                    elif kind in ("win_pro", "diff_pro"):
                        maps = 1 if kind == "win_pro" else 2
                        for m in range(maps):
                            r, w = 64 * (n % 2) + 32 * m, 64 // maps
                            q0, k0 = (0, 2) if kind == "win_pro" else (4, 6)
                            q, k = fm[r:r + w, q0 + n // 2, :], fm[r:r + w, k0 + n // 2, :]
                            mm(ps[:, b0 + m, 0:128], q[:, 0:128], k[:, 0:128], start=True, stop=True)
                            last = mm(ps[:, b0 + m, 128:384], q[:, 128:256], k[:, 0:256], start=True, stop=True)
                    elif kind == "cross_dec":
                        cache_in(k_ready, 8 + n)
                        for b2 in range(2):
                            r = 32 * b2
                            for c in range(KD):
                                last = mm(ps[r:r + 32, b0, 0:256], qc[:, c, 2 * n + b2, :],
                                          cache[:, b2, 256 * c:256 * c + 256], start=(c == 0), stop=(c == KD - 1))
                    else:
                        for qb in range(2):
                            for c in (2 * n, 2 * n + 1):
                                last = mm(ps[:, b0, 256 * qb:256 * qb + 256], qxT[:, c, P * qb:P * qb + P], mkT[:, c, :],
                                          start=(c == 2 * n), stop=(c == 2 * n + 1))
                    last.then_inc(s_psum.sem, 1)

                def transposes(i, first):
                    kind, n = ITEMS[i]
                    p = prob[i % 2]
                    wait_apart(pe, "pe", p_done.sem, p_done.upto(l, i + 1))
                    for b in range(BATCHES[i]):
                        if i > first or b:
                            wait_apart(pe, "pe", t_done.sem, t_done.upto(l, BEFORE[i] + b))
                        if kind == "diff_dec":
                            if b < 2:
                                for c in range(4):
                                    last = tr(ps[:, 6, P * c:P * c + P], p[:, 512 * b + P * c:512 * b + P * c + P])
                            else:
                                last = tr(ps[0:NS, 6, 0:P], p[:, PAST:PAST + NS])
                        elif kind == "win_dec":
                            for c in range(6):
                                tr(ps[:, 6, 64 * c:64 * c + 64], p[0:64, P * c:P * c + P])
                            last = tr(ps[0:NS, 6, 384:448], p[0:64, WK:WK + NS])
                        elif kind == "cross_dec":
                            for c in range(2):
                                last = tr(ps[:, 6, 64 * c:64 * c + 64], p[0:64, P * c:P * c + P])
                        elif kind == "cross_pro":
                            for qb in range(2):
                                for kb in range(2):
                                    last = tr(ps[:, 6, 256 * kb + P * qb:256 * kb + P * qb + P],
                                              p[:, 256 * qb + P * kb:256 * qb + P * kb + P])
                        else:
                            for c in range(3):
                                last = tr(ps[:, 6, P * c:P * c + P], p[:, P * c:P * c + P])
                        last.then_inc(t_psum.sem, 1)

                def values(i, first):
                    kind, n = ITEMS[i]
                    t = pT[i % 2]
                    pe.wait_ge(t_done.sem, t_done.upto(l, BEFORE[i] + BATCHES[i]))
                    if i > first:
                        pe.wait_ge(o_done.sem, o_done.upto(l, i))
                    if kind in ("diff_dec", "win_dec"):
                        nk, rows, w, col, v0 = (8, 128, 32, 64, 256) if kind == "diff_dec" else (6, 64, 16, 32, 0)
                        cache_in(v_ready, n if kind == "diff_dec" else 4 + n)
                        for hp in range(2):
                            for b2 in range(2):
                                at = w * (2 * hp + b2)
                                for k in range(nk + 1):
                                    q = col * b2 + w * hp
                                    if k == nk:
                                        lhs = tmat(0, NS, 2, 1536 + v0 + P * hp, P)
                                        rhs = t[0:NS, rows * nk + q:rows * nk + q + w]
                                    else:
                                        lhs = cache[:, 2 + b2, 256 * k + P * hp:256 * k + P * hp + P]
                                        rhs = t[:, rows * k + q:rows * k + q + w]
                                    last = mm(ps[:, 7, at:at + w], lhs, rhs, start=(k == 0), stop=(k == nk))
                    elif kind == "win_pro":
                        r = 64 * (n % 2)
                        mm(ps[r:r + 64, 7, 0:256], tmat(0, P, 0, 1536 + 64 * n, 64), t[:, 0:256], start=True, stop=False)
                        last = mm(ps[r:r + 64, 7, 128:256], tmat(0, P, 1, 1536 + 64 * n, 64), t[:, 256:384],
                                  start=False, stop=True)
                    elif kind == "diff_pro":
                        v = [tmat(0, P, kb, 1792 + 64 * n, 64) for kb in range(2)]
                        mm(ps[:, 7, 0:64], t[:, 0:128], v[0], start=True, stop=True)
                        mm(ps[:, 7, 64:128], t[:, 128:256], v[0], start=True, stop=False)
                        last = mm(ps[:, 7, 64:128], t[:, 256:384], v[1], start=False, stop=True)
                    elif kind == "cross_dec":
                        cache_in(v_ready, 8 + n)
                        for c in range(KD):
                            for b2 in range(2):
                                for kb in range(2):
                                    q = 64 * kb + 32 * b2 + DT * (c // 2)
                                    last = mm(ps[:, 7, 16 * c + DT * b2:16 * c + DT * b2 + DT],
                                              cache[:, 2 + b2, 1024 * kb + P * c:1024 * kb + P * c + P],
                                              t[:, q:q + DT], start=(kb == 0), stop=(kb == 1))
                    else:
                        for cc in range(2):
                            for kb in range(2):
                                last = mm(ps[:, 7, 256 * cc:256 * cc + 256],
                                          mvt[:, kb, 256 * n + P * cc:256 * n + P * cc + P],
                                          t[:, 256 * kb:256 * kb + 256], start=(kb == 0), stop=(kb == 1))
                    last.then_inc(o_psum.sem, 1)

                def attention(first, end):
                    scores(first, first)
                    for i in range(first, end):
                        if i + 1 < end:
                            scores(i + 1, first)
                        transposes(i, first)
                        values(i, first)

                def retention():
                    pe.wait_ge(o_done.sem, o_done.upto(l, len(MIXER)))
                    for b, at in ((0, 0), (1, 256)):
                        for c in range(2):
                            for g in range(2):
                                last = tr(ps[:, b, 256 * c + P * g:256 * c + P * g + P], tmat(0, P, g, at + P * c, P))
                        last.then_inc(rt_psum.sem, 1)
                    for h in range(HX):
                        for r in (0, 64):
                            last = mm(ps[r:r + 64, 2, 64 * h:64 * h + 64], tmat(0, NS, 2, 64 * h, 64), ident[0:NS, 0:NS],
                                      start=True, stop=True)
                    last.then_inc(rt_psum.sem, 1)
                    for h in range(HX):
                        last = mm(ps[0:64, 3, 64 * h:64 * h + 64], tmat(0, NS, 2, 256 + 64 * h, 64), ident[0:NS, 0:NS],
                                  start=True, stop=True)
                    last.then_inc(rt_psum.sem, 1)
                    pe.wait_ge(rt_act.sem, rt_act.upto(l, 2))

                    def head_scores(h):
                        r = 64 * (h % 2)
                        q, k = qTp[r:r + 64, h // 2, :], kTp[r:r + 64, h // 2, :]
                        if h >= 2:
                            pe.wait_ge(ra_done.sem, ra_done.upto(l, h - 1))
                        mm(ps[:, 4 + h % 2, 0:256], k[:, 0:128], q, start=True, stop=True)
                        mm(ps[:, 4 + h % 2, 256:384], k[:, 128:256], q[:, 128:256], start=True, stop=True)\
                            .then_inc(ra_psum.sem, 1)

                    head_scores(0)
                    for h in range(HX):
                        if h + 1 < HX:
                            head_scores(h + 1)
                        pe.wait_ge(ra_done.sem, ra_done.upto(l, h + 1))
                        t, at = aT[h % 2], P * h
                        v = [tmat(0, P, g, 512 + P * h, P) for g in range(2)]
                        mm(ps[:, 6, at:at + P], t[:, 0:128], v[0], start=True, stop=True)
                        mm(ps[:, 7, at:at + P], t[:, 128:256], v[0], start=True, stop=False)
                        last = mm(ps[:, 7, at:at + P], t[:, 256:384], v[1], start=False, stop=True)
                    last.then_inc(ro_psum.sem, 1)
                    wait_apart(pe, "pe", rt_dve.sem, rt_dve.upto(l, 2))
                    for h in range(HX):
                        last = mm(ps[0:NS, 2, 64 * h:64 * h + 64], kTs[:, h, :], qTs[:, h, :], start=True, stop=True)
                    last.then_inc(ra_psum.sem, 1)
                    pe.wait_ge(ra_done.sem, ra_done.upto(l, 5))
                    wait_apart(pe, "pe", st_in.sem, st_in.upto(l, 16))
                    for h in range(HX):
                        at = P * h
                        mm(ps[0:NS, 3, at:at + P], aTs[:, h, :], tmat(0, NS, 2, 512 + P * h, P), start=True, stop=False)
                        for g in range(4):
                            last = mm(ps[0:NS, 3, at:at + P], qx[:, h, g, :], s_dec[:, g, h, :], start=False, stop=(g == 3))
                    last.then_inc(ro_psum.sem, 1)
                    pe.wait_ge(k_decayed.sem, k_decayed.upto(l, 1))
                    for h in range(HX):
                        for g in range(2):
                            last = mm(ps[0:64, 0, P * h:P * h + P], kd[:, g, h, :], tmat(0, P, g, 512 + P * h, P),
                                      start=(g == 0), stop=(g == 1))
                    last.then_inc(st_psum.sem, 1)
                    for g, bank in enumerate((1, 4, 5, 2)):
                        for h in range(HX):
                            last = mm(ps[:, bank, P * h:P * h + P],
                                      view(kx[:, h, 2 * g, 0:1], [[1, P]]), tmat(0, NS, 2, 512 + P * h, P),
                                      start=True, stop=True)
                        last.then_inc(st_psum.sem, 1)
                    wait_apart(pe, "pe", st_act.sem, st_act.upto(l, 1))
                    for hp in range(2):
                        last = tr(ps[0:NS, 0, P * hp:P * hp + P], ocT[:, hp, :])
                    last.then_inc(oc_psum.sem, 1)
                    pe.wait_ge(y_done.sem, y_done.upto(l, 1))
                    for i, c in enumerate((0, 1, 2, 3, 6, 7)):
                        if i >= 2:
                            pe.wait_ge(y_act.sem, y_act.upto(l, i - 1))
                        for g in range(3):
                            w = min(P, T - P * g)
                            col = P * min(i, 5)
                            last = tr(ps[:, i % 2, P * g:P * g + w], ytok[0:w, g, col:col + P])
                        last.then_inc(y_psum.sem, 1)
                    pe.wait_ge(y_act.sem, y_act.upto(l, 6))

                x_ready(0)
                ffn_in(0, POS_FFN1)
                project_ffn(0, POS_FFN1 + NF)
                back_to_features(0)
                x_ready(1)
                projections()
                pe.wait_ge(fm_done.sem, fm_done.upto(l, 8))
                pe.wait_ge(tm_act.sem, tm_act.upto(l, 3))
                pe.wait_ge(tm_dve.sem, tm_dve.upto(l, 9))
                pe.wait_ge(q_built.sem, q_built.upto(l, 1))
                attention(0, len(MIXER))
                retention()
                project(1, POS_MIX + 12)
                memory()
                back_to_features(1)
                x_ready(2)

                def free(m):
                    if m >= 2:
                        pe.wait_ge(qx_act.sem, qx_act.upto(l, m - 1))
                for _ in chunks(POS_MIX + 24, xT, T, free, qx_psum):
                    pass
                pe.wait_ge(qx_act.sem, qx_act.upto(l, 8))
                attention(len(MIXER), NI)
                pe.wait_ge(o_done.sem, o_done.upto(l, NI))
                project(2, POS_MIX + 28)
                back_to_features(2)
                x_ready(3)
                ffn_in(1, POS_FFN2)
                project_ffn(3, POS_FFN2 + NF)
                back_to_features(3)

        @block.scalar
        def _(act):
            fn = nc.scalar.activation

            act.sem_inc(x_act.sem, 1)
            act.wait_ge(set_dve, 2)
            fn(small[:, 4:8], small[:, 0:4], ACT.Exp).then_inc(set_act, 1)

            with act.Fori(0, L) as l:
                act.wait_ge(cur_done.sem, cur_done.upto(l, 1))

                def ffn_gate(u, pos0):
                    def chunk(j, i, c):
                        act.wait_ge(a_psum.sem, a_psum.upto(l, NF * u + j + 1) + i)
                        fn(gate[:, j % 2, :], ps[:, 2 * (j % 2), 0:T], ACT.Silu).then_inc(silu_done.sem, 1)
                    whole = NF // RING * RING
                    with act.Fori(0, whole // RING) as turn:
                        i = turn * RING
                        for j in range(RING):
                            chunk(j, i, i + j)
                    for j in range(whole, NF):
                        chunk(j, 0, j)

                def norm(u, fill=None):
                    act.wait_ge(var_done.sem, var_done.upto(l, u + 1))
                    fn(lnst[:, :, 1], lnst[:, :, 0], ACT.Sqrt).then_inc(sd_done.sem, 1)
                    act.wait_ge(par_done.sem, par_done.upto(l, u + 1))
                    fn(tok[:, 1, :], banks(4, 0, P, 1024), ACT.Identity, bias=lnst[:, 1, 2:3],
                       scale=lnst[:, 1, 1:2]).then_inc(norm_act.sem, 1)
                    if fill:
                        fill()
                    for m in range(0, KD, 2):
                        act.wait_ge(xt_psum.sem, xt_psum.upto(l, 8 * u + m + 1))
                        fn(xT[:, m, :], ps[:, 0, 0:T], ACT.Identity, bias=cur[:, 64 + 8 * u + m:65 + 8 * u + m], scale=cur[:, 8 * u + m:8 * u + m + 1]
                           ).then_inc(x_act.sem, 1)

                def mk_copies():
                    for m in range(KD):
                        if m % 2:
                            act.wait_ge(w_used.sem, w_used.upto(l, POS_MIX + 16 + m // 2 + 1))
                        else:
                            act.wait_ge(mk_psum.sem, mk_psum.upto(l, m // 2 + 1))
                        fn(mkT[:, m, :], ps[:, m % 2, 0:256], ACT.Copy).then_inc(mk_act.sem, 1)

                def exponentials(i):
                    kind, n = ITEMS[i]
                    p, st, b0 = prob[i % 2], stat[:, i % 2, :], 3 * (i % 2)
                    act.wait_ge(m_done.sem, m_done.upto(l, i + 1))
                    parts = {"diff_dec": [(0, P, 0, PAST + NS)], "win_dec": [(0, 64, 0, WK + NS)],
                             "win_pro": [(0, P, 0, 128), (0, P, 128, 256)],
                             "diff_pro": [(0, P, 0, 128), (0, P, 128, 256), (0, P, 384, 128), (0, P, 512, 256)],
                             "cross_dec": [(0, 64, 0, 256)], "cross_pro": [(0, P, 0, 256), (0, P, 256, 256)]}[kind]
                    for j, (r0, r1, at, w) in enumerate(parts):
                        cross = kind[:5] == "cross"
                        src = banks(b0, r0, r1, 512)[:, at:at + w] if cross else p[r0:r1, at:at + w]
                        last = fn(p[r0:r1, at:at + w], src, ACT.Exp, bias=st[r0:r1, 4 + j:5 + j],
                                  scale=XSCALE if cross else 1.0, accum_out=st[r0:r1, 8 + j:9 + j])
                    last.then_inc(e_done.sem, 1)

                def copies(i):
                    kind, n = ITEMS[i]
                    t = pT[i % 2]
                    for b in range(BATCHES[i]):
                        act.wait_ge(t_psum.sem, t_psum.upto(l, BEFORE[i] + b + 1))
                        if kind == "diff_dec":
                            last = (fn(t[:, 512 * b:512 * b + 512], ps[:, 6, :], ACT.Copy) if b < 2 else
                                    fn(t[0:NS, 1024:1152], ps[0:NS, 6, 0:P], ACT.Copy))
                        elif kind == "win_dec":
                            fn(t[:, 0:384], ps[:, 6, 0:384], ACT.Copy)
                            last = fn(t[0:NS, 384:448], ps[0:NS, 6, 384:448], ACT.Copy)
                        else:
                            w = {"cross_dec": 128, "cross_pro": 512}.get(kind, 384)
                            last = fn(t[:, 0:w], ps[:, 6, 0:w], ACT.Copy)
                        last.then_inc(t_done.sem, 1)

                def attention(first, end):
                    exponentials(first)
                    for i in range(first, end):
                        copies(i)
                        if i + 1 < end:
                            exponentials(i + 1)

                ffn_gate(0, POS_FFN1)
                norm(0)
                for m in range(8):
                    if m % 2:
                        act.wait_ge(w_used.sem, w_used.upto(l, POS_MIX + m // 2 + 1))
                    else:
                        act.wait_ge(fm_psum.sem, fm_psum.upto(l, m // 2 + 1))
                    scale = {0: 64 ** -0.5, 2: 32 ** -0.5}.get(m // 2, 1.0)
                    fn(fm[:, m, :], ps[:, m % 2, 0:T], ACT.Copy, scale=scale).then_inc(fm_done.sem, 1)
                for g in range(3):
                    if g < 2:
                        act.wait_ge(tm_psum.sem, tm_psum.upto(l, 4 + g + 1))
                    else:
                        act.wait_ge(w_used.sem, w_used.upto(l, POS_MIX + 4 + 6))
                    w = min(P, T - P * g)
                    fn(tmat(0, w, g, 1024, 512), ps[0:w, 2 + (6 + g) % 2, :], ACT.Silu).then_inc(tm_act.sem, 1)
                attention(0, len(MIXER))
                for b, dst, scale in ((0, qTp, 1.0), (1, kTp, 0.125)):
                    act.wait_ge(rt_psum.sem, rt_psum.upto(l, b + 1))
                    fn(view(dst, [[1, 512]]), ps[:, b, :], ACT.Copy, scale=scale).then_inc(rt_act.sem, 1)
                for g, bank in ((0, 6), (1, 7), (2, 3)):
                    act.wait_ge(ro_psum.sem, ro_psum.upto(l, 1 if g < 2 else 2))
                    w = min(P, T - P * g)
                    for h in range(HX):
                        last = fn(ytok[0:w, g, P * h:P * h + P], ps[0:w, bank, P * h:P * h + P], ACT.Square,
                                  accum_out=small[0:w, 12 + 4 * g + h:13 + 4 * g + h])
                last.then_inc(rsq_done.sem, 1)
                act.wait_ge(st_psum.sem, st_psum.upto(l, 1))
                fn(view(s_pro, [[1, 512]]), ps[0:64, 0, :], ACT.Copy).then_inc(st_act.sem, 1)
                act.wait_ge(rss_done.sem, rss_done.upto(l, 1))
                fn(small[:, 24:48], small[:, 0:24], ACT.Sqrt).then_inc(rsd_done.sem, 1)
                for i, c in enumerate((0, 1, 2, 3, 6, 7)):
                    act.wait_ge(y_psum.sem, y_psum.upto(l, i + 1))
                    fn(xT[:, c, :], ps[:, i % 2, 0:T], ACT.Copy).then_inc(y_act.sem, 1)
                norm(1, mk_copies)
                act.wait_ge(qc_zero.sem, qc_zero.upto(l, 1))
                for m in range(KD):
                    if m % 2:
                        act.wait_ge(w_used.sem, w_used.upto(l, POS_MIX + 24 + m // 2 + 1))
                    else:
                        act.wait_ge(qx_psum.sem, qx_psum.upto(l, m // 2 + 1))
                    fn(qxT[:, m, :], ps[:, m % 2, 0:SEQ], ACT.Copy)
                    fn(qc[:, m, :, DT * (m // 2):DT * (m // 2) + DT],
                       ps[:, m % 2, SEQ:T].rearrange("p (b t) -> p b t", b=DB), ACT.Copy).then_inc(qx_act.sem, 1)
                attention(len(MIXER), NI)
                norm(2)
                ffn_gate(1, POS_FFN2)
                norm(3)

        @block.vector
        def _(dve):
            V = nc.vector
            dve.sem_inc(x_dve.sem, 1)
            dve.sem_inc(gate_done.sem, 2)
            own = [0]

            def own_step(ins):
                own[0] += 1
                ins.then_inc(own_set, 1)
                dve.wait_ge(own_set, own[0])

            V.memset(qd[:], 0.0)
            V.memset(qw[:], 0.0)
            V.memset(small[:], 1.0)
            V.memset(lnst[:], 1.0)
            V.memset(tok[:, 2, :], 0.0)
            V.memset(mean_var[:], 1.0)
            dve.wait_ge(const_in, 16 * (len(CONSTS) + 2))
            V.tensor_scalar(yT[:], xT[:], ALPHA, None, ALU.mult)
            dve.wait_ge(set_pe, 1)
            V.tensor_tensor(brow, banks(0, 0, NH, NU), counts, ALU.add).then_inc(set_dve, 1)
            lv = lamv[:, :, :, :]
            own_step(V.tensor_tensor(lamt.rearrange("p (l v d) -> p l v d", l=L, v=2), lv[:, :, 0::2, :], lv[:, :, 1::2, :],
                                     ALU.mult))
            V.tensor_reduce(small[:, 0:4], lamt.rearrange("p (a d) -> p a d", d=32), AX.X, ALU.add).then_inc(set_dve, 1)
            dve.wait_ge(set_pe, 2)
            V.tensor_copy(view(bias_pro[:, 0, 0:1], [[1, 2048]]), banks(3, 0, P, 2048)).then_inc(set_dve, 1)
            dve.wait_ge(set_pe, 3)
            V.tensor_copy(bias_dd[:], banks(0, 0, P, PAST))
            V.tensor_tensor(view(bias_dn[:, 0, 0:1], [[DT, 32], [1, DT]]), view(ps[:, 2, 0:1], [[0, 32], [1, DT]]),
                            view(mask_d[:, 0, 0:1], [[1, 32], [0, DT]]), ALU.add).then_inc(set_dve, 1)
            dve.wait_ge(set_pe, 4)
            V.tensor_copy(bias_wd[:, 0:256], ps[0:64, 0, 0:256])
            V.tensor_copy(bias_wd[:, 256:768], ps[0:64, 1, :])
            V.tensor_tensor(view(bias_wn[:, 0, 0:1], [[DT, 32], [1, DT]]), view(ps[0:64, 2, 0:1], [[0, 32], [1, DT]]),
                            view(mask_w[:, 0, 0:1], [[1, 32], [0, DT]]), ALU.add).then_inc(set_dve, 1)
            dve.wait_ge(set_act, 1)
            for i in range(L):
                own_step(V.tensor_tensor(params[:, i, 128:129], small[:, 5 + 2 * i:6 + 2 * i], small[:, 4 + 2 * i:5 + 2 * i],
                                         ALU.subtract))
                own_step(V.tensor_tensor(params[:, i, 128:129], params[:, i, 128:129], lconst[:, i:i + 1], ALU.subtract))
                V.scalar_tensor_tensor(params[:, i, 129:130], lconst[:, 5:6], params[:, i, 128:129], lconst[:, 4:5],
                                       ALU.mult, ALU.add)
                own_step(V.tensor_scalar(subg[:, i, :], subg[:, i, :], lconst[:, 2 + i:3 + i], None, ALU.mult))

            with dve.Fori(0, L) as l:
                step = [0]

                def link(ins, alone=False):
                    step[0] += 1
                    ins.then_inc(dve_step.sem, 1)
                    if alone:
                        wait_apart(dve, "dve", dve_step.sem, dve_step.upto(l, step[0]))
                    else:
                        dve.wait_ge(dve_step.sem, dve_step.upto(l, step[0]))

                V.tensor_copy(cur[:], params[:, bass.ds(l, 1), :].rearrange("p a c -> p (a c)"))
                V.tensor_copy(curg[:], subg[:, bass.ds(l, 1), :].rearrange("p a c -> p (a c)")).then_inc(cur_done.sem, 1)
                wait_apart(dve, "dve", cur_done.sem, cur_done.upto(l, 1))
                neglam, sign = cur[:, 128:129], cur[:, 129:130]

                def ffn_gate(u, pos0):
                    def chunk(j, i):
                        dve.wait_ge(silu_done.sem, silu_done.upto(l, NF * u + j + 1) + i)
                        dve.wait_ge(w_used.sem, w_used.upto(l, pos0 + j + 1) + i)
                        V.tensor_tensor(hid[:, bass.ds(i + j, 1), :], gate[:, j % 2:j % 2 + 1, :],
                                        ps[:, 2 * (j % 2) + 1:2 * (j % 2) + 2, 0:T], ALU.mult).then_inc(gate_done.sem, 1)
                    whole = NF // RING * RING
                    with dve.Fori(0, whole // RING) as turn:
                        i = turn * RING
                        for j in range(RING):
                            chunk(j, i)
                    for j in range(whole, NF):
                        chunk(j, 0)

                def statistics(half):
                    for g in range(3):
                        w = min(P, T - P * g)
                        last = V.bn_stats(bn[0:w, g, half, :], ps[0:w, 2 + 2 * g + half, :])
                    return last

                def norm(u, scale, ready, fill=None):
                    for m in range(KD):
                        ready(m)
                        V.scalar_tensor_tensor(yT[:, m, :], ps[:, m % 2, 0:T], scale, yT[:, m, :], ALU.mult, ALU.add)\
                            .then_inc(res_done.sem, 1)
                        if m == 6:
                            dve.wait_ge(tok_psum.sem, tok_psum.upto(l, 2 * u + 1))
                            statistics(0)
                    dve.wait_ge(tok_psum.sem, tok_psum.upto(l, 2 * u + 2))
                    link(statistics(1), alone=True)
                    for g in range(3):
                        w = min(P, T - P * g)
                        last = V.bn_aggr(mean_var[0:w, g, :], bn[0:w, g, :, :].rearrange("p a b -> p (a b)"))
                    link(last)
                    V.tensor_scalar(lnst[:, :, 0], mean_var[:, :, 1], LN_EPS, None, ALU.add).then_inc(var_done.sem, 1)
                    dve.wait_ge(sd_done.sem, sd_done.upto(l, u + 1))
                    link(V.reciprocal(lnst[:, :, 1], lnst[:, :, 1]))
                    V.scalar_tensor_tensor(lnst[:, :, 2], mean_var[:, :, 0], -1.0, lnst[:, :, 1], ALU.mult, ALU.mult)\
                        .then_inc(par_done.sem, 1)
                    for g in (0, 2):
                        w = min(P, T - P * g)
                        last = V.tensor_scalar(tok[0:w, g, :], banks(2 + 2 * g, 0, w, 1024), mean_var[0:w, g, 0:1],
                                               lnst[0:w, g, 1:2], ALU.subtract, ALU.mult)
                    last.then_inc(norm_dve.sem, 1)
                    if fill:
                        fill()
                    for m in range(1, KD, 2):
                        dve.wait_ge(xt_psum.sem, xt_psum.upto(l, 8 * u + m + 1))
                        V.tensor_scalar(xT[:, m, :], ps[:, 1, 0:T], cur[:, 8 * u + m:8 * u + m + 1],
                                        cur[:, 64 + 8 * u + m:65 + 8 * u + m], ALU.mult, ALU.add).then_inc(x_dve.sem, 1)
                    dve.wait_ge(x_dve.sem, x_dve.upto(l, 4 * u + 4))
                    dve.wait_ge(x_act.sem, x_act.upto(l, 4 * u + 4))
                    V.tensor_scalar(yT[:], xT[:], ALPHA, None, ALU.mult)

                def ffn_out(pos0):
                    return lambda m: dve.wait_ge(w_used.sem, w_used.upto(l, pos0 + NF + 2 * m + 2))

                def square_out(u, pos0):
                    def ready(m):
                        if m % 2:
                            dve.wait_ge(w_used.sem, w_used.upto(l, pos0 + m // 2 + 1))
                        else:
                            dve.wait_ge(out_psum.sem, out_psum.upto(l, 4 * (u - 1) + m // 2 + 1))
                    return ready

                def token_major(n):
                    for g in range(3):
                        if g < 2:
                            dve.wait_ge(tm_psum.sem, tm_psum.upto(l, 2 * n + g + 1))
                        else:
                            dve.wait_ge(w_used.sem, w_used.upto(l, POS_MIX + 4 + 2 * n + 2))
                        w = min(P, T - P * g)
                        V.tensor_copy(tmat(0, w, g, 512 * n, 512), ps[0:w, 2 + (3 * n + g) % 2, :]).then_inc(tm_dve.sem, 1)

                def rotate():
                    dve.wait_ge(tm_dve.sem, tm_dve.upto(l, 3))
                    def bc(t, g):
                        return view(t[:, g, 0:1], [[0, 8], [1, 32]])
                    def half(g, i):
                        return view(tmat(0, P, g, 32 * i, 1), [[64, 8], [1, 32]])
                    for g in range(3):
                        for i, (x, t) in enumerate(((0, cos), (1, sin), (0, sin), (1, cos))):
                            last = V.tensor_tensor(rp[i][:, g, :, :], half(g, x), bc(t, g), ALU.mult)
                    link(last)
                    for g in range(3):
                        V.tensor_tensor(half(g, 0), rp[0][:, g, :, :], rp[1][:, g, :, :], ALU.subtract)
                        last = V.tensor_tensor(half(g, 1), rp[2][:, g, :, :], rp[3][:, g, :, :], ALU.add)
                    link(last)

                def spread_queries():
                    dve.wait_ge(fm_done.sem, fm_done.upto(l, 8))
                    for hp in range(2):
                        for m in range(2):
                            r = 64 * hp + 32 * m
                            V.tensor_copy(view(qd[r:r + 32, 0, 0, 16 * hp + 8 * m:16 * hp + 8 * m + 1],
                                               [[DB * 64 + 32, 2], [64, DB], [1, DT]]),
                                          view(fm[r:r + 32, 4, SEQ:SEQ + 1], [[T, 2], [DT, DB], [1, DT]]))
                    for hp in range(2):
                        r = 64 * hp
                        last = V.tensor_copy(view(qw[r:r + 64, 0, 0, DT * hp:DT * hp + 1],
                                                  [[DB * 32 + 2 * DT, 2], [32, DB], [1, DT]]),
                                             view(fm[r:r + 64, 0, SEQ:SEQ + 1], [[T, 2], [DT, DB], [1, DT]]))
                    last.then_inc(q_built.sem, 1)

                def maxima(i):
                    kind, n = ITEMS[i]
                    p, st, b0 = prob[i % 2], stat[:, i % 2, :], 3 * (i % 2)
                    if kind[:5] != "cross":
                        wait_apart(dve, "dve", s_psum.sem, s_psum.upto(l, i + 1))
                    else:
                        dve.wait_ge(s_psum.sem, s_psum.upto(l, i + 1))

                    def add_max(r1, at, w, src, bias, j):
                        return V.tensor_tensor_reduce(out=p[0:r1, at:at + w], in0=src, in1=bias, scale=1.0, scalar=LOW,
                                                      op0=ALU.add, op1=ALU.max, accum_out=st[0:r1, j:j + 1])
                    if kind in ("diff_dec", "win_dec"):
                        r1, w, past, new = (P, PAST, bias_dd, bias_dn) if kind == "diff_dec" else (64, WK, bias_wd, bias_wn)
                        add_max(r1, 0, w, banks(b0, 0, r1, w), past[:], 0)
                        link(add_max(r1, w, NS, banks(b0, 0, r1, w + NS)[:, w:w + NS], new[:, n, :], 1))
                        V.tensor_reduce(st[0:r1, 4:5], st[0:r1, 0:2], AX.X, ALU.max, negate=True).then_inc(m_done.sem, 1)
                    elif kind in ("win_pro", "diff_pro"):
                        h = n if kind == "win_pro" else HX + n
                        maps = 1 if kind == "win_pro" else 2
                        for m in range(maps):
                            add_max(P, 384 * m, 128, ps[:, b0 + m, 0:128], bias_pro[:, h, 128:256], 2 * m)
                            last = add_max(P, 384 * m + 128, 256, ps[:, b0 + m, 128:384], bias_pro[:, h, :], 2 * m + 1)
                        link(last)
                        V.tensor_scalar(st[:, 4:4 + 2 * maps], st[:, 0:2 * maps], -1.0, None, ALU.mult)\
                            .then_inc(m_done.sem, 1)
                    else:
                        r1, k = (64, 1) if kind == "cross_dec" else (P, 2)
                        link(V.tensor_reduce(st[0:r1, 0:k], ps[0:r1, b0, 0:256 * k].rearrange("p (a b) -> p a b", a=k),
                                             AX.X, ALU.max))
                        V.tensor_scalar(st[0:r1, 4:4 + k], st[0:r1, 0:k], -XSCALE, None, ALU.mult).then_inc(m_done.sem, 1)

                def normalise(i):
                    kind, n = ITEMS[i]
                    p, st = prob[i % 2], stat[:, i % 2, :]
                    dve.wait_ge(e_done.sem, e_done.upto(l, i + 1))
                    r1, k = {"diff_dec": (P, 1), "win_dec": (64, 1), "win_pro": (P, 2), "diff_pro": (P, 4),
                             "cross_dec": (64, 1), "cross_pro": (P, 2)}[kind]
                    link(V.reciprocal(st[0:r1, 12:12 + k], st[0:r1, 8:8 + k]))
                    if kind == "diff_dec":
                        link(V.tensor_tensor(st[:, 12:13], st[:, 12:13], sign, ALU.mult))
                    if kind == "diff_pro":
                        link(V.tensor_scalar(st[:, 14:16], st[:, 14:16], neglam, None, ALU.mult))
                    parts = {"diff_dec": [(0, PAST + NS)], "win_dec": [(0, WK + NS)], "win_pro": [(0, 128), (128, 256)],
                             "diff_pro": [(0, 128), (128, 256)], "cross_dec": [(0, 256)],
                             "cross_pro": [(0, 256), (256, 256)]}[kind]
                    for j, (at, w) in enumerate(parts):
                        last = V.tensor_scalar(p[0:r1, at:at + w], p[0:r1, at:at + w], st[0:r1, 12 + j:13 + j], None, ALU.mult)
                    if kind == "diff_pro":
                        link(last)
                        for j, (at, w) in enumerate(parts):
                            last = V.scalar_tensor_tensor(p[:, at:at + w], p[:, 384 + at:384 + at + w], st[:, 14 + j:15 + j],
                                                          p[:, at:at + w], ALU.mult, ALU.add)
                    last.then_inc(p_done.sem, 1)

                def outputs(i):
                    kind, n = ITEMS[i]
                    dve.wait_ge(o_psum.sem, o_psum.upto(l, i + 1))
                    if kind == "diff_dec":
                        for hp in range(2):
                            r = 64 * hp
                            last = V.tensor_reduce(view(ocT[r:r + 64, 0, 16 * n:16 * n + 1], [[NS, 2], [DT, 2], [1, DT]]),
                                                   view(ps[r:r + 64, 7, 16 * hp:16 * hp + 1], [[64, 2], [32, 2], [1, DT], [DT, 2]]),
                                                   AX.X, ALU.add)
                    elif kind == "win_dec":
                        for hp in range(2):
                            r = 64 * hp
                            last = V.tensor_copy(view(xT[r:r + 64, 4, SEQ + 16 * n:SEQ + 16 * n + 1], [[T, 2], [DT, 2], [1, DT]]),
                                                 view(ps[r:r + 64, 7, DT * hp:DT * hp + 1], [[32, 2], [16, 2], [1, DT]]))
                    elif kind == "win_pro":
                        r = 64 * (n % 2)
                        last = V.tensor_copy(xT[r:r + 64, 4 + n // 2, 0:256], ps[r:r + 64, 7, 0:256])
                    elif kind == "diff_pro":
                        last = V.tensor_copy(ytok[:, 0:2, 512 + 64 * n:576 + 64 * n],
                                             ps[:, 7, 0:128].rearrange("p (g e) -> p g e", g=2))
                    elif kind == "cross_dec":
                        last = V.tensor_copy(xT[:, :, SEQ + 16 * n:SEQ + 16 * n + 16],
                                             ps[:, 7, 0:128].rearrange("p (c t) -> p c t", c=KD))
                    else:
                        last = V.tensor_copy(xT[:, 2 * n:2 * n + 2, 0:256], ps[:, 7, :].rearrange("p (c t) -> p c t", c=2))
                    last.then_inc(o_done.sem, 1)

                def attention(first, end):
                    maxima(first)
                    normalise(first)
                    for i in range(first, end):
                        if i + 1 < end:
                            maxima(i + 1)
                        outputs(i)
                        if i + 1 < end:
                            normalise(i + 1)

                def retention():
                    dve.wait_ge(out_prj.sem, out_prj.upto(l, 32))
                    for g in range(2):
                        V.tensor_tensor(kd[:, g, :, :], view(tmat(0, P, g, 256, 1), [[64, HX], [1, 64]]),
                                        view(kdec[:, g, 0:1], [[1, HX], [0, 64]]), ALU.mult)
                    V.tensor_tensor(kx[:, :, :, :], view(tmat(0, NS, 2, 256, 1), [[64, HX], [0, DB], [1, 64]]),
                                    view(kmask[:, 0, 0:1], [[DB, HX], [1, DB], [0, 64]]), ALU.mult).then_inc(k_decayed.sem, 1)
                    dve.wait_ge(rt_psum.sem, rt_psum.upto(l, 3))
                    V.tensor_copy(view(qTs, [[1, 256]]), ps[0:64, 2, 0:256])
                    V.tensor_tensor(qx[:, :, :, :], view(ps[:, 2, 0:1], [[64, HX], [0, 4], [1, NS]]), qdec[:], ALU.mult)\
                        .then_inc(rt_dve.sem, 1)
                    dve.wait_ge(rt_psum.sem, rt_psum.upto(l, 4))
                    V.tensor_scalar(view(kTs, [[1, 256]]), ps[0:64, 3, 0:256], 0.125, None, ALU.mult).then_inc(rt_dve.sem, 1)
                    for h in range(HX):
                        dve.wait_ge(ra_psum.sem, ra_psum.upto(l, h + 1))
                        V.tensor_tensor(aT[h % 2][:, 0:256], ps[:, 4 + h % 2, 0:256], decay[:, h, :], ALU.mult)
                        V.tensor_tensor(aT[h % 2][:, 256:384], ps[:, 4 + h % 2, 256:384], decay[:, h, 0:128], ALU.mult)\
                            .then_inc(ra_done.sem, 1)
                    dve.wait_ge(ra_psum.sem, ra_psum.upto(l, 5))
                    V.tensor_tensor(view(aTs, [[1, 256]]), ps[0:NS, 2, 0:256], view(decay_s[:, 0, 0:1], [[1, 256]]), ALU.mult)\
                        .then_inc(ra_done.sem, 1)
                    dve.wait_ge(ro_psum.sem, ro_psum.upto(l, 2))
                    for g, bank in enumerate((1, 4, 5, 2)):
                        dve.wait_ge(st_psum.sem, st_psum.upto(l, g + 2))
                        for h in range(HX):
                            last = V.scalar_tensor_tensor(s_dec[:, g, h, :], s_dec[:, g, h, :], CHUNK_DECAY[h],
                                                          ps[:, bank, P * h:P * h + P], ALU.mult, ALU.add)
                        last.then_inc(st_dve.sem, 1)
                    dve.wait_ge(oc_psum.sem, oc_psum.upto(l, 1))
                    link(V.tensor_copy(ytok[0:NS, 2, 512:768], ps[0:NS, 0, 0:256]))
                    c = ytok[:, :, 512:768]
                    link(V.tensor_tensor(sq.rearrange("p (g c) -> p g c", g=3), c, c, ALU.mult))
                    link(V.tensor_reduce(small[:, 0:12], sq.rearrange("p (a e) -> p a e", e=64), AX.X, ALU.add))
                    V.tensor_scalar(small[:, 0:12], small[:, 0:12], 1.0 / 64, RMS_EPS, ALU.mult, ALU.add)
                    dve.wait_ge(rsq_done.sem, rsq_done.upto(l, 1))
                    V.tensor_scalar(small[:, 12:24], small[:, 12:24], 1.0 / P, RMS_EPS, ALU.mult, ALU.add)\
                        .then_inc(rss_done.sem, 1)
                    dve.wait_ge(rsd_done.sem, rsd_done.upto(l, 1))
                    link(V.reciprocal(small[:, 24:48], small[:, 24:48]))
                    for g, bank in ((0, 6), (1, 7), (2, 3)):
                        w = min(P, T - P * g)
                        for h in range(HX):
                            V.scalar_tensor_tensor(ytok[0:w, g, P * h:P * h + P], ps[0:w, bank, P * h:P * h + P],
                                                   small[0:w, 36 + 4 * g + h:37 + 4 * g + h],
                                                   tmat(0, w, g, 1024 + P * h, P), ALU.mult, ALU.mult)
                    heads = view(ytok[:, 0, 512:513], [[768, 3], [64, HX], [1, 64]])
                    link(V.tensor_tensor(heads, heads, view(small[:, 24:25], [[HX, 3], [1, HX], [0, 64]]), ALU.mult))
                    V.tensor_tensor(heads, heads, view(curg[:, 0:1], [[0, 3], [0, HX], [1, 64]]), ALU.mult)\
                        .then_inc(y_done.sem, 1)

                def mv_copies():
                    for n in range(2):
                        for g in range(2):
                            if g == 0:
                                dve.wait_ge(mv_psum.sem, mv_psum.upto(l, n + 1))
                            else:
                                dve.wait_ge(w_used.sem, w_used.upto(l, POS_MIX + 20 + 2 * n + 2))
                            V.tensor_copy(mvt[:, g, 512 * n:512 * n + 512], ps[:, g, :]).then_inc(mv_dve.sem, 1)

                ffn_gate(0, POS_FFN1)
                norm(0, 0.5, ffn_out(POS_FFN1))
                token_major(0)
                rotate()
                token_major(1)
                token_major(3)
                spread_queries()
                attention(0, len(MIXER))
                retention()
                norm(1, 1.0, square_out(1, POS_MIX + 12), mv_copies)
                V.memset(view(tok[:, 0, 0:1], [[1, 2048]]), 0.0).then_inc(qc_zero.sem, 1)
                attention(len(MIXER), NI)
                norm(2, 1.0, square_out(2, POS_MIX + 28))
                wait_apart(dve, "dve", out_mem.sem, out_mem.upto(l, 32))
                ffn_gate(1, POS_FFN2)
                norm(3, 0.5, ffn_out(POS_FFN2))
                assert step[0] == DVE_STEPS, step[0]


def constants():
    f = np.float32
    c = {}
    c["ident"] = np.eye(P, dtype=f)
    c["selJ"] = np.eye(P, dtype=f)[::-1].copy()
    sel_d, sel_w = np.zeros((32, P), f), np.zeros((32, 64), f)
    for h in range(HX):
        for t in range(DT):
            for b2 in range(2):
                for m in range(2):
                    sel_d[DT * h + DT - 1 - t, 64 * b2 + 16 * h + 8 * m + t] = 1
                sel_w[DT * h + DT - 1 - t, 32 * b2 + DT * h + t] = 1
    c["sel_d"], c["sel_w"] = sel_d, sel_w
    dist = OFF - np.arange(NU)
    n = np.maximum(dist, 0)
    half = NBUCKET // 2
    large = half + (np.log(np.maximum(n, 1).astype(f) / half) / math.log(128 / half) * half).astype(np.int32)
    bucket = np.where(n < half, n, np.minimum(large, NBUCKET - 1))
    c["onehot"] = (np.arange(NBUCKET)[:, None] == bucket[None]).astype(f)
    times = ((dist >= 0) & (dist <= 128)) * 1 + ((dist >= 0) & (dist <= 512) & (dist % 4 == 0)) \
        + ((dist >= 0) & (dist <= 2048) & (dist % 16 == 0))
    window = np.where(times > 0, np.log(np.maximum(times, 1)), NEG)
    causal = np.where(dist >= 0, 0.0, NEG)
    c["counts"] = np.stack([window] * HX + [causal] * HX).astype(f)
    for name, rows in (("mask_d", 64), ("mask_w", 32)):
        m = np.full((2 * rows, 4, DB), NEG, f)
        for g in range(4):
            for b2 in range(2):
                m[rows * b2:rows * b2 + rows, g, 2 * g + b2] = 0
        c[name] = m
    lg = np.log1p(-np.exp2(-5.0 - np.arange(HX)))
    i, j = np.arange(256), np.arange(P)
    rel = i[None] - j[:, None]
    c["decay"] = np.where(rel[:, None] >= 0, np.exp(lg[None, :, None] * np.maximum(rel, 0)[:, None]), 0).astype(f)
    s = np.arange(NS)
    rel = s[None] - s[:, None]
    same = (s[None] // DT == s[:, None] // DT) & (rel >= 0)
    c["decay_s"] = np.where(same[:, None], np.exp(lg[None, :, None] * np.maximum(rel, 0)[:, None]), 0).astype(f)
    part = np.arange(P) // 64
    pair = np.arange(4)
    own = (s // DT)[None, None, None, :] == (2 * pair[None, None, :, None] + part[:, None, None, None])
    c["qdec"] = (own * np.exp(lg[None, :, None, None] * (s % DT + 1.0)[None, None, None, :])).astype(f)
    c["kmask"] = ((s // DT)[:, None, None] == np.arange(DB)[None, None]) * \
        np.exp(lg[None, :, None] * (DT - 1.0 - s % DT)[:, None, None]) * 0.125
    c["kmask"] = c["kmask"].astype(f)
    tokn = np.arange(P)[:, None, None] + P * np.arange(2)[None, :, None]
    c["kdec"] = (np.exp(lg[None, None] * (SEQ - 1.0 - tokn)) * 0.125).astype(f)
    pos = np.zeros((3, P), f)
    pos[0], pos[1] = np.arange(P), P + np.arange(P)
    pos[2, :NS] = PAST + s % DT
    inv = (f(10000.0) ** (-np.arange(32, dtype=f) / f(32))).astype(f)
    ang = (pos.T[:, :, None] * inv[None, None]).astype(f)
    c["cos"], c["sin"] = np.cos(ang.astype(np.float64)).astype(f), np.sin(ang.astype(np.float64)).astype(f)
    lam = [0.8 - 0.6 * math.exp(-0.3 * i) for i in range(L)]
    row = np.zeros((P, 8), f)
    row[:, 0:2], row[:, 2:4] = lam, [1 - x for x in lam]
    m = (np.arange(P) // DT) % 2
    row[:, 4], row[:, 5] = m == 0, m == 1
    c["lconst"] = row
    return c


def kernel(**inputs):
    import concourse.bacc as _bacc
    from concourse.bass_utils import run_bass_kernel_spmd as _run

    x = {k: np.asarray(v) for k, v in inputs.items()}
    a = constants()

    def rows_of_features(t):
        return t.T.reshape(KD, P, -1).transpose(1, 0, 2)

    a["x"] = rows_of_features(np.concatenate([x["x_prompt"][0], x["x_sample"].reshape(NS, D)]))
    a["memT"] = rows_of_features(x["mem_prompt"][0])
    a["rel_bias"] = x["rel_bias"]
    a["diff_lambda"], a["diff_subln_g"] = x["diff_lambda"], x["diff_subln_g"]
    a["page_table"] = x["page_table"].reshape(1, -1)
    ln = [x[k].reshape(L, 4, KD, P).transpose(3, 0, 1, 2).reshape(P, L, 32) for k in ("ln_g", "ln_b")]
    a["ln"] = np.concatenate([ln[0], np.zeros_like(ln[0]), ln[1], np.zeros_like(ln[1])], 2)

    def stationary(w, cols):
        w = w[:, cols]
        n = w.shape[1] // P
        return w.reshape(KD, P, n, P).transpose(1, 2, 0, 3).reshape(P, n // 2, 2048).transpose(1, 0, 2)

    def moving(w, cols):
        w = w[:, cols]
        n = w.shape[1] // 512
        return w.reshape(2, 4, P, n, 512).transpose(3, 0, 2, 1, 4).reshape(2 * n, P, 2048)

    def gate_value(w):
        return w.reshape(KD, P, 2, NF, P).transpose(3, 1, 2, 0, 4).reshape(NF, P, 2048)

    def down(w):
        return w.reshape(2, 11, P, KD, P).transpose(3, 0, 2, 1, 4).reshape(16, P, 1408)

    every = np.arange(D)
    fcols = np.r_[1536:2048, 2304:2816]
    tcols = np.r_[0:1536, 2048:2304, 2816:3072]
    w16, w11 = [], []
    for l in range(L):
        w16 += [gate_value(x["ffn1_in"][l]), stationary(x["w_in"][l], fcols), moving(x["w_in"][l], tcols),
                stationary(x["w_out"][l], every), stationary(x["w_xk"][l], every), moving(x["w_xv"][l], every),
                stationary(x["w_xq"][l], every), stationary(x["w_xo"][l], every), gate_value(x["ffn2_in"][l])]
        w11 += [down(x["ffn1_out"][l]), down(x["ffn2_out"][l])]
    a["w16"], a["w11"] = np.concatenate(w16), np.concatenate(w11)

    n = x["cache_diff_k"].shape[0]
    a["dk"] = x["cache_diff_k"].reshape(n, L, PAGE, 2, P).transpose(0, 1, 4, 3, 2).reshape(n, L, P, 256)
    a["dv"] = x["cache_diff_v"].reshape(n, L, PAGE, 256)
    reach = np.r_[[i for i in range(512) if i % 16 < 8], 512:PAST].astype(int)
    a["wk"] = x["cache_win_k"][:, :, reach].reshape(DB, L, WK, 2, P).transpose(1, 0, 4, 3, 2).reshape(L, DB, P, 2 * WK)
    a["wv"] = x["cache_win_v"][:, :, reach].reshape(DB, L, WK // P, P, 256).transpose(1, 0, 3, 2, 4).reshape(L, DB, P, 2 * WK)
    a["ck"] = x["cache_mem_k"].reshape(DB, L, 256, KD, P).transpose(1, 0, 4, 3, 2).reshape(L, DB, P, 2048)
    a["cv"] = x["cache_mem_v"].reshape(DB, L, 2, P, D).transpose(1, 0, 3, 2, 4).reshape(L, DB, P, 2048)
    a["state"] = x["state_ret"].reshape(4, 2, L, HX, 64, P).transpose(2, 1, 4, 0, 3, 5).reshape(L, P, 2048)

    nc = _bacc.Bacc("TRN2", target_bir_lowering=False, num_devices=1)
    a = {k: np.ascontiguousarray(v) for k, v in a.items()}
    ins = {k: nc.dram_tensor(f"in_{k}", v.shape, mybir.dt.from_np(v.dtype), kind="ExternalInput").ap()
           for k, v in a.items()}
    ins["brow"] = nc.dram_tensor("bias_rows", [NH, NU], F32, kind="Internal").ap()
    shapes = {"x": [P, KD, T], "fm": [L, P, 2, 2 * T], "tm": [L, P, 3, 512], "s_pro": [L, 64, 512],
              "s_dec": [L, P, 2048], "mk": [L, P, 2048], "mv": [L, P, 2048]}
    outs = {k: nc.dram_tensor(f"out_{k}", s, F32, kind="ExternalOutput").ap() for k, s in shapes.items()}
    build(nc, ins, outs)
    r = _run(nc, [{f"in_{k}": v for k, v in a.items()}], core_ids=[0]).results[0]
    r = {k: np.asarray(r[f"out_{k}"]) for k in shapes}

    y = r["x"].transpose(2, 1, 0).reshape(T, D)
    fm = r["fm"].reshape(L, P, 2, 2, T).transpose(2, 0, 4, 3, 1).reshape(2, L, T, 256)
    tm = r["tm"].transpose(0, 2, 1, 3).reshape(L, 384, 512)[:, :T]
    bk, ck, bv, cv = fm[0], fm[1], tm[:, :, 0:256], tm[:, :, 256:512]

    def prompt(t):
        return t[None, :, :SEQ].reshape(1, L, SEQ, HX, 64)

    def decode(t):
        return t[:, SEQ:].reshape(L, DB, DT, HX, 64).transpose(1, 0, 2, 3, 4)

    p_ret = r["s_pro"].reshape(L, 64, HX, P).transpose(0, 2, 1, 3)[None]
    s_ret = r["s_dec"].reshape(L, 2, 64, 4, HX, P).transpose(3, 1, 0, 4, 2, 5).reshape(DB, L, HX, 64, P)
    mk = r["mk"].reshape(L, P, KD, 256).transpose(0, 3, 2, 1).reshape(1, L, 256, HX, 256)
    mv = r["mv"].reshape(L, P, 2, D).transpose(0, 2, 1, 3).reshape(1, L, 256, HX, 256)
    got = (y[None, :SEQ], y[SEQ:].reshape(DB, DT, D), prompt(ck), prompt(cv), prompt(bk), prompt(bv), p_ret, mk, mv,
           decode(ck), decode(cv), decode(bk), decode(bv), s_ret)
    return tuple(np.ascontiguousarray(t) for t in got)
```

```python
import math
from contextlib import ExitStack

import numpy as np

import concourse.bass as bass
from concourse import mybir

F32 = mybir.dt.float32
F32R = mybir.dt.float32r
I32 = mybir.dt.int32
ALU = mybir.AluOpType
ACT = mybir.ActivationFunctionType
AX = mybir.AxisListType

P = 128
D = 1024
KD = D // P
SEQ, DB, DT = 256, 8, 8
NS = DB * DT
T = SEQ + NS
L = 2
PAST, PAGE = 1024, 128
NPG = PAST // PAGE
F = 2816
NF = F // P
HX = 4
NH = 2 * HX
NBUCKET = 32
WK = 768
OFF = PAST + DT - 1
NU = 1288
ALPHA = (2 * L) ** 0.25
LN_EPS, RMS_EPS = 1e-5, 1e-6
NEG = -1e30
LOW = -3.0e38
XSCALE = 256.0 ** -0.5

RING = 4
SEGMENTS = [("w16", 22), ("w11", 16), ("w16", 32), ("w16", 22), ("w11", 16)]
SLOTS = sum(n for _, n in SEGMENTS)
POS_FFN1, POS_MIX, POS_FFN2 = 0, 38, 70
FFN_SLOTS = NF + 2 * KD
assert SLOTS % RING == 0

MIXER = [(k, i) for k in ("diff_dec", "win_dec", "win_pro", "diff_pro") for i in range(4)]
CROSS = [(k, i) for k in ("cross_dec", "cross_pro") for i in range(4)]
ITEMS = MIXER + CROSS
NI = len(ITEMS)
BATCHES = [3 if k == "diff_dec" else 1 for k, _ in ITEMS]
BEFORE = [sum(BATCHES[:i]) for i in range(NI)]
NB = sum(BATCHES)

DVE_STEPS = 79
CHUNK_DECAY = [float(np.float32(np.exp(DT * np.log1p(-2.0 ** (-5.0 - h))))) for h in range(HX)]


class Signal:

    def __init__(self, sem, per_layer, first=0):
        self.sem, self.per_layer, self.first = sem, per_layer, first

    def upto(self, layer, n):
        return layer * self.per_layer + (self.first + n)


def view(ap, dims):
    ap = ap[:]
    return bass.AP(ap.tensor, ap.offset, [list(ap.ap[0])] + [list(d) for d in dims])


def build(nc, a, o):
    ctx = ExitStack()
    with ctx:
        def sb(name, shape, dt=F32):
            return ctx.enter_context(nc.sbuf_tensor(name, shape, dt))

        def sem(name):
            return ctx.enter_context(nc.semaphore(name))

        def signal(name, per_layer, first=0):
            return Signal(sem(name), per_layer, first)

        ring = sb("ring", [P, RING, 2048])
        cache_at = nc.sbuf_base
        cache = sb("cache", [P, 4, 2048])
        xT_at = nc.sbuf_base
        xT = sb("xT", [P, KD, T])
        yT = sb("yT", [P, KD, T])
        tok = sb("tok", [P, 3, 1024])
        hid_at = nc.sbuf_base
        hid = sb("hid", [P, NF, T])
        fm_at = nc.sbuf_base
        fm = sb("fm", [P, 8, T])
        arena = sb("arena", [P, 4480])
        qd = sb("qd", [P, 2, DB, 64])
        qw = sb("qw", [P, 2, DB, 32])
        s_dec_at = nc.sbuf_base
        s_dec = sb("s_dec", [P, 4, HX, P])
        s_pro = sb("s_pro", [64, HX, P])
        bias_pro = sb("bias_pro", [P, NH, 256])
        bias_dd = sb("bias_dd", [P, PAST])
        bias_dn = sb("bias_dn", [P, 4, NS])
        bias_wd = sb("bias_wd", [64, WK])
        bias_wn = sb("bias_wn", [64, 4, NS])
        decay = sb("decay", [P, HX, 256])
        decay_s = sb("decay_s", [NS, HX, NS])
        qdec = sb("qdec", [P, HX, 4, NS])
        kmask = sb("kmask", [NS, HX, DB])
        kdec = sb("kdec", [P, 2, HX])
        cos = sb("cos", [P, 3, 32])
        sin = sb("sin", [P, 3, 32])
        ident = sb("ident", [P, P])
        heads_d = sb("heads_d", [P, 256])
        heads_w = sb("heads_w", [64, 256])
        token_d = sb("token_d", [P, 4, NS])
        token_w = sb("token_w", [64, 4, NS])
        gate = sb("gate", [P, 2, T])
        params = sb("params", [P, L, 130])
        cur = sb("cur", [P, 130])
        subg = sb("subg", [P, L, 64])
        curg = sb("curg", [P, 64])
        stat = sb("stat", [P, 2, 16])
        small = sb("small", [P, 64])
        bn = sb("bn", [P, 3, 2, 6])
        mean_var = sb("mean_var", [P, 3, 2])
        lnst = sb("lnst", [P, 3, 3])
        pt = sb("pt", [1, DB * NPG], I32)
        ps = ctx.enter_context(nc.psum_tensor("ps", [P, 8, 512], F32))

        def part(name, shape, at):
            return nc.alloc_sbuf_tensor_at(name, shape, F32R, offset=at)

        w_high = part("w_high", [P, 2, 2048], cache_at)
        w_low = part("w_low", [P, 2, 2048], cache_at + 2 * 2048 * 4)
        x_high = part("x_high", [P, KD, T], s_dec_at)
        x_low = part("x_low", [P, KD, T], xT_at)
        h_high = part("h_high", [P, NF, T], hid_at)
        h_low = part("h_low", [P, NF, T], fm_at)

        hflat = hid[:, :, :].rearrange("p a b -> p (a b)")
        def tmat(r0, r1, g, c, n):
            return hflat[r0:r1, 2048 * g + c:2048 * g + c + n]

        memT = hflat[:, 0:2048].rearrange("p (a b) -> p a b", a=KD)
        mkT = hflat[:, 2048:4096].rearrange("p (a b) -> p a b", a=KD)
        mvt = hflat[:, 4096:6144].rearrange("p (a b) -> p a b", a=2)
        tflat = tok[:, :, :].rearrange("p a b -> p (a b)")
        rp = [tflat[:, 768 * i:768 * (i + 1)].rearrange("p (g h d) -> p g h d", g=3, h=8) for i in range(4)]
        ytok = tflat[:, 0:2304].rearrange("p (g c) -> p g c", g=3)
        qc = tflat[:, 0:2048].rearrange("p (c b r) -> p c b r", c=KD, b=DB)
        prob = [arena[:, 0:1088], arena[:, 1088:2176]]
        pT = [arena[:, 2176:3328], arena[:, 3328:4480]]
        kd = arena[:, 0:512].rearrange("p (g h d) -> p g h d", g=2, h=HX)
        qTp = arena[:, 512:1024].rearrange("p (c t) -> p c t", c=2)
        kTp = arena[:, 1024:1536].rearrange("p (c t) -> p c t", c=2)
        qTs = arena[0:64, 1536:1792].rearrange("p (h t) -> p h t", h=HX)
        kTs = arena[0:64, 1792:2048].rearrange("p (h t) -> p h t", h=HX)
        qx = arena[:, 2048:3072].rearrange("p (h g t) -> p h g t", h=HX, g=4)
        aT = [arena[:, 3072:3456], arena[:, 3456:3840]]
        aTs = arena[0:NS, 3840:4096].rearrange("p (h t) -> p h t", h=HX)
        kx = fm[:, :, :].rearrange("p a b -> p (a b)")[0:NS, 0:2048].rearrange("p (h g d) -> p h g d", h=HX, g=DB)
        sq = fm[:, :, :].rearrange("p a b -> p (a b)")[:, 0:768]
        own_d = [hflat[:, 6144 + 256 * n:6400 + 256 * n] for n in range(3)] + [gate[:, 0, 0:256]]
        own_w = [tflat[0:64, 2304 + 256 * n:2560 + 256 * n] for n in range(3)] + [gate[0:64, 1, 0:256]]
        qxT = fm[:, :, 0:256]
        onehot = hflat[0:NBUCKET, 0:NU]
        counts = hflat[0:NH, 1288:1288 + NU]
        brow = hflat[0:NH, 2576:2576 + NU]
        hank_d = hflat[0:32, 3864:3864 + 1032]
        hank_w = hflat[0:32, 4896:4896 + 1032]
        rel = hflat[0:NBUCKET, 5928:5936]
        selJ = hflat[:, 5936:6064]
        sel_d = hflat[0:32, 6064:6192]
        sel_w = hflat[0:32, 6192:6256]
        mask_d = hflat[:, 6256:6288].rearrange("p (g b) -> p g b", g=4)
        mask_w = hflat[0:64, 6288:6320].rearrange("p (g b) -> p g b", g=4)
        lamv = hflat[:, 6320:6320 + 256].rearrange("p (l v d) -> p l v d", l=L, v=4)
        lamt = hflat[:, 6576:6576 + 128]
        lconst = hflat[:, 6704:6704 + 8]
        hank = tflat[:, 0:2048].rearrange("p (h c) -> p h c", h=NH)

        w_ready = [signal(f"w_ready{i}", 16 * SLOTS // RING) for i in range(RING)]
        w_used = signal("w_used", SLOTS, RING)
        k_ready = [signal(f"k_ready{i}", 16 * (4 * NPG + 8)) for i in range(2)]
        v_ready = [signal(f"v_ready{i}", 16 * (4 * NPG + 8)) for i in range(2)]
        bias_in = sem("bias_in")
        x_in = sem("x_in")
        small_in = sem("small_in")
        const_in = sem("const_in")
        hank_in = sem("hank_in")
        brow_out = sem("brow_out")
        set_pe, set_act, set_dve = sem("set_pe"), sem("set_act"), sem("set_dve")
        dve_step = signal("dve_step", DVE_STEPS)
        own_set = sem("own_set")
        cur_done = signal("cur_done", 1)
        a_psum = signal("a_psum", 2 * NF)
        silu_done = signal("silu_done", 2 * NF)
        hi_w = signal("hi_w", 2 * FFN_SLOTS)
        lo_w = signal("lo_w", 2 * FFN_SLOTS)
        hi_x = signal("hi_x", 8, 4)
        lo_x = signal("lo_x", 8)
        prod_done = signal("prod_done", 2 * NF)
        hi_h = signal("hi_h", 2 * NF)
        gate_done = signal("gate_done", 2 * NF, 2)
        out_psum = signal("out_psum", 8)
        res_done = signal("res_done", 32)
        tok_psum = signal("tok_psum", 8)
        var_done = signal("var_done", 4)
        sd_done = signal("sd_done", 4)
        par_done = signal("par_done", 4)
        norm_dve = signal("norm_dve", 4)
        norm_act = signal("norm_act", 4)
        xt_psum = signal("xt_psum", 32)
        x_act = signal("x_act", 16, 1)
        x_dve = signal("x_dve", 16, 1)
        fm_psum = signal("fm_psum", 4)
        fm_done = signal("fm_done", 8)
        tm_psum = signal("tm_psum", 8)
        tm_act = signal("tm_act", 3)
        tm_dve = signal("tm_dve", 9)
        q_built = signal("q_built", 1)
        s_psum = signal("s_psum", NI)
        m_done = signal("m_done", NI)
        e_done = signal("e_done", NI)
        p_done = signal("p_done", NI)
        t_psum = signal("t_psum", NB)
        t_done = signal("t_done", NB)
        o_psum = signal("o_psum", NI)
        o_done = signal("o_done", NI)
        rt_psum = signal("rt_psum", 4)
        rt_act = signal("rt_act", 2)
        rt_dve = signal("rt_dve", 2)
        k_decayed = signal("k_decayed", 1)
        ra_psum = signal("ra_psum", 5)
        ra_done = signal("ra_done", 5)
        ro_psum = signal("ro_psum", 2)
        st_in = signal("st_in", 16)
        st_psum = signal("st_psum", 5)
        st_act = signal("st_act", 1)
        st_dve = signal("st_dve", 4)
        oc_psum = signal("oc_psum", 1)
        rsq_done = signal("rsq_done", 1)
        rss_done = signal("rss_done", 1)
        rsd_done = signal("rsd_done", 1)
        y_done = signal("y_done", 1)
        y_psum = signal("y_psum", 6)
        y_act = signal("y_act", 6)
        mem_in = signal("mem_in", 16)
        mk_psum = signal("mk_psum", 4)
        mk_act = signal("mk_act", 8)
        mv_psum = signal("mv_psum", 2)
        mv_dve = signal("mv_dve", 4)
        qx_psum = signal("qx_psum", 4)
        qx_act = signal("qx_act", 8)
        qc_zero = signal("qc_zero", 1)
        out_prj = signal("out_prj", 32)
        out_st = signal("out_st", 32)
        out_mem = signal("out_mem", 32)
        out_x = sem("out_x")

        def banks(b, r0, r1, n):
            return view(ps[r0:r1, b, 0:1], [[1, n]])

        def layer_of(ap, l):
            return ap[bass.ds(l, 1)].rearrange("a p c -> (a p) c")

        passed = {e: sem(f"passed_{e}") for e in ("sp", "pe", "dve")}

        def wait_apart(eng, name, awaited, value):
            eng.wait_ge(awaited, value)
            eng.sem_inc(passed[name], 1)

        block = ctx.enter_context(nc.Block())

        BIAS = [(rel, "rel_bias"), (onehot, "onehot"), (counts, "counts")]
        SMALL = [(selJ, "selJ"), (sel_d, "sel_d"), (sel_w, "sel_w"), (mask_d, "mask_d"), (mask_w, "mask_w"),
                 (lconst, "lconst"), (ident[:], "ident"), (params[:, :, 0:128], "ln")]
        CONSTS = [(decay[:], "decay"), (decay_s[:], "decay_s"), (qdec[:], "qdec"),
                  (kmask[:], "kmask"), (kdec[:], "kdec"), (cos[:], "cos"), (sin[:], "sin"),
                  (heads_d[:], "heads_d"), (heads_w[:], "heads_w"), (token_d[:], "token_d"), (token_w[:], "token_w"),
                  (pt[:], "page_table")]

        @block.sync
        def _(sp):
            for dst, name in BIAS:
                sp.dma_start(dst, a[name]).then_inc(bias_in, 16)
            sp.dma_start(xT[:], a["x"]).then_inc(x_in, 16)
            for dst, name, n in ((lamv, "diff_lambda", L * 128), (subg, "diff_subln_g", L * 64)):
                sp.dma_start(view(dst, [[1, n]]), bass.AP(a[name].tensor, 0, [[0, P], [1, n]])).then_inc(small_in, 16)
            for dst, name in SMALL:
                sp.dma_start(dst, a[name]).then_inc(small_in, 16)
            sp.wait_ge(set_dve, 1)
            sp.dma_start(a["brow"], brow).then_inc(brow_out, 16)
            sp.wait_ge(brow_out, 16)
            sp.dma_start(hank[:, :, :], bass.AP(a["brow"].tensor, OFF - 255, [[1, P], [NU, NH], [1, 256]])).then_inc(hank_in, 16)
            for dst, h0 in ((hank_d, HX), (hank_w, 0)):
                src = bass.AP(a["brow"].tensor, h0 * NU, [[NU, HX], [1, DT], [1, 1032]])
                sp.dma_start(dst, src).then_inc(hank_in, 16)
            for dst, name in CONSTS:
                sp.dma_start(dst, a[name]).then_inc(const_in, 16)
            sp.wait_ge(const_in, 16 * len(CONSTS))
            with sp.Fori(0, L) as l:
                def page_numbers(g):
                    return [nc.values_load_multi_w_load_instructions(
                        pt[0:1, bass.ds(g * (2 * NPG) + b2 * NPG, NPG)], [mybir.EngineType.SP],
                        min_val=0, max_val=a["dk"].shape[0] - 1,
                        skip_runtime_bounds_check_because="a page table holds numbers of pages of its cache")[1]
                        for b2 in range(2)]

                def pages(numbers, what, ready, slot0):
                    for b2 in range(2):
                        for pg in range(NPG):
                            src = a[what][bass.ds(numbers[b2][pg], 1), bass.ds(l, 1)].rearrange("a b p c -> (a b p) c")
                            sp.dma_start(cache[:, slot0 + b2, 256 * pg:256 * pg + 256], src).then_inc(ready[b2].sem, 16)

                def diff_keys(numbers, before):
                    if before:
                        wait_apart(sp, "sp", s_psum.sem, s_psum.upto(l, before))
                    pages(numbers, "dk", k_ready, 0)

                def diff_values(numbers, before):
                    if before:
                        wait_apart(sp, "sp", o_psum.sem, o_psum.upto(l, before))
                    pages(numbers, "dv", v_ready, 2)

                def pair(name, used, before, g, ready, slot0, n):
                    sp.wait_ge(used.sem, used.upto(l, before) + g)
                    for b2 in range(2):
                        src = a[name][bass.ds(l, 1), bass.ds(g * 2 + b2, 1)].rearrange("a b p c -> (a b p) c")
                        sp.dma_start(cache[:, slot0 + b2, 0:n], src).then_inc(ready[b2].sem, 16)

                def win_keys(g):
                    pair("wk", s_psum, 4, g, k_ready, 0, 2 * WK)

                def win_values(g):
                    pair("wv", o_psum, 4, g, v_ready, 2, 2 * WK)

                def cross_keys(g, before):
                    pair("ck", s_psum, before, g, k_ready, 0, 2048)

                def cross_values(g, before):
                    pair("cv", o_psum, before, g, v_ready, 2, 2048)

                def outputs_of_projections():
                    sp.wait_ge(fm_done.sem, fm_done.upto(l, 8))
                    sp.wait_ge(tm_dve.sem, tm_dve.upto(l, 9))
                    sp.dma_start(o["fm"][bass.ds(l, 1)].rearrange("a p c t -> (a p) c t"),
                                 view(fm[:, 2, 0:1], [[4 * T, 2], [1, 2 * T]])).then_inc(out_prj.sem, 16)
                    sp.dma_start(o["tm"][bass.ds(l, 1)].rearrange("a p g c -> (a p) g c"),
                                 view(tmat(0, P, 0, 1536, 1), [[2048, 3], [1, 512]])).then_inc(out_prj.sem, 16)

                numbers = [page_numbers(0)]
                wait_apart(sp, "sp", w_used.sem, w_used.upto(l, POS_FFN1 + FFN_SLOTS))
                diff_keys(numbers[0], 0)
                diff_values(numbers[0], 0)
                sp.dma_start(view(s_dec, [[1, 2048]]), layer_of(a["state"], l)).then_inc(st_in.sem, 16)
                for g in range(1, 4):
                    numbers.append(page_numbers(g))
                    diff_keys(numbers[g], g)
                    if g == 1:
                        outputs_of_projections()
                    else:
                        diff_values(numbers[g - 1], g - 1)
                win_keys(0)
                diff_values(numbers[3], 3)
                with sp.Fori(1, 4) as g:
                    win_keys(g)
                    win_values(g - 1)
                cross_keys(0, 8)
                win_values(3)
                cross_values(0, 8)
                wait_apart(sp, "sp", st_act.sem, st_act.upto(l, 1))
                sp.dma_start(layer_of(o["s_pro"], l), view(s_pro, [[1, 512]])).then_inc(out_st.sem, 16)
                sp.wait_ge(st_dve.sem, st_dve.upto(l, 4))
                sp.dma_start(layer_of(o["s_dec"], l), view(s_dec, [[1, 2048]])).then_inc(out_st.sem, 16)
                sp.wait_ge(y_done.sem, y_done.upto(l, 1))
                sp.wait_ge(out_prj.sem, out_prj.upto(l, 32))
                sp.dma_start(memT, a["memT"]).then_inc(mem_in.sem, 16)
                cross_keys(1, len(MIXER))
                with sp.Fori(2, 4) as g:
                    cross_keys(g, len(MIXER))
                    cross_values(g - 1, len(MIXER))
                cross_values(3, len(MIXER))
                sp.wait_ge(mk_act.sem, mk_act.upto(l, 8))
                sp.dma_start(layer_of(o["mk"], l), view(mkT, [[1, 2048]])).then_inc(out_mem.sem, 16)
                sp.wait_ge(mv_dve.sem, mv_dve.upto(l, 4))
                sp.dma_start(layer_of(o["mv"], l), view(mvt, [[1, 2048]])).then_inc(out_mem.sem, 16)
            sp.wait_ge(x_act.sem, x_act.upto(L - 1, 16))
            sp.wait_ge(x_dve.sem, x_dve.upto(L - 1, 16))
            sp.dma_start(o["x"], xT[:]).then_inc(out_x, 16)
            sp.wait_ge(out_prj.sem, out_prj.upto(L - 1, 32))
            sp.wait_ge(out_mem.sem, out_mem.upto(L - 1, 32))
            sp.wait_ge(out_st.sem, out_st.upto(L - 1, 32))
            sp.wait_ge(out_x, 16)

        @block.gpsimd
        def _(pool):
            with pool.Fori(0, L) as l:
                def load(name, r, at, idx):
                    n = a[name].shape[2]
                    pool.wait_ge(w_used.sem, w_used.upto(l, 1 - RING) + at)
                    pool.dma_start(ring[:, r, 0:n],
                                   a[name][bass.ds(l * (a[name].shape[0] // L) + idx, 1)].rearrange("a p c -> (a p) c")
                                   ).then_inc(w_ready[r].sem, 16)

                pos, index = 0, {"w16": 0, "w11": 0}
                for name, count in SEGMENTS:
                    whole = count // RING * RING
                    with pool.Fori(0, whole // RING) as turn:
                        i = turn * RING
                        for j in range(RING):
                            load(name, (pos + j) % RING, i + (pos + j), i + (index[name] + j))
                    for j in range(whole, count):
                        load(name, (pos + j) % RING, pos + j, index[name] + j)
                    pos += count
                    index[name] += count

        @block.tensor
        def _(pe):
            mm = nc.tensor.matmul

            def tr(out, in_):
                return nc.tensor.transpose(out, in_, ident[0:in_.shape[0], 0:in_.shape[0]])

            pe.sem_inc(w_used.sem, RING)
            pe.wait_ge(bias_in, 16 * len(BIAS))
            for i in range(3):
                w = min(512, NU - 512 * i)
                last = mm(ps[0:NH, i, 0:w], rel, onehot[:, 512 * i:512 * i + w], start=True, stop=True)
            last.then_inc(set_pe, 1)
            pe.wait_ge(small_in, 16 * (len(SMALL) + 2))
            pe.wait_ge(hank_in, 16 * 3)
            for h in range(NH):
                last = mm(ps[:, 3 + h // 2, 256 * (h % 2):256 * (h % 2) + 256], selJ, hank[:, h, :],
                          start=True, stop=True)
            last.then_inc(set_pe, 1)
            mm(ps[:, 0, :], sel_d, hank_d[:, 0:512], start=True, stop=True)
            mm(ps[:, 1, :], sel_d, hank_d[:, 512:1024], start=True, stop=True)
            mm(ps[:, 2, 0:DT], sel_d, hank_d[:, 1024:1032], start=True, stop=True).then_inc(set_pe, 1)
            pe.wait_ge(set_dve, 4)
            mm(ps[0:64, 0, 0:256], sel_w, hank_w[:, 0:512].rearrange("p (a c) -> p a c", c=16)[:, :, 0:8],
               start=True, stop=True)
            mm(ps[0:64, 1, :], sel_w, hank_w[:, 512:1024], start=True, stop=True)
            mm(ps[0:64, 2, 0:DT], sel_w, hank_w[:, 1024:1032], start=True, stop=True).then_inc(set_pe, 1)
            pe.wait_ge(set_dve, 5)

            with pe.Fori(0, L) as l:
                def slot(pos, add=0):
                    r = w_ready[pos % RING]
                    pe.wait_ge(r.sem, r.upto(l, 16 * (pos // RING + 1)) + add)
                    return ring[:, pos % RING, :]

                def x_ready(u):
                    pe.wait_ge(x_dve.sem, x_dve.upto(l, 4 * u))
                    wait_apart(pe, "pe", x_act.sem, x_act.upto(l, 4 * u))

                def split_product(out, r, tile, high, low, first, last):
                    w = slice(tile * P, (tile + 1) * P)
                    mm(out, w_high[:, r, w], high, start=first, stop=False)
                    mm(out, w_high[:, r, w], low, start=False, stop=False)
                    return mm(out, w_low[:, r, w], high, start=False, stop=last)

                def ffn_in(u):
                    wait_apart(pe, "pe", lo_x.sem, lo_x.upto(l, 4 * (u + 1)))

                    def chunk(j, i):
                        pe.wait_ge(lo_w.sem, lo_w.upto(l, FFN_SLOTS * u + j + 1) + i)
                        pe.wait_ge(gate_done.sem, gate_done.upto(l, NF * u + j - 1) + i)
                        for half, done in ((0, a_psum), (1, w_used)):
                            for k in range(KD):
                                last = split_product(ps[:, 2 * (j % 2) + half, 0:T], j % 2, half * KD + k,
                                                     x_high[:, k, :], x_low[:, k, :], k == 0, k == KD - 1)
                            last.then_inc(done.sem, 1)

                    whole = NF // RING * RING
                    with pe.Fori(0, whole // RING) as turn:
                        i = turn * RING
                        for j in range(RING):
                            chunk(j, i)
                    for j in range(whole, NF):
                        chunk(j, 0)
                    pe.wait_ge(gate_done.sem, gate_done.upto(l, NF * (u + 1)))

                def back_to_tokens(u, m):
                    pe.wait_ge(res_done.sem, res_done.upto(l, 8 * u + m + 1))
                    for g in range(3):
                        w = min(P, T - P * g)
                        last = tr(ps[0:w, 2 + 2 * g + m // 4, P * (m % 4):P * (m % 4) + P], yT[:, m, P * g:P * g + w])
                    if m % 4 == 3:
                        last.then_inc(tok_psum.sem, 1)

                def project_ffn(u, f):
                    for m in range(KD):
                        if m >= 2:
                            pe.wait_ge(res_done.sem, res_done.upto(l, 8 * u + m - 1))
                        for half in range(2):
                            pe.wait_ge(lo_w.sem, lo_w.upto(l, FFN_SLOTS * f + NF + 2 * m + half + 1))
                            for k in range(11):
                                last = split_product(ps[:, m % 2, 0:T], half, k, h_high[:, 11 * half + k, :],
                                                     h_low[:, 11 * half + k, :], half == 0 and k == 0,
                                                     half == 1 and k == 10)
                            last.then_inc(w_used.sem, 1)
                        if m:
                            back_to_tokens(u, m - 1)
                    back_to_tokens(u, KD - 1)

                def chunks(pos0, src, n, free, even):
                    for m in range(KD):
                        if m % 2 == 0:
                            w = slot(pos0 + m // 2)
                        free(m)
                        for k in range(KD):
                            last = mm(ps[:, m % 2, 0:n], w[:, ((m % 2) * KD + k) * P:((m % 2) * KD + k + 1) * P],
                                      src[:, k, :], start=(k == 0), stop=(k == KD - 1))
                        last.then_inc((w_used if m % 2 else even).sem, 1)
                        yield m

                def project(u, pos0):
                    def free(m):
                        if m >= 2:
                            pe.wait_ge(res_done.sem, res_done.upto(l, 8 * u + m - 1))
                    for m in chunks(pos0, xT, T, free, out_psum):
                        if m:
                            back_to_tokens(u, m - 1)
                    back_to_tokens(u, KD - 1)

                def back_to_features(u):
                    pe.wait_ge(norm_dve.sem, norm_dve.upto(l, u + 1))
                    pe.wait_ge(norm_act.sem, norm_act.upto(l, u + 1))
                    for m in range(KD):
                        if m >= 2:
                            x = x_dve if m % 2 else x_act
                            pe.wait_ge(x.sem, x.upto(l, 4 * u + m // 2))
                        for g in range(3):
                            w = min(P, T - P * g)
                            last = tr(ps[:, m % 2, P * g:P * g + w], tok[0:w, g, P * m:P * m + P])
                        last.then_inc(xt_psum.sem, 1)

                def projections():
                    def free(m):
                        if m >= 2:
                            pe.wait_ge(fm_done.sem, fm_done.upto(l, m - 1))
                    for _ in chunks(POS_MIX, xT, T, free, fm_psum):
                        pass
                    for n in range(4):
                        for g in range(3):
                            i = 3 * n + g
                            if i >= 2:
                                nb, gb = divmod(i - 2, 3)
                                if nb == 2:
                                    pe.wait_ge(tm_act.sem, tm_act.upto(l, gb + 1))
                                else:
                                    pe.wait_ge(tm_dve.sem, tm_dve.upto(l, 3 * min(nb, 2) + gb + 1))
                            w = min(P, T - P * g)
                            for k in range(KD):
                                if g == 0 and k % 4 == 0:
                                    slot(POS_MIX + 4 + 2 * n + k // 4)
                                last = mm(ps[0:w, 2 + i % 2, :], xT[:, k, P * g:P * g + w],
                                          ring[:, (POS_MIX + 4 + 2 * n + k // 4) % RING, 512 * (k % 4):512 * (k % 4) + 512],
                                          start=(k == 0), stop=(k == KD - 1))
                                if g == 2 and k % 4 == 3:
                                    last.then_inc(w_used.sem, 1)
                            if g < 2:
                                last.then_inc(tm_psum.sem, 1)

                def memory():
                    pe.wait_ge(mem_in.sem, mem_in.upto(l, 16))
                    def free(m):
                        if m >= 2:
                            pe.wait_ge(mk_act.sem, mk_act.upto(l, m - 1))
                    for _ in chunks(POS_MIX + 16, memT, 256, free, mk_psum):
                        pass
                    for n in range(2):
                        for g in range(2):
                            if n == 0:
                                pe.wait_ge(mk_act.sem, mk_act.upto(l, 7 + g))
                            else:
                                pe.wait_ge(mv_dve.sem, mv_dve.upto(l, g + 1))
                            for k in range(KD):
                                if g == 0 and k % 4 == 0:
                                    slot(POS_MIX + 20 + 2 * n + k // 4)
                                last = mm(ps[:, g, :], memT[:, k, P * g:P * g + P],
                                          ring[:, (POS_MIX + 20 + 2 * n + k // 4) % RING, 512 * (k % 4):512 * (k % 4) + 512],
                                          start=(k == 0), stop=(k == KD - 1))
                                if g == 1 and k % 4 == 3:
                                    last.then_inc(w_used.sem, 1)
                            if g == 0:
                                last.then_inc(mv_psum.sem, 1)
                    pe.wait_ge(mv_dve.sem, mv_dve.upto(l, 4))

                def cache_in(ready, s, b2):
                    r = ready[b2]
                    pe.wait_ge(r.sem, r.upto(l, 16 * (NPG * min(s + 1, 4) + max(s - 3, 0))))

                def scores(i, first):
                    kind, n = ITEMS[i]
                    b0 = 3 * (i % 2)
                    if i - 2 >= first:
                        s = m_done if kind[:5] != "cross" else e_done
                        pe.wait_ge(s.sem, s.upto(l, i - 1))
                    if kind == "diff_dec":
                        for b2 in range(2):
                            cache_in(k_ready, n, b2)
                            r = 64 * b2
                            for c in range(3):
                                for hp in range(2):
                                    rhs = (view(cache[:, b2, 1024 * c + 128 * hp:1024 * c + 128 * hp + 1], [[256, 4], [1, 128]])
                                           if c < 2 else fm[:, 6 + hp, SEQ:T])
                                    last = mm(ps[r:r + 64, b0 + c, 0:(512 if c < 2 else NS)], qd[:, hp, 2 * n + b2, :], rhs,
                                              start=(hp == 0), stop=(hp == 1))
                    elif kind == "win_dec":
                        for b2 in range(2):
                            cache_in(k_ready, 4 + n, b2)
                            r = 32 * b2
                            for c, (at, w, bank, col) in enumerate(((0, 512, 0, 0), (512, 256, 1, 0), (0, NS, 1, 256))):
                                for hp in range(2):
                                    rhs = cache[:, b2, WK * hp + at:WK * hp + at + w] if c < 2 else fm[:, 2 + hp, SEQ:T]
                                    last = mm(ps[r:r + 32, b0 + bank, col:col + w], qw[:, hp, 2 * n + b2, :], rhs,
                                              start=(hp == 0), stop=(hp == 1))
                    elif kind in ("win_pro", "diff_pro"):
                        maps = 1 if kind == "win_pro" else 2
                        for m in range(maps):
                            r, w = 64 * (n % 2) + 32 * m, 64 // maps
                            q0, k0 = (0, 2) if kind == "win_pro" else (4, 6)
                            q, k = fm[r:r + w, q0 + n // 2, :], fm[r:r + w, k0 + n // 2, :]
                            mm(ps[:, b0 + m, 0:128], q[:, 0:128], k[:, 0:128], start=True, stop=True)
                            last = mm(ps[:, b0 + m, 128:384], q[:, 128:256], k[:, 0:256], start=True, stop=True)
                    elif kind == "cross_dec":
                        for b2 in range(2):
                            cache_in(k_ready, 8 + n, b2)
                            r = 32 * b2
                            for c in range(KD):
                                last = mm(ps[r:r + 32, b0, 0:256], qc[:, c, 2 * n + b2, :],
                                          cache[:, b2, 256 * c:256 * c + 256], start=(c == 0), stop=(c == KD - 1))
                    else:
                        for qb in range(2):
                            for c in (2 * n, 2 * n + 1):
                                last = mm(ps[:, b0, 256 * qb:256 * qb + 256], qxT[:, c, P * qb:P * qb + P], mkT[:, c, :],
                                          start=(c == 2 * n), stop=(c == 2 * n + 1))
                    last.then_inc(s_psum.sem, 1)

                def transposes(i, first):
                    kind, n = ITEMS[i]
                    p = prob[i % 2]
                    wait_apart(pe, "pe", p_done.sem, p_done.upto(l, i + 1))
                    for b in range(BATCHES[i]):
                        if i > first or b:
                            wait_apart(pe, "pe", t_done.sem, t_done.upto(l, BEFORE[i] + b))
                        if kind == "diff_dec":
                            if b < 2:
                                for c in range(4):
                                    last = tr(ps[:, 6, P * c:P * c + P], p[:, 512 * b + P * c:512 * b + P * c + P])
                            else:
                                last = tr(ps[0:NS, 6, 0:P], p[:, PAST:PAST + NS])
                        elif kind == "win_dec":
                            for c in range(6):
                                tr(ps[:, 6, 64 * c:64 * c + 64], p[0:64, P * c:P * c + P])
                            last = tr(ps[0:NS, 6, 384:448], p[0:64, WK:WK + NS])
                        elif kind == "cross_dec":
                            for c in range(2):
                                last = tr(ps[:, 6, 64 * c:64 * c + 64], p[0:64, P * c:P * c + P])
                        elif kind == "cross_pro":
                            for qb in range(2):
                                for kb in range(2):
                                    last = tr(ps[:, 6, 256 * kb + P * qb:256 * kb + P * qb + P],
                                              p[:, 256 * qb + P * kb:256 * qb + P * kb + P])
                        else:
                            for c in range(3):
                                last = tr(ps[:, 6, P * c:P * c + P], p[:, P * c:P * c + P])
                        last.then_inc(t_psum.sem, 1)

                def values(i, first):
                    kind, n = ITEMS[i]
                    t = pT[i % 2]
                    pe.wait_ge(t_done.sem, t_done.upto(l, BEFORE[i] + BATCHES[i]))
                    if i > first:
                        pe.wait_ge(o_done.sem, o_done.upto(l, i))
                    if kind in ("diff_dec", "win_dec"):
                        nk, w, v0 = (8, 64, 256) if kind == "diff_dec" else (6, 32, 0)
                        for b2 in range(2):
                            cache_in(v_ready, n if kind == "diff_dec" else 4 + n, b2)
                            for k in range(nk + 1):
                                at = 2 * w * k + w * b2
                                if k == nk:
                                    lhs, rhs = t[0:NS, at:at + w], tmat(0, NS, 2, 1536 + v0, 256)
                                else:
                                    lhs, rhs = t[:, at:at + w], cache[:, 2 + b2, 256 * k:256 * k + 256]
                                last = mm(ps[w * b2:w * b2 + w, 7, 0:256], lhs, rhs, start=(k == 0), stop=(k == nk))
                    elif kind == "win_pro":
                        r = 64 * (n % 2)
                        mm(ps[r:r + 64, 7, 0:256], tmat(0, P, 0, 1536 + 64 * n, 64), t[:, 0:256], start=True, stop=False)
                        last = mm(ps[r:r + 64, 7, 128:256], tmat(0, P, 1, 1536 + 64 * n, 64), t[:, 256:384],
                                  start=False, stop=True)
                    elif kind == "diff_pro":
                        v = [tmat(0, P, kb, 1792 + 64 * n, 64) for kb in range(2)]
                        mm(ps[:, 7, 0:64], t[:, 0:128], v[0], start=True, stop=True)
                        mm(ps[:, 7, 64:128], t[:, 128:256], v[0], start=True, stop=False)
                        last = mm(ps[:, 7, 64:128], t[:, 256:384], v[1], start=False, stop=True)
                    elif kind == "cross_dec":
                        for c in range(KD):
                            for b2 in range(2):
                                if c == 0:
                                    cache_in(v_ready, 8 + n, b2)
                                for kb in range(2):
                                    q = 64 * kb + 32 * b2 + DT * (c // 2)
                                    last = mm(ps[:, 7, 16 * c + DT * b2:16 * c + DT * b2 + DT],
                                              cache[:, 2 + b2, 1024 * kb + P * c:1024 * kb + P * c + P],
                                              t[:, q:q + DT], start=(kb == 0), stop=(kb == 1))
                    else:
                        for cc in range(2):
                            for kb in range(2):
                                last = mm(ps[:, 7, 256 * cc:256 * cc + 256],
                                          mvt[:, kb, 256 * n + P * cc:256 * n + P * cc + P],
                                          t[:, 256 * kb:256 * kb + 256], start=(kb == 0), stop=(kb == 1))
                    last.then_inc(o_psum.sem, 1)

                def attention(first, end):
                    scores(first, first)
                    for i in range(first, end):
                        if i + 1 < end:
                            scores(i + 1, first)
                        transposes(i, first)
                        values(i, first)

                def retention():
                    pe.wait_ge(o_done.sem, o_done.upto(l, len(MIXER)))
                    for b, at in ((0, 0), (1, 256)):
                        for c in range(2):
                            for g in range(2):
                                last = tr(ps[:, b, 256 * c + P * g:256 * c + P * g + P], tmat(0, P, g, at + P * c, P))
                        last.then_inc(rt_psum.sem, 1)
                    for h in range(HX):
                        for r in (0, 64):
                            last = mm(ps[r:r + 64, 2, 64 * h:64 * h + 64], tmat(0, NS, 2, 64 * h, 64), ident[0:NS, 0:NS],
                                      start=True, stop=True)
                    last.then_inc(rt_psum.sem, 1)
                    for h in range(HX):
                        last = mm(ps[0:64, 3, 64 * h:64 * h + 64], tmat(0, NS, 2, 256 + 64 * h, 64), ident[0:NS, 0:NS],
                                  start=True, stop=True)
                    last.then_inc(rt_psum.sem, 1)
                    pe.wait_ge(rt_act.sem, rt_act.upto(l, 2))

                    def head_scores(h):
                        r = 64 * (h % 2)
                        q, k = qTp[r:r + 64, h // 2, :], kTp[r:r + 64, h // 2, :]
                        if h >= 2:
                            pe.wait_ge(ra_done.sem, ra_done.upto(l, h - 1))
                        mm(ps[:, 4 + h % 2, 0:256], k[:, 0:128], q, start=True, stop=True)
                        mm(ps[:, 4 + h % 2, 256:384], k[:, 128:256], q[:, 128:256], start=True, stop=True)\
                            .then_inc(ra_psum.sem, 1)

                    head_scores(0)
                    for h in range(HX):
                        if h + 1 < HX:
                            head_scores(h + 1)
                        pe.wait_ge(ra_done.sem, ra_done.upto(l, h + 1))
                        t, at = aT[h % 2], P * h
                        v = [tmat(0, P, g, 512 + P * h, P) for g in range(2)]
                        mm(ps[:, 6, at:at + P], t[:, 0:128], v[0], start=True, stop=True)
                        mm(ps[:, 7, at:at + P], t[:, 128:256], v[0], start=True, stop=False)
                        last = mm(ps[:, 7, at:at + P], t[:, 256:384], v[1], start=False, stop=True)
                    last.then_inc(ro_psum.sem, 1)
                    wait_apart(pe, "pe", rt_dve.sem, rt_dve.upto(l, 2))
                    for h in range(HX):
                        last = mm(ps[0:NS, 2, 64 * h:64 * h + 64], kTs[:, h, :], qTs[:, h, :], start=True, stop=True)
                    last.then_inc(ra_psum.sem, 1)
                    pe.wait_ge(ra_done.sem, ra_done.upto(l, 5))
                    wait_apart(pe, "pe", st_in.sem, st_in.upto(l, 16))
                    for h in range(HX):
                        at = P * h
                        mm(ps[0:NS, 3, at:at + P], aTs[:, h, :], tmat(0, NS, 2, 512 + P * h, P), start=True, stop=False)
                        for g in range(4):
                            last = mm(ps[0:NS, 3, at:at + P], qx[:, h, g, :], s_dec[:, g, h, :], start=False, stop=(g == 3))
                    last.then_inc(ro_psum.sem, 1)
                    pe.wait_ge(k_decayed.sem, k_decayed.upto(l, 1))
                    for h in range(HX):
                        for g in range(2):
                            last = mm(ps[0:64, 0, P * h:P * h + P], kd[:, g, h, :], tmat(0, P, g, 512 + P * h, P),
                                      start=(g == 0), stop=(g == 1))
                    last.then_inc(st_psum.sem, 1)
                    for g, bank in enumerate((1, 4, 5, 2)):
                        for h in range(HX):
                            last = mm(ps[:, bank, P * h:P * h + P],
                                      view(kx[:, h, 2 * g, 0:1], [[1, P]]), tmat(0, NS, 2, 512 + P * h, P),
                                      start=True, stop=True)
                        last.then_inc(st_psum.sem, 1)
                    wait_apart(pe, "pe", st_act.sem, st_act.upto(l, 1))
                    for n in range(4):
                        mm(ps[0:NS, 0, 0:256], token_d[:, n, :], own_d[n], start=(n == 0), stop=(n == 3))
                    for c in range(2):
                        for n in range(4):
                            last = mm(ps[:, 0, 256 + NS * c:256 + NS * c + NS], own_w[n][:, P * c:P * c + P], token_w[:, n, :],
                                      start=(n == 0), stop=(n == 3))
                    last.then_inc(oc_psum.sem, 1)
                    pe.wait_ge(y_done.sem, y_done.upto(l, 1))
                    for i, c in enumerate((0, 1, 2, 3, 6, 7)):
                        if i >= 2:
                            pe.wait_ge(y_act.sem, y_act.upto(l, i - 1))
                        for g in range(3):
                            w = min(P, T - P * g)
                            col = P * min(i, 5)
                            last = tr(ps[:, i % 2, P * g:P * g + w], ytok[0:w, g, col:col + P])
                        last.then_inc(y_psum.sem, 1)
                    pe.wait_ge(y_act.sem, y_act.upto(l, 6))

                ffn_in(0)
                project_ffn(0, 0)
                back_to_features(0)
                x_ready(1)
                projections()
                pe.wait_ge(fm_done.sem, fm_done.upto(l, 8))
                pe.wait_ge(tm_act.sem, tm_act.upto(l, 3))
                pe.wait_ge(tm_dve.sem, tm_dve.upto(l, 9))
                pe.wait_ge(q_built.sem, q_built.upto(l, 1))
                attention(0, len(MIXER))
                retention()
                project(1, POS_MIX + 12)
                memory()
                back_to_features(1)
                x_ready(2)

                def free(m):
                    if m >= 2:
                        pe.wait_ge(qx_act.sem, qx_act.upto(l, m - 1))
                for _ in chunks(POS_MIX + 24, xT, T, free, qx_psum):
                    pass
                pe.wait_ge(qx_act.sem, qx_act.upto(l, 8))
                attention(len(MIXER), NI)
                pe.wait_ge(o_done.sem, o_done.upto(l, NI))
                project(2, POS_MIX + 28)
                back_to_features(2)
                ffn_in(1)
                project_ffn(3, 1)
                back_to_features(3)

        @block.scalar
        def _(act):
            fn = nc.scalar.activation

            act.sem_inc(x_act.sem, 1)
            act.wait_ge(x_in, 16)
            fn(x_high[:], xT[:], ACT.Copy).then_inc(hi_x.sem, 4)
            act.wait_ge(set_dve, 2)
            fn(small[:, 4:8], small[:, 0:4], ACT.Exp).then_inc(set_act, 1)

            with act.Fori(0, L) as l:
                def high_weights(f, s, add=0):
                    pos = (POS_FFN1, POS_FFN2)[f] + s
                    n = 2048 if s < NF else 11 * P
                    r = w_ready[pos % RING]
                    act.wait_ge(r.sem, r.upto(l, 16 * (pos // RING + 1)) + 4 * add)
                    if s >= 2:
                        act.wait_ge(w_used.sem, w_used.upto(l, pos - 1) + add)
                    fn(w_high[:, pos % 2, 0:n], ring[:, pos % RING, 0:n], ACT.Copy).then_inc(hi_w.sem, 1)

                high_weights(0, 0)
                high_weights(0, 1)
                act.wait_ge(cur_done.sem, cur_done.upto(l, 1))

                def ffn_gate(u):
                    def chunk(j, i):
                        act.wait_ge(a_psum.sem, a_psum.upto(l, NF * u + j + 1) + i)
                        fn(gate[:, j % 2, :], ps[:, 2 * (j % 2), 0:T], ACT.Silu).then_inc(silu_done.sem, 1)
                        high_weights(u, j + 2, i)

                    whole = NF // RING * RING
                    with act.Fori(0, whole // RING) as turn:
                        i = turn * RING
                        for j in range(RING):
                            chunk(j, i)
                    for j in range(whole, NF):
                        chunk(j, 0)
                    for s in range(NF + 2, FFN_SLOTS):
                        high_weights(u, s)

                def high_x(u, pair):
                    act.wait_ge(x_act.sem, x_act.upto(l, 4 * u + pair + 1))
                    act.wait_ge(x_dve.sem, x_dve.upto(l, 4 * u + pair + 1))
                    c = slice(2 * pair, 2 * pair + 2)
                    fn(x_high[:, c, :], xT[:, c, :], ACT.Copy).then_inc(hi_x.sem, 1)

                def norm(u, fill=None):
                    act.wait_ge(var_done.sem, var_done.upto(l, u + 1))
                    fn(lnst[:, :, 1], lnst[:, :, 0], ACT.Sqrt).then_inc(sd_done.sem, 1)
                    act.wait_ge(par_done.sem, par_done.upto(l, u + 1))
                    fn(tok[:, 1, :], banks(4, 0, P, 1024), ACT.Identity, bias=lnst[:, 1, 2:3],
                       scale=lnst[:, 1, 1:2]).then_inc(norm_act.sem, 1)
                    if fill:
                        fill()
                    if u == 2:
                        act.wait_ge(out_st.sem, out_st.upto(l, 32))
                    for m in range(0, KD, 2):
                        act.wait_ge(xt_psum.sem, xt_psum.upto(l, 8 * u + m + 1))
                        fn(xT[:, m, :], ps[:, 0, 0:T], ACT.Identity, bias=cur[:, 64 + 8 * u + m:65 + 8 * u + m], scale=cur[:, 8 * u + m:8 * u + m + 1]
                           ).then_inc(x_act.sem, 1)
                        if u >= 2 and m:
                            high_x(u, m // 2 - 1)
                    if u >= 2:
                        high_x(u, 3)

                def mk_copies():
                    for m in range(KD):
                        if m % 2:
                            act.wait_ge(w_used.sem, w_used.upto(l, POS_MIX + 16 + m // 2 + 1))
                        else:
                            act.wait_ge(mk_psum.sem, mk_psum.upto(l, m // 2 + 1))
                        fn(mkT[:, m, :], ps[:, m % 2, 0:256], ACT.Copy).then_inc(mk_act.sem, 1)

                def exponentials(i):
                    kind, n = ITEMS[i]
                    p, st, b0 = prob[i % 2], stat[:, i % 2, :], 3 * (i % 2)
                    act.wait_ge(m_done.sem, m_done.upto(l, i + 1))
                    parts = {"diff_dec": [(0, P, 0, PAST + NS)], "win_dec": [(0, 64, 0, WK + NS)],
                             "win_pro": [(0, P, 0, 128), (0, P, 128, 256)],
                             "diff_pro": [(0, P, 0, 128), (0, P, 128, 256), (0, P, 384, 128), (0, P, 512, 256)],
                             "cross_dec": [(0, 64, 0, 256)], "cross_pro": [(0, P, 0, 256), (0, P, 256, 256)]}[kind]
                    for j, (r0, r1, at, w) in enumerate(parts):
                        cross = kind[:5] == "cross"
                        src = banks(b0, r0, r1, 512)[:, at:at + w] if cross else p[r0:r1, at:at + w]
                        last = fn(p[r0:r1, at:at + w], src, ACT.Exp, bias=st[r0:r1, 4 + j:5 + j],
                                  scale=XSCALE if cross else 1.0, accum_out=st[r0:r1, 8 + j:9 + j])
                    last.then_inc(e_done.sem, 1)

                def copies(i):
                    kind, n = ITEMS[i]
                    t = pT[i % 2]
                    for b in range(BATCHES[i]):
                        act.wait_ge(t_psum.sem, t_psum.upto(l, BEFORE[i] + b + 1))
                        if kind == "diff_dec":
                            last = (fn(t[:, 512 * b:512 * b + 512], ps[:, 6, :], ACT.Copy) if b < 2 else
                                    fn(t[0:NS, 1024:1152], ps[0:NS, 6, 0:P], ACT.Copy))
                        elif kind == "win_dec":
                            fn(t[:, 0:384], ps[:, 6, 0:384], ACT.Copy)
                            last = fn(t[0:NS, 384:448], ps[0:NS, 6, 384:448], ACT.Copy)
                        else:
                            w = {"cross_dec": 128, "cross_pro": 512}.get(kind, 384)
                            last = fn(t[:, 0:w], ps[:, 6, 0:w], ACT.Copy)
                        last.then_inc(t_done.sem, 1)

                def attention(first, end):
                    exponentials(first)
                    for i in range(first, end):
                        copies(i)
                        if i + 1 < end:
                            exponentials(i + 1)

                ffn_gate(0)
                norm(0)
                for m in range(8):
                    if m % 2:
                        act.wait_ge(w_used.sem, w_used.upto(l, POS_MIX + m // 2 + 1))
                    else:
                        act.wait_ge(fm_psum.sem, fm_psum.upto(l, m // 2 + 1))
                    scale = {0: 64 ** -0.5, 2: 32 ** -0.5}.get(m // 2, 1.0)
                    fn(fm[:, m, :], ps[:, m % 2, 0:T], ACT.Copy, scale=scale).then_inc(fm_done.sem, 1)
                for g in range(3):
                    if g < 2:
                        act.wait_ge(tm_psum.sem, tm_psum.upto(l, 4 + g + 1))
                    else:
                        act.wait_ge(w_used.sem, w_used.upto(l, POS_MIX + 4 + 6))
                    w = min(P, T - P * g)
                    fn(tmat(0, w, g, 1024, 512), ps[0:w, 2 + (6 + g) % 2, :], ACT.Silu).then_inc(tm_act.sem, 1)
                attention(0, len(MIXER))
                for b, dst, scale in ((0, qTp, 1.0), (1, kTp, 0.125)):
                    act.wait_ge(rt_psum.sem, rt_psum.upto(l, b + 1))
                    fn(view(dst, [[1, 512]]), ps[:, b, :], ACT.Copy, scale=scale).then_inc(rt_act.sem, 1)
                for g, bank in ((0, 6), (1, 7), (2, 3)):
                    act.wait_ge(ro_psum.sem, ro_psum.upto(l, 1 if g < 2 else 2))
                    w = min(P, T - P * g)
                    for h in range(HX):
                        last = fn(ytok[0:w, g, P * h:P * h + P], ps[0:w, bank, P * h:P * h + P], ACT.Square,
                                  accum_out=small[0:w, 12 + 4 * g + h:13 + 4 * g + h])
                last.then_inc(rsq_done.sem, 1)
                act.wait_ge(st_psum.sem, st_psum.upto(l, 1))
                fn(view(s_pro, [[1, 512]]), ps[0:64, 0, :], ACT.Copy).then_inc(st_act.sem, 1)
                act.wait_ge(rss_done.sem, rss_done.upto(l, 1))
                fn(small[:, 24:48], small[:, 0:24], ACT.Sqrt).then_inc(rsd_done.sem, 1)
                for i, c in enumerate((0, 1, 2, 3, 6, 7)):
                    act.wait_ge(y_psum.sem, y_psum.upto(l, i + 1))
                    fn(xT[:, c, :], ps[:, i % 2, 0:T], ACT.Copy).then_inc(y_act.sem, 1)
                norm(1, mk_copies)
                act.wait_ge(qc_zero.sem, qc_zero.upto(l, 1))
                for m in range(KD):
                    if m % 2:
                        act.wait_ge(w_used.sem, w_used.upto(l, POS_MIX + 24 + m // 2 + 1))
                    else:
                        act.wait_ge(qx_psum.sem, qx_psum.upto(l, m // 2 + 1))
                    fn(qxT[:, m, :], ps[:, m % 2, 0:SEQ], ACT.Copy)
                    fn(qc[:, m, :, DT * (m // 2):DT * (m // 2) + DT],
                       ps[:, m % 2, SEQ:T].rearrange("p (b t) -> p b t", b=DB), ACT.Copy).then_inc(qx_act.sem, 1)
                attention(len(MIXER), NI)
                high_weights(1, 0)
                high_weights(1, 1)
                norm(2)
                ffn_gate(1)
                norm(3)

        @block.vector
        def _(dve):
            V = nc.vector
            dve.sem_inc(x_dve.sem, 1)
            dve.sem_inc(gate_done.sem, 2)
            own = [0]

            def own_step(ins):
                own[0] += 1
                ins.then_inc(own_set, 1)
                dve.wait_ge(own_set, own[0])

            V.memset(qd[:], 0.0)
            V.memset(qw[:], 0.0)
            V.memset(small[:], 1.0)
            V.memset(lnst[:], 1.0)
            V.memset(tok[:, 2, :], 0.0)
            V.memset(mean_var[:], 1.0)
            dve.wait_ge(bias_in, 16 * len(BIAS))
            dve.wait_ge(set_pe, 1)
            V.tensor_tensor(brow, banks(0, 0, NH, NU), counts, ALU.add).then_inc(set_dve, 1)
            dve.wait_ge(x_in, 16)
            V.tensor_scalar(yT[:], xT[:], ALPHA, None, ALU.mult)
            dve.wait_ge(small_in, 16 * (len(SMALL) + 2))
            lv = lamv[:, :, :, :]
            own_step(V.tensor_tensor(lamt.rearrange("p (l v d) -> p l v d", l=L, v=2), lv[:, :, 0::2, :], lv[:, :, 1::2, :],
                                     ALU.mult))
            V.tensor_reduce(small[:, 0:4], lamt.rearrange("p (a d) -> p a d", d=32), AX.X, ALU.add).then_inc(set_dve, 1)
            dve.wait_ge(set_pe, 2)
            V.tensor_copy(view(bias_pro[:, 0, 0:1], [[1, 2048]]), banks(3, 0, P, 2048)).then_inc(set_dve, 1)
            dve.wait_ge(set_pe, 3)
            V.tensor_copy(bias_dd[:], banks(0, 0, P, PAST))
            V.tensor_tensor(view(bias_dn[:, 0, 0:1], [[DT, 32], [1, DT]]), view(ps[:, 2, 0:1], [[0, 32], [1, DT]]),
                            view(mask_d[:, 0, 0:1], [[1, 32], [0, DT]]), ALU.add).then_inc(set_dve, 1)
            dve.wait_ge(set_pe, 4)
            V.tensor_copy(bias_wd[:, 0:256], ps[0:64, 0, 0:256])
            V.tensor_copy(bias_wd[:, 256:768], ps[0:64, 1, :])
            V.tensor_tensor(view(bias_wn[:, 0, 0:1], [[DT, 32], [1, DT]]), view(ps[0:64, 2, 0:1], [[0, 32], [1, DT]]),
                            view(mask_w[:, 0, 0:1], [[1, 32], [0, DT]]), ALU.add).then_inc(set_dve, 1)
            dve.wait_ge(set_act, 1)
            for i in range(L):
                own_step(V.tensor_tensor(params[:, i, 128:129], small[:, 5 + 2 * i:6 + 2 * i], small[:, 4 + 2 * i:5 + 2 * i],
                                         ALU.subtract))
                own_step(V.tensor_tensor(params[:, i, 128:129], params[:, i, 128:129], lconst[:, i:i + 1], ALU.subtract))
                V.scalar_tensor_tensor(params[:, i, 129:130], lconst[:, 5:6], params[:, i, 128:129], lconst[:, 4:5],
                                       ALU.mult, ALU.add)
                own_step(V.tensor_scalar(subg[:, i, :], subg[:, i, :], lconst[:, 2 + i:3 + i], None, ALU.mult))

            dve.wait_ge(const_in, 16 * len(CONSTS))
            with dve.Fori(0, L) as l:
                step = [0]

                def link(ins, alone=False):
                    step[0] += 1
                    ins.then_inc(dve_step.sem, 1)
                    if alone:
                        wait_apart(dve, "dve", dve_step.sem, dve_step.upto(l, step[0]))
                    else:
                        dve.wait_ge(dve_step.sem, dve_step.upto(l, step[0]))

                V.tensor_copy(cur[:], params[:, bass.ds(l, 1), :].rearrange("p a c -> p (a c)"))
                V.tensor_copy(curg[:], subg[:, bass.ds(l, 1), :].rearrange("p a c -> p (a c)")).then_inc(cur_done.sem, 1)
                wait_apart(dve, "dve", cur_done.sem, cur_done.upto(l, 1))
                neglam, sign = cur[:, 128:129], cur[:, 129:130]

                def low_weights(f, s, add=0):
                    pos = (POS_FFN1, POS_FFN2)[f] + s
                    n = 2048 if s < NF else 11 * P
                    dve.wait_ge(hi_w.sem, hi_w.upto(l, FFN_SLOTS * f + s + 1) + add)
                    V.tensor_tensor(w_low[:, pos % 2, 0:n], ring[:, pos % RING, 0:n],
                                    w_high[:, pos % 2, 0:n].bitcast(F32), ALU.subtract).then_inc(lo_w.sem, 1)

                def low_x(f, pair):
                    dve.wait_ge(hi_x.sem, hi_x.upto(l, 4 * (f - 1) + pair + 1))
                    c = slice(2 * pair, 2 * pair + 2)
                    V.tensor_tensor(x_low[:, c, :], xT[:, c, :], x_high[:, c, :].bitcast(F32), ALU.subtract)\
                        .then_inc(lo_x.sem, 1)

                def ffn_gate(u, pos0):
                    def chunk(j, i):
                        dve.wait_ge(silu_done.sem, silu_done.upto(l, NF * u + j + 1) + i)
                        dve.wait_ge(w_used.sem, w_used.upto(l, pos0 + j + 1) + i)
                        h, c = gate[:, j % 2:j % 2 + 1, :], bass.ds(i + j, 1)
                        V.tensor_tensor(h, h, ps[:, 2 * (j % 2) + 1:2 * (j % 2) + 2, 0:T], ALU.mult).then_inc(prod_done.sem, 1)
                        dve.wait_ge(prod_done.sem, prod_done.upto(l, NF * u + j + 1) + i)
                        V.tensor_copy(h_high[:, c, :], h).then_inc(hi_h.sem, 1)
                        dve.wait_ge(hi_h.sem, hi_h.upto(l, NF * u + j + 1) + i)
                        V.tensor_tensor(h_low[:, c, :], h, h_high[:, c, :].bitcast(F32), ALU.subtract)\
                            .then_inc(gate_done.sem, 1)
                        low_weights(u, j + 2, i)
                    whole = NF // RING * RING
                    with dve.Fori(0, whole // RING) as turn:
                        i = turn * RING
                        for j in range(RING):
                            chunk(j, i)
                    for j in range(whole, NF):
                        chunk(j, 0)

                def statistics(half):
                    for g in range(3):
                        w = min(P, T - P * g)
                        last = V.bn_stats(bn[0:w, g, half, :], ps[0:w, 2 + 2 * g + half, :])
                    return last

                def norm(u, scale, ready, fill=None, after=None):
                    for m in range(KD):
                        ready(m)
                        V.scalar_tensor_tensor(yT[:, m, :], ps[:, m % 2, 0:T], scale, yT[:, m, :], ALU.mult, ALU.add)\
                            .then_inc(res_done.sem, 1)
                        if after:
                            after(m)
                        if m == 6:
                            dve.wait_ge(tok_psum.sem, tok_psum.upto(l, 2 * u + 1))
                            statistics(0)
                    dve.wait_ge(tok_psum.sem, tok_psum.upto(l, 2 * u + 2))
                    link(statistics(1), alone=True)
                    for g in range(3):
                        w = min(P, T - P * g)
                        last = V.bn_aggr(mean_var[0:w, g, :], bn[0:w, g, :, :].rearrange("p a b -> p (a b)"))
                    link(last)
                    V.tensor_scalar(lnst[:, :, 0], mean_var[:, :, 1], LN_EPS, None, ALU.add).then_inc(var_done.sem, 1)
                    dve.wait_ge(sd_done.sem, sd_done.upto(l, u + 1))
                    link(V.reciprocal(lnst[:, :, 1], lnst[:, :, 1]))
                    V.scalar_tensor_tensor(lnst[:, :, 2], mean_var[:, :, 0], -1.0, lnst[:, :, 1], ALU.mult, ALU.mult)\
                        .then_inc(par_done.sem, 1)
                    for g in (0, 2):
                        w = min(P, T - P * g)
                        last = V.tensor_scalar(tok[0:w, g, :], banks(2 + 2 * g, 0, w, 1024), mean_var[0:w, g, 0:1],
                                               lnst[0:w, g, 1:2], ALU.subtract, ALU.mult)
                    last.then_inc(norm_dve.sem, 1)
                    if fill:
                        fill()
                    for m in range(1, KD, 2):
                        dve.wait_ge(xt_psum.sem, xt_psum.upto(l, 8 * u + m + 1))
                        V.tensor_scalar(xT[:, m, :], ps[:, 1, 0:T], cur[:, 8 * u + m:8 * u + m + 1],
                                        cur[:, 64 + 8 * u + m:65 + 8 * u + m], ALU.mult, ALU.add).then_inc(x_dve.sem, 1)
                        if m > 1:
                            residual(u, m // 2 - 1)
                    residual(u, 3)

                def residual(u, pair):
                    dve.wait_ge(x_dve.sem, x_dve.upto(l, 4 * u + pair + 1))
                    dve.wait_ge(x_act.sem, x_act.upto(l, 4 * u + pair + 1))
                    c = slice(2 * pair, 2 * pair + 2)
                    V.tensor_scalar(yT[:, c, :], xT[:, c, :], ALPHA, None, ALU.mult)
                    if u == 2:
                        low_x(1, pair)

                def ffn_out(f):
                    def ready(m):
                        if m < KD - 1:
                            low_weights(f, NF + 2 * m + 2)
                        dve.wait_ge(w_used.sem, w_used.upto(l, (POS_FFN1, POS_FFN2)[f] + NF + 2 * m + 2))

                    def after(m):
                        if m < KD - 1:
                            low_weights(f, NF + 2 * m + 3)
                    return ready, after

                def square_out(u, pos0):
                    def ready(m):
                        if m % 2:
                            dve.wait_ge(w_used.sem, w_used.upto(l, pos0 + m // 2 + 1))
                        else:
                            dve.wait_ge(out_psum.sem, out_psum.upto(l, 4 * (u - 1) + m // 2 + 1))
                    return ready

                def token_major(n):
                    for g in range(3):
                        if g < 2:
                            dve.wait_ge(tm_psum.sem, tm_psum.upto(l, 2 * n + g + 1))
                        else:
                            dve.wait_ge(w_used.sem, w_used.upto(l, POS_MIX + 4 + 2 * n + 2))
                        w = min(P, T - P * g)
                        V.tensor_copy(tmat(0, w, g, 512 * n, 512), ps[0:w, 2 + (3 * n + g) % 2, :]).then_inc(tm_dve.sem, 1)

                def rotate():
                    dve.wait_ge(tm_dve.sem, tm_dve.upto(l, 3))
                    def bc(t, g):
                        return view(t[:, g, 0:1], [[0, 8], [1, 32]])
                    def half(g, i):
                        return view(tmat(0, P, g, 32 * i, 1), [[64, 8], [1, 32]])
                    for g in range(3):
                        for i, (x, t) in enumerate(((0, cos), (1, sin), (0, sin), (1, cos))):
                            last = V.tensor_tensor(rp[i][:, g, :, :], half(g, x), bc(t, g), ALU.mult)
                    link(last)
                    for g in range(3):
                        V.tensor_tensor(half(g, 0), rp[0][:, g, :, :], rp[1][:, g, :, :], ALU.subtract)
                        last = V.tensor_tensor(half(g, 1), rp[2][:, g, :, :], rp[3][:, g, :, :], ALU.add)
                    link(last)

                def spread_queries():
                    dve.wait_ge(fm_done.sem, fm_done.upto(l, 8))
                    for hp in range(2):
                        for m in range(2):
                            r = 64 * hp + 32 * m
                            V.tensor_copy(view(qd[r:r + 32, 0, 0, 16 * hp + 8 * m:16 * hp + 8 * m + 1],
                                               [[DB * 64 + 32, 2], [64, DB], [1, DT]]),
                                          view(fm[r:r + 32, 4, SEQ:SEQ + 1], [[T, 2], [DT, DB], [1, DT]]))
                    for hp in range(2):
                        r = 64 * hp
                        last = V.tensor_copy(view(qw[r:r + 64, 0, 0, DT * hp:DT * hp + 1],
                                                  [[DB * 32 + 2 * DT, 2], [32, DB], [1, DT]]),
                                             view(fm[r:r + 64, 0, SEQ:SEQ + 1], [[T, 2], [DT, DB], [1, DT]]))
                    last.then_inc(q_built.sem, 1)

                def maxima(i):
                    kind, n = ITEMS[i]
                    p, st, b0 = prob[i % 2], stat[:, i % 2, :], 3 * (i % 2)
                    if kind[:5] != "cross":
                        wait_apart(dve, "dve", s_psum.sem, s_psum.upto(l, i + 1))
                    else:
                        dve.wait_ge(s_psum.sem, s_psum.upto(l, i + 1))

                    def add_max(r1, at, w, src, bias, j):
                        return V.tensor_tensor_reduce(out=p[0:r1, at:at + w], in0=src, in1=bias, scale=1.0, scalar=LOW,
                                                      op0=ALU.add, op1=ALU.max, accum_out=st[0:r1, j:j + 1])
                    if kind in ("diff_dec", "win_dec"):
                        r1, w, past, new = (P, PAST, bias_dd, bias_dn) if kind == "diff_dec" else (64, WK, bias_wd, bias_wn)
                        add_max(r1, 0, w, banks(b0, 0, r1, w), past[:], 0)
                        link(add_max(r1, w, NS, banks(b0, 0, r1, w + NS)[:, w:w + NS], new[:, n, :], 1))
                        V.tensor_reduce(st[0:r1, 4:5], st[0:r1, 0:2], AX.X, ALU.max, negate=True).then_inc(m_done.sem, 1)
                    elif kind in ("win_pro", "diff_pro"):
                        h = n if kind == "win_pro" else HX + n
                        maps = 1 if kind == "win_pro" else 2
                        for m in range(maps):
                            add_max(P, 384 * m, 128, ps[:, b0 + m, 0:128], bias_pro[:, h, 128:256], 2 * m)
                            last = add_max(P, 384 * m + 128, 256, ps[:, b0 + m, 128:384], bias_pro[:, h, :], 2 * m + 1)
                        link(last)
                        V.tensor_scalar(st[:, 4:4 + 2 * maps], st[:, 0:2 * maps], -1.0, None, ALU.mult)\
                            .then_inc(m_done.sem, 1)
                    else:
                        r1, k = (64, 1) if kind == "cross_dec" else (P, 2)
                        link(V.tensor_reduce(st[0:r1, 0:k], ps[0:r1, b0, 0:256 * k].rearrange("p (a b) -> p a b", a=k),
                                             AX.X, ALU.max))
                        V.tensor_scalar(st[0:r1, 4:4 + k], st[0:r1, 0:k], -XSCALE, None, ALU.mult).then_inc(m_done.sem, 1)

                def normalise(i):
                    kind, n = ITEMS[i]
                    p, st = prob[i % 2], stat[:, i % 2, :]
                    dve.wait_ge(e_done.sem, e_done.upto(l, i + 1))
                    r1, k = {"diff_dec": (P, 1), "win_dec": (64, 1), "win_pro": (P, 2), "diff_pro": (P, 4),
                             "cross_dec": (64, 1), "cross_pro": (P, 2)}[kind]
                    link(V.reciprocal(st[0:r1, 12:12 + k], st[0:r1, 8:8 + k]))
                    if kind == "diff_dec":
                        link(V.tensor_tensor(st[:, 12:13], st[:, 12:13], sign, ALU.mult))
                    if kind == "diff_pro":
                        link(V.tensor_scalar(st[:, 14:16], st[:, 14:16], neglam, None, ALU.mult))
                    parts = {"diff_dec": [(0, PAST + NS)], "win_dec": [(0, WK + NS)], "win_pro": [(0, 128), (128, 256)],
                             "diff_pro": [(0, 128), (128, 256)], "cross_dec": [(0, 256)],
                             "cross_pro": [(0, 256), (256, 256)]}[kind]
                    for j, (at, w) in enumerate(parts):
                        last = V.tensor_scalar(p[0:r1, at:at + w], p[0:r1, at:at + w], st[0:r1, 12 + j:13 + j], None, ALU.mult)
                    if kind == "diff_pro":
                        link(last)
                        for j, (at, w) in enumerate(parts):
                            last = V.scalar_tensor_tensor(p[:, at:at + w], p[:, 384 + at:384 + at + w], st[:, 14 + j:15 + j],
                                                          p[:, at:at + w], ALU.mult, ALU.add)
                    last.then_inc(p_done.sem, 1)

                def outputs(i):
                    kind, n = ITEMS[i]
                    dve.wait_ge(o_psum.sem, o_psum.upto(l, i + 1))
                    if kind == "diff_dec":
                        last = V.tensor_tensor(own_d[n], ps[:, 7, 0:256], heads_d[:], ALU.mult)
                    elif kind == "win_dec":
                        last = V.tensor_tensor(own_w[n], ps[0:64, 7, 0:256], heads_w[:], ALU.mult)
                    elif kind == "win_pro":
                        r = 64 * (n % 2)
                        last = V.tensor_copy(xT[r:r + 64, 4 + n // 2, 0:256], ps[r:r + 64, 7, 0:256])
                    elif kind == "diff_pro":
                        last = V.tensor_copy(ytok[:, 0:2, 512 + 64 * n:576 + 64 * n],
                                             ps[:, 7, 0:128].rearrange("p (g e) -> p g e", g=2))
                    elif kind == "cross_dec":
                        last = V.tensor_copy(xT[:, :, SEQ + 16 * n:SEQ + 16 * n + 16],
                                             ps[:, 7, 0:128].rearrange("p (c t) -> p c t", c=KD))
                    else:
                        last = V.tensor_copy(xT[:, 2 * n:2 * n + 2, 0:256], ps[:, 7, :].rearrange("p (c t) -> p c t", c=2))
                    last.then_inc(o_done.sem, 1)

                def attention(first, end):
                    maxima(first)
                    normalise(first)
                    for i in range(first, end):
                        if i + 1 < end:
                            maxima(i + 1)
                        outputs(i)
                        if i + 1 < end:
                            normalise(i + 1)

                def retention():
                    dve.wait_ge(out_prj.sem, out_prj.upto(l, 32))
                    for g in range(2):
                        V.tensor_tensor(kd[:, g, :, :], view(tmat(0, P, g, 256, 1), [[64, HX], [1, 64]]),
                                        view(kdec[:, g, 0:1], [[1, HX], [0, 64]]), ALU.mult)
                    V.tensor_tensor(kx[:, :, :, :], view(tmat(0, NS, 2, 256, 1), [[64, HX], [0, DB], [1, 64]]),
                                    view(kmask[:, 0, 0:1], [[DB, HX], [1, DB], [0, 64]]), ALU.mult).then_inc(k_decayed.sem, 1)
                    dve.wait_ge(rt_psum.sem, rt_psum.upto(l, 3))
                    V.tensor_copy(view(qTs, [[1, 256]]), ps[0:64, 2, 0:256])
                    V.tensor_tensor(qx[:, :, :, :], view(ps[:, 2, 0:1], [[64, HX], [0, 4], [1, NS]]), qdec[:], ALU.mult)\
                        .then_inc(rt_dve.sem, 1)
                    dve.wait_ge(rt_psum.sem, rt_psum.upto(l, 4))
                    V.tensor_scalar(view(kTs, [[1, 256]]), ps[0:64, 3, 0:256], 0.125, None, ALU.mult).then_inc(rt_dve.sem, 1)
                    for h in range(HX):
                        dve.wait_ge(ra_psum.sem, ra_psum.upto(l, h + 1))
                        V.tensor_tensor(aT[h % 2][:, 0:256], ps[:, 4 + h % 2, 0:256], decay[:, h, :], ALU.mult)
                        V.tensor_tensor(aT[h % 2][:, 256:384], ps[:, 4 + h % 2, 256:384], decay[:, h, 0:128], ALU.mult)\
                            .then_inc(ra_done.sem, 1)
                    dve.wait_ge(ra_psum.sem, ra_psum.upto(l, 5))
                    V.tensor_tensor(view(aTs, [[1, 256]]), ps[0:NS, 2, 0:256], view(decay_s[:, 0, 0:1], [[1, 256]]), ALU.mult)\
                        .then_inc(ra_done.sem, 1)
                    dve.wait_ge(ro_psum.sem, ro_psum.upto(l, 2))
                    for g, bank in enumerate((1, 4, 5, 2)):
                        dve.wait_ge(st_psum.sem, st_psum.upto(l, g + 2))
                        for h in range(HX):
                            last = V.scalar_tensor_tensor(s_dec[:, g, h, :], s_dec[:, g, h, :], CHUNK_DECAY[h],
                                                          ps[:, bank, P * h:P * h + P], ALU.mult, ALU.add)
                        last.then_inc(st_dve.sem, 1)
                    dve.wait_ge(oc_psum.sem, oc_psum.upto(l, 1))
                    V.tensor_copy(xT[:, 4:6, SEQ:T], ps[:, 0, 256:384].rearrange("p (c t) -> p c t", c=2))
                    link(V.tensor_copy(ytok[0:NS, 2, 512:768], ps[0:NS, 0, 0:256]))
                    c = ytok[:, :, 512:768]
                    link(V.tensor_tensor(sq.rearrange("p (g c) -> p g c", g=3), c, c, ALU.mult))
                    link(V.tensor_reduce(small[:, 0:12], sq.rearrange("p (a e) -> p a e", e=64), AX.X, ALU.add))
                    V.tensor_scalar(small[:, 0:12], small[:, 0:12], 1.0 / 64, RMS_EPS, ALU.mult, ALU.add)
                    dve.wait_ge(rsq_done.sem, rsq_done.upto(l, 1))
                    V.tensor_scalar(small[:, 12:24], small[:, 12:24], 1.0 / P, RMS_EPS, ALU.mult, ALU.add)\
                        .then_inc(rss_done.sem, 1)
                    dve.wait_ge(rsd_done.sem, rsd_done.upto(l, 1))
                    link(V.reciprocal(small[:, 24:48], small[:, 24:48]))
                    for g, bank in ((0, 6), (1, 7), (2, 3)):
                        w = min(P, T - P * g)
                        for h in range(HX):
                            V.scalar_tensor_tensor(ytok[0:w, g, P * h:P * h + P], ps[0:w, bank, P * h:P * h + P],
                                                   small[0:w, 36 + 4 * g + h:37 + 4 * g + h],
                                                   tmat(0, w, g, 1024 + P * h, P), ALU.mult, ALU.mult)
                    heads = view(ytok[:, 0, 512:513], [[768, 3], [64, HX], [1, 64]])
                    link(V.tensor_tensor(heads, heads, view(small[:, 24:25], [[HX, 3], [1, HX], [0, 64]]), ALU.mult))
                    V.tensor_tensor(heads, heads, view(curg[:, 0:1], [[0, 3], [0, HX], [1, 64]]), ALU.mult)\
                        .then_inc(y_done.sem, 1)

                def mv_copies():
                    for n in range(2):
                        for g in range(2):
                            if g == 0:
                                dve.wait_ge(mv_psum.sem, mv_psum.upto(l, n + 1))
                            else:
                                dve.wait_ge(w_used.sem, w_used.upto(l, POS_MIX + 20 + 2 * n + 2))
                            V.tensor_copy(mvt[:, g, 512 * n:512 * n + 512], ps[:, g, :]).then_inc(mv_dve.sem, 1)

                for pair in range(4):
                    low_x(0, pair)
                low_weights(0, 0)
                low_weights(0, 1)
                ffn_gate(0, POS_FFN1)
                ready, after = ffn_out(0)
                norm(0, 0.5, ready, after=after)
                V.memset(tmat(64, P, 2, 0, 2048), 0.0)
                token_major(0)
                rotate()
                token_major(1)
                token_major(3)
                spread_queries()
                attention(0, len(MIXER))
                retention()
                norm(1, 1.0, square_out(1, POS_MIX + 12), mv_copies)
                V.memset(view(tok[:, 0, 0:1], [[1, 2048]]), 0.0).then_inc(qc_zero.sem, 1)
                attention(len(MIXER), NI)
                norm(2, 1.0, square_out(2, POS_MIX + 28), after=lambda m: low_weights(1, m - 4) if m in (4, 5) else None)
                wait_apart(dve, "dve", out_mem.sem, out_mem.upto(l, 32))
                ffn_gate(1, POS_FFN2)
                ready, after = ffn_out(1)
                norm(3, 0.5, ready, after=after)
                assert step[0] == DVE_STEPS, step[0]


def constants():
    f = np.float32
    c = {}
    c["ident"] = np.eye(P, dtype=f)
    c["selJ"] = np.eye(P, dtype=f)[::-1].copy()
    sel_d, sel_w = np.zeros((32, P), f), np.zeros((32, 64), f)
    for h in range(HX):
        for t in range(DT):
            for b2 in range(2):
                for m in range(2):
                    sel_d[DT * h + DT - 1 - t, 64 * b2 + 16 * h + 8 * m + t] = 1
                sel_w[DT * h + DT - 1 - t, 32 * b2 + DT * h + t] = 1
    c["sel_d"], c["sel_w"] = sel_d, sel_w
    dist = OFF - np.arange(NU)
    n = np.maximum(dist, 0)
    half = NBUCKET // 2
    large = half + (np.log(np.maximum(n, 1).astype(f) / half) / math.log(128 / half) * half).astype(np.int32)
    bucket = np.where(n < half, n, np.minimum(large, NBUCKET - 1))
    c["onehot"] = (np.arange(NBUCKET)[:, None] == bucket[None]).astype(f)
    times = ((dist >= 0) & (dist <= 128)) * 1 + ((dist >= 0) & (dist <= 512) & (dist % 4 == 0)) \
        + ((dist >= 0) & (dist <= 2048) & (dist % 16 == 0))
    window = np.where(times > 0, np.log(np.maximum(times, 1)), NEG)
    causal = np.where(dist >= 0, 0.0, NEG)
    c["counts"] = np.stack([window] * HX + [causal] * HX).astype(f)
    for kind, rows, maps in (("d", 64, 2), ("w", 32, 1)):
        r = np.arange(2 * rows)
        head, b2 = r % rows // (DT * maps), r // rows
        c["heads_" + kind] = (head[:, None] == np.arange(256)[None] // 64).astype(f)
        token = DT * (2 * np.arange(4)[None] + b2[:, None]) + (r % DT)[:, None]
        c["token_" + kind] = (token[:, :, None] == np.arange(NS)).astype(f)
    for name, rows in (("mask_d", 64), ("mask_w", 32)):
        m = np.full((2 * rows, 4, DB), NEG, f)
        for g in range(4):
            for b2 in range(2):
                m[rows * b2:rows * b2 + rows, g, 2 * g + b2] = 0
        c[name] = m
    lg = np.log1p(-np.exp2(-5.0 - np.arange(HX)))
    i, j = np.arange(256), np.arange(P)
    rel = i[None] - j[:, None]
    c["decay"] = np.where(rel[:, None] >= 0, np.exp(lg[None, :, None] * np.maximum(rel, 0)[:, None]), 0).astype(f)
    s = np.arange(NS)
    rel = s[None] - s[:, None]
    same = (s[None] // DT == s[:, None] // DT) & (rel >= 0)
    c["decay_s"] = np.where(same[:, None], np.exp(lg[None, :, None] * np.maximum(rel, 0)[:, None]), 0).astype(f)
    part = np.arange(P) // 64
    pair = np.arange(4)
    own = (s // DT)[None, None, None, :] == (2 * pair[None, None, :, None] + part[:, None, None, None])
    c["qdec"] = (own * np.exp(lg[None, :, None, None] * (s % DT + 1.0)[None, None, None, :])).astype(f)
    c["kmask"] = ((s // DT)[:, None, None] == np.arange(DB)[None, None]) * \
        np.exp(lg[None, :, None] * (DT - 1.0 - s % DT)[:, None, None]) * 0.125
    c["kmask"] = c["kmask"].astype(f)
    tokn = np.arange(P)[:, None, None] + P * np.arange(2)[None, :, None]
    c["kdec"] = (np.exp(lg[None, None] * (SEQ - 1.0 - tokn)) * 0.125).astype(f)
    pos = np.zeros((3, P), f)
    pos[0], pos[1] = np.arange(P), P + np.arange(P)
    pos[2, :NS] = PAST + s % DT
    inv = (f(10000.0) ** (-np.arange(32, dtype=f) / f(32))).astype(f)
    ang = (pos.T[:, :, None] * inv[None, None]).astype(f)
    c["cos"], c["sin"] = np.cos(ang.astype(np.float64)).astype(f), np.sin(ang.astype(np.float64)).astype(f)
    lam = [0.8 - 0.6 * math.exp(-0.3 * i) for i in range(L)]
    row = np.zeros((P, 8), f)
    row[:, 0:2], row[:, 2:4] = lam, [1 - x for x in lam]
    m = (np.arange(P) // DT) % 2
    row[:, 4], row[:, 5] = m == 0, m == 1
    c["lconst"] = row
    return c


def kernel(**inputs):
    import concourse.bacc as _bacc
    from concourse.bass_utils import run_bass_kernel_spmd as _run

    x = {k: np.asarray(v) for k, v in inputs.items()}
    a = constants()

    def rows_of_features(t):
        return t.T.reshape(KD, P, -1).transpose(1, 0, 2)

    a["x"] = rows_of_features(np.concatenate([x["x_prompt"][0], x["x_sample"].reshape(NS, D)]))
    a["memT"] = rows_of_features(x["mem_prompt"][0])
    a["rel_bias"] = x["rel_bias"]
    a["diff_lambda"], a["diff_subln_g"] = x["diff_lambda"], x["diff_subln_g"]
    a["page_table"] = x["page_table"].reshape(1, -1)
    ln = [x[k].reshape(L, 4, KD, P).transpose(3, 0, 1, 2).reshape(P, L, 32) for k in ("ln_g", "ln_b")]
    a["ln"] = np.concatenate([ln[0], np.zeros_like(ln[0]), ln[1], np.zeros_like(ln[1])], 2)

    def stationary(w, cols):
        w = w[:, cols]
        n = w.shape[1] // P
        return w.reshape(KD, P, n, P).transpose(1, 2, 0, 3).reshape(P, n // 2, 2048).transpose(1, 0, 2)

    def moving(w, cols):
        w = w[:, cols]
        n = w.shape[1] // 512
        return w.reshape(2, 4, P, n, 512).transpose(3, 0, 2, 1, 4).reshape(2 * n, P, 2048)

    def gate_value(w):
        return w.reshape(KD, P, 2, NF, P).transpose(3, 1, 2, 0, 4).reshape(NF, P, 2048)

    def down(w):
        return w.reshape(2, 11, P, KD, P).transpose(3, 0, 2, 1, 4).reshape(16, P, 1408)

    every = np.arange(D)
    fcols = np.r_[1536:2048, 2304:2816]
    tcols = np.r_[0:1536, 2048:2304, 2816:3072]
    w16, w11 = [], []
    for l in range(L):
        w16 += [gate_value(x["ffn1_in"][l]), stationary(x["w_in"][l], fcols), moving(x["w_in"][l], tcols),
                stationary(x["w_out"][l], every), stationary(x["w_xk"][l], every), moving(x["w_xv"][l], every),
                stationary(x["w_xq"][l], every), stationary(x["w_xo"][l], every), gate_value(x["ffn2_in"][l])]
        w11 += [down(x["ffn1_out"][l]), down(x["ffn2_out"][l])]
    a["w16"], a["w11"] = np.concatenate(w16), np.concatenate(w11)

    n = x["cache_diff_k"].shape[0]
    a["dk"] = x["cache_diff_k"].reshape(n, L, PAGE, 2, P).transpose(0, 1, 4, 3, 2).reshape(n, L, P, 256)
    a["dv"] = x["cache_diff_v"].reshape(n, L, PAGE, 256)
    reach = np.r_[[i for i in range(512) if i % 16 < 8], 512:PAST].astype(int)
    a["wk"] = x["cache_win_k"][:, :, reach].reshape(DB, L, WK, 2, P).transpose(1, 0, 4, 3, 2).reshape(L, DB, P, 2 * WK)
    a["wv"] = x["cache_win_v"][:, :, reach].reshape(DB, L, WK // P, P, 256).transpose(1, 0, 3, 2, 4).reshape(L, DB, P, 2 * WK)
    a["ck"] = x["cache_mem_k"].reshape(DB, L, 256, KD, P).transpose(1, 0, 4, 3, 2).reshape(L, DB, P, 2048)
    a["cv"] = x["cache_mem_v"].reshape(DB, L, 2, P, D).transpose(1, 0, 3, 2, 4).reshape(L, DB, P, 2048)
    a["state"] = x["state_ret"].reshape(4, 2, L, HX, 64, P).transpose(2, 1, 4, 0, 3, 5).reshape(L, P, 2048)

    nc = _bacc.Bacc("TRN2", target_bir_lowering=False, num_devices=1)
    a = {k: np.ascontiguousarray(v) for k, v in a.items()}
    ins = {k: nc.dram_tensor(f"in_{k}", v.shape, mybir.dt.from_np(v.dtype), kind="ExternalInput").ap()
           for k, v in a.items()}
    ins["brow"] = nc.dram_tensor("bias_rows", [NH, NU], F32, kind="Internal").ap()
    shapes = {"x": [P, KD, T], "fm": [L, P, 2, 2 * T], "tm": [L, P, 3, 512], "s_pro": [L, 64, 512],
              "s_dec": [L, P, 2048], "mk": [L, P, 2048], "mv": [L, P, 2048]}
    outs = {k: nc.dram_tensor(f"out_{k}", s, F32, kind="ExternalOutput").ap() for k, s in shapes.items()}
    build(nc, ins, outs)
    r = _run(nc, [{f"in_{k}": v for k, v in a.items()}], core_ids=[0]).results[0]
    r = {k: np.asarray(r[f"out_{k}"]) for k in shapes}

    y = r["x"].transpose(2, 1, 0).reshape(T, D)
    fm = r["fm"].reshape(L, P, 2, 2, T).transpose(2, 0, 4, 3, 1).reshape(2, L, T, 256)
    tm = r["tm"].transpose(0, 2, 1, 3).reshape(L, 384, 512)[:, :T]
    bk, ck, bv, cv = fm[0], fm[1], tm[:, :, 0:256], tm[:, :, 256:512]

    def prompt(t):
        return t[None, :, :SEQ].reshape(1, L, SEQ, HX, 64)

    def decode(t):
        return t[:, SEQ:].reshape(L, DB, DT, HX, 64).transpose(1, 0, 2, 3, 4)

    p_ret = r["s_pro"].reshape(L, 64, HX, P).transpose(0, 2, 1, 3)[None]
    s_ret = r["s_dec"].reshape(L, 2, 64, 4, HX, P).transpose(3, 1, 0, 4, 2, 5).reshape(DB, L, HX, 64, P)
    mk = r["mk"].reshape(L, P, KD, 256).transpose(0, 3, 2, 1).reshape(1, L, 256, HX, 256)
    mv = r["mv"].reshape(L, P, 2, D).transpose(0, 2, 1, 3).reshape(1, L, 256, HX, 256)
    got = (y[None, :SEQ], y[SEQ:].reshape(DB, DT, D), prompt(ck), prompt(cv), prompt(bk), prompt(bv), p_ret, mk, mv,
           decode(ck), decode(cv), decode(bk), decode(bv), s_ret)
    return tuple(np.ascontiguousarray(t) for t in got)
```

```python
import math
from contextlib import ExitStack

import numpy as np

import concourse.bass as bass
from concourse import mybir

F32 = mybir.dt.float32
F32R = mybir.dt.float32r
I32 = mybir.dt.int32
ALU = mybir.AluOpType
ACT = mybir.ActivationFunctionType
AX = mybir.AxisListType

P = 128
D = 1024
KD = D // P
SEQ, DB, DT = 256, 8, 8
NS = DB * DT
T = SEQ + NS
L = 2
PAST, PAGE = 1024, 128
NPG = PAST // PAGE
F = 2816
NF = F // P
HX = 4
NH = 2 * HX
NBUCKET = 32
WK = 768
OFF = PAST + DT - 1
NU = 1288
ALPHA = (2 * L) ** 0.25
LN_EPS, RMS_EPS = 1e-5, 1e-6
NEG = -1e30
LOW = -3.0e38
XSCALE = 256.0 ** -0.5

RING = 4
SEGMENTS = [("w16", 22), ("w11", 16), ("w16", 32), ("w16", 22), ("w11", 16)]
SLOTS = sum(n for _, n in SEGMENTS)
POS_FFN1, POS_MIX, POS_FFN2 = 0, 38, 70
FFN_SLOTS = NF + 2 * KD
HALVES = 2 * (POS_FFN2 - POS_MIX)
H_FM, H_TM, H_OUT, H_MK, H_MV, H_XQ, H_XO = 0, 8, 24, 32, 40, 48, 56
assert SLOTS % RING == 0

MIXER = ([("diff_dec", 0)] + [("win_pro", i) for i in range(4)] + [("diff_dec", i) for i in (1, 2, 3)]
         + [("win_dec", 0), ("win_dec", 1), ("win_dec", 2), ("diff_pro", 0), ("win_dec", 3)]
         + [("diff_pro", i) for i in (1, 2, 3)])
CROSS = ([("cross_dec", 0), ("cross_pro", 0)] + [("cross_dec", i) for i in (1, 2, 3)]
         + [("cross_pro", i) for i in (1, 2, 3)])
ITEMS = MIXER + CROSS
NI = len(ITEMS)
BATCHES = [3 if k == "diff_dec" else 1 for k, _ in ITEMS]
BEFORE = [sum(BATCHES[:i]) for i in range(NI)]
NB = sum(BATCHES)

DVE_STEPS = 95
CHUNK_DECAY = [float(np.float32(np.exp(DT * np.log1p(-2.0 ** (-5.0 - h))))) for h in range(HX)]


class Signal:

    def __init__(self, sem, per_layer, first=0):
        self.sem, self.per_layer, self.first = sem, per_layer, first

    def upto(self, layer, n):
        return layer * self.per_layer + (self.first + n)


def view(ap, dims):
    ap = ap[:]
    return bass.AP(ap.tensor, ap.offset, [list(ap.ap[0])] + [list(d) for d in dims])


def build(nc, a, o):
    ctx = ExitStack()
    with ctx:
        def sb(name, shape, dt=F32):
            return ctx.enter_context(nc.sbuf_tensor(name, shape, dt))

        def sem(name):
            return ctx.enter_context(nc.semaphore(name))

        def signal(name, per_layer, first=0):
            return Signal(sem(name), per_layer, first)

        ring = sb("ring", [P, RING, 2048])
        cache_at = nc.sbuf_base
        cache = sb("cache", [P, 4, 2048])
        xT_at = nc.sbuf_base
        x_pad = sb("xT", [P, KD * T + 64])
        yT = sb("yT", [P, KD, T])
        tok_at = nc.sbuf_base
        tok = sb("tok", [P, 3, 1024])
        xT = x_pad[:, 0:KD * T].rearrange("p (k t) -> p k t", k=KD)
        hid_at = nc.sbuf_base
        hid = sb("hid", [P, NF, T])
        fm_at = nc.sbuf_base
        fm = sb("fm", [P, 8, T])
        arena_at = nc.sbuf_base
        arena = sb("arena", [P, 4480])
        qd = sb("qd", [P, 2, DB, 64])
        qw = sb("qw", [P, 2, DB, 32])
        s_dec_at = nc.sbuf_base
        s_dec = sb("s_dec", [P, 4, HX, P])
        s_pro = sb("s_pro", [64, HX, P])
        sb("high_pad", [P, 64])
        bias_pro = sb("bias_pro", [P, NH, 256])
        bias_dd = sb("bias_dd", [P, PAST])
        bias_dn = sb("bias_dn", [P, 4, NS])
        bias_wd = sb("bias_wd", [64, WK])
        bias_wn = sb("bias_wn", [64, 4, NS])
        decay = sb("decay", [P, HX, 256])
        decay_s = sb("decay_s", [NS, HX, NS])
        qdec = sb("qdec", [P, HX, 4, NS])
        kmask = sb("kmask", [NS, HX, DB])
        kdec = sb("kdec", [P, 2, HX])
        cos = sb("cos", [P, 3, 32])
        sin = sb("sin", [P, 3, 32])
        ident = sb("ident", [P, P])
        heads_d = sb("heads_d", [P, 256])
        heads_w = sb("heads_w", [64, 256])
        token_d = sb("token_d", [P, 4, NS])
        token_w = sb("token_w", [64, 4, NS])
        gate = sb("gate", [P, 2, T])
        params = sb("params", [P, L, 130])
        cur = sb("cur", [P, 130])
        subg = sb("subg", [P, L, 64])
        curg = sb("curg", [P, 64])
        stat = sb("stat", [P, 2, 16])
        small = sb("small", [P, 64])
        bn = sb("bn", [P, 3, 2, 6])
        mean_var = sb("mean_var", [P, 3, 2])
        lnst = sb("lnst", [P, 3, 3])
        pt = sb("pt", [1, DB * NPG], I32)
        ps = ctx.enter_context(nc.psum_tensor("ps", [P, 8, 512], F32))

        def part(name, shape, at):
            return nc.alloc_sbuf_tensor_at(name, shape, F32R, offset=at)

        w_high = part("w_high", [P, 2, 2048], cache_at)
        w_low = part("w_low", [P, 2, 2048], cache_at + 2 * 2048 * 4)
        xh_pad = part("x_high", [P, KD * T + 64], s_dec_at)
        xl_pad = part("x_low", [P, KD * T + 64], xT_at)
        x_high, x_low = (t[:, 0:KD * T].rearrange("p (k t) -> p k t", k=KD) for t in (xh_pad, xl_pad))
        h_high = part("h_high", [P, NF, T], hid_at)
        h_low = part("h_low", [P, NF, T], fm_at)
        m_high = [part("m_high", [P, 2, 1024], arena_at), part("mo_high", [P, 2, 1024], hid_at)]
        m_low = [part("m_low", [P, 2, 1024], arena_at + 8192), part("mo_low", [P, 2, 1024], tok_at)]
        mem_high = part("mem_high", [P, KD, 256], fm_at)
        mem_low = part("mem_low", [P, KD, 256], hid_at)

        hflat = hid[:, :, :].rearrange("p a b -> p (a b)")
        def tmat(r0, r1, g, c, n):
            return hflat[r0:r1, 2048 * g + c:2048 * g + c + n]

        memT = hflat[:, 0:2048].rearrange("p (a b) -> p a b", a=KD)
        mkT = hflat[:, 2048:4096].rearrange("p (a b) -> p a b", a=KD)
        mvt = hflat[:, 4096:6144].rearrange("p (a b) -> p a b", a=2)
        tflat = tok[:, :, :].rearrange("p a b -> p (a b)")
        rp = [tflat[:, 768 * i:768 * (i + 1)].rearrange("p (g h d) -> p g h d", g=3, h=8) for i in range(4)]
        ytok = tflat[:, 0:2304].rearrange("p (g c) -> p g c", g=3)
        qc = tflat[:, 0:2048].rearrange("p (c b r) -> p c b r", c=KD, b=DB)
        prob = [arena[:, 0:1088], arena[:, 1088:2176]]
        pT = [arena[:, 2176:3328], arena[:, 3328:4480]]
        own_x = [t[0:64, 128:1152] for t in pT]
        kd = arena[:, 0:512].rearrange("p (g h d) -> p g h d", g=2, h=HX)
        qTp = arena[:, 512:1024].rearrange("p (c t) -> p c t", c=2)
        kTp = arena[:, 1024:1536].rearrange("p (c t) -> p c t", c=2)
        qTs = arena[0:64, 1536:1792].rearrange("p (h t) -> p h t", h=HX)
        kTs = arena[0:64, 1792:2048].rearrange("p (h t) -> p h t", h=HX)
        qx = arena[:, 2048:3072].rearrange("p (h g t) -> p h g t", h=HX, g=4)
        aT = [arena[:, 3072:3456], arena[:, 3456:3840]]
        aTs = arena[0:NS, 3840:4096].rearrange("p (h t) -> p h t", h=HX)
        kx = fm[:, :, :].rearrange("p a b -> p (a b)")[0:NS, 0:2048].rearrange("p (h g d) -> p h g d", h=HX, g=DB)
        sq = fm[:, :, :].rearrange("p a b -> p (a b)")[:, 0:768]
        own_d = [hflat[:, 6144 + 256 * n:6400 + 256 * n] for n in range(3)] + [gate[:, 0, 0:256]]
        own_w = [tflat[0:64, 2304 + 256 * n:2560 + 256 * n] for n in range(3)] + [gate[0:64, 1, 0:256]]
        qxT = fm[:, :, 0:256]
        onehot = hflat[0:NBUCKET, 0:NU]
        counts = hflat[0:NH, 1288:1288 + NU]
        brow = hflat[0:NH, 2576:2576 + NU]
        hank_d = hflat[0:32, 3864:3864 + 1032]
        hank_w = hflat[0:32, 4896:4896 + 1032]
        rel = hflat[0:NBUCKET, 5928:5936]
        selJ = hflat[:, 5936:6064]
        sel_d = hflat[0:32, 6064:6192]
        sel_w = hflat[0:32, 6192:6256]
        mask_d = hflat[:, 6256:6288].rearrange("p (g b) -> p g b", g=4)
        mask_w = hflat[0:64, 6288:6320].rearrange("p (g b) -> p g b", g=4)
        lamv = hflat[:, 6320:6320 + 256].rearrange("p (l v d) -> p l v d", l=L, v=4)
        lamt = hflat[:, 6576:6576 + 128]
        lconst = hflat[:, 6704:6704 + 8]
        hank = tflat[:, 0:2048].rearrange("p (h c) -> p h c", h=NH)

        w_ready = [signal(f"w_ready{i}", 16 * SLOTS // RING) for i in range(RING)]
        w_used = signal("w_used", SLOTS, RING)
        k_ready = [signal(f"k_ready{i}", 16 * (4 * NPG + 8)) for i in range(2)]
        v_ready = [signal(f"v_ready{i}", 16 * (4 * NPG + 8)) for i in range(2)]
        bias_in = sem("bias_in")
        x_in = sem("x_in")
        small_in = sem("small_in")
        const_in = sem("const_in")
        hank_in = sem("hank_in")
        brow_out = sem("brow_out")
        set_pe, set_act, set_dve = sem("set_pe"), sem("set_act"), sem("set_dve")
        dve_step = signal("dve_step", DVE_STEPS)
        own_set = sem("own_set")
        cur_done = signal("cur_done", 1)
        a_psum = signal("a_psum", 2 * NF)
        silu_done = signal("silu_done", 2 * NF)
        hi_w = signal("hi_w", 2 * FFN_SLOTS)
        lo_w = signal("lo_w", 2 * FFN_SLOTS)
        hi_x = signal("hi_x", 16, 4)
        lo_x = signal("lo_x", 16)
        hi_m = signal("hi_m", HALVES)
        lo_m = signal("lo_m", HALVES)
        hi_mem = signal("hi_mem", 2)
        lo_mem = signal("lo_mem", 2)
        prod_done = signal("prod_done", 2 * NF)
        hi_h = signal("hi_h", 2 * NF)
        gate_done = signal("gate_done", 2 * NF, 2)
        out_psum = signal("out_psum", 8)
        res_done = signal("res_done", 32)
        tok_psum = signal("tok_psum", 8)
        var_done = signal("var_done", 4)
        sd_done = signal("sd_done", 4)
        par_done = signal("par_done", 4)
        norm_dve = signal("norm_dve", 8)
        norm_act = signal("norm_act", 8)
        xt_psum = signal("xt_psum", 32)
        x_act = signal("x_act", 16, 1)
        x_dve = signal("x_dve", 16, 1)
        fm_psum = signal("fm_psum", 4)
        fm_done = signal("fm_done", 8)
        tm_psum = signal("tm_psum", 8)
        tm_act = signal("tm_act", 3)
        tm_dve = signal("tm_dve", 9)
        q_built = signal("q_built", 1)
        s_psum = signal("s_psum", NI)
        m_done = signal("m_done", NI)
        e_done = signal("e_done", NI)
        p_done = signal("p_done", NI)
        t_psum = signal("t_psum", NB)
        t_done = signal("t_done", NB)
        o_psum = signal("o_psum", NI)
        xv_psum = signal("xv_psum", 4)
        xv_done = signal("xv_done", 4)
        o_done = signal("o_done", NI)
        rt_psum = signal("rt_psum", 4)
        rt_act = signal("rt_act", 2)
        rt_dve = signal("rt_dve", 2)
        k_decayed = signal("k_decayed", 1)
        ra_psum = signal("ra_psum", 5)
        ra_done = signal("ra_done", 5)
        ro_psum = signal("ro_psum", 2)
        st_in = signal("st_in", 16)
        st_psum = signal("st_psum", 5)
        st_act = signal("st_act", 1)
        st_dve = signal("st_dve", 4)
        oc_psum = signal("oc_psum", 1)
        rsq_done = signal("rsq_done", 1)
        rss_done = signal("rss_done", 2)
        rsd_done = signal("rsd_done", 2)
        ya_done = signal("ya_done", 1)
        y_done = signal("y_done", 1)
        y_psum = signal("y_psum", 6)
        y_high = signal("y_high", 7)
        y_low = signal("y_low", 7)
        mem_in = signal("mem_in", 16)
        mk_psum = signal("mk_psum", 4)
        mk_act = signal("mk_act", 8)
        mv_psum = signal("mv_psum", 4)
        mv_dve = signal("mv_dve", 4)
        qx_psum = signal("qx_psum", 4)
        qx_act = signal("qx_act", 8)
        qc_zero = signal("qc_zero", 1)
        out_prj = signal("out_prj", 32)
        out_st = signal("out_st", 32)
        out_mem = signal("out_mem", 32)
        out_x = sem("out_x")

        def banks(b, r0, r1, n):
            return view(ps[r0:r1, b, 0:1], [[1, n]])

        def layer_of(ap, l):
            return ap[bass.ds(l, 1)].rearrange("a p c -> (a p) c")

        def half_done(eng, l, q):
            if q % 2:
                eng.wait_ge(w_used.sem, w_used.upto(l, POS_MIX + q // 2 + 1))
                return
            for s, first, before in ((out_psum, H_XO, 4), (qx_psum, H_XQ, 0), (mv_psum, H_MV, 0), (mk_psum, H_MK, 0),
                                     (out_psum, H_OUT, 0), (tm_psum, H_TM, 0), (fm_psum, H_FM, 0)):
                if q >= first:
                    eng.wait_ge(s.sem, s.upto(l, before + (q - first) // 2 + 1))
                    return

        passed = {e: sem(f"passed_{e}") for e in ("sp", "pe", "dve")}

        def wait_apart(eng, name, awaited, value):
            eng.wait_ge(awaited, value)
            eng.sem_inc(passed[name], 1)

        block = ctx.enter_context(nc.Block())

        BIAS = [(rel, "rel_bias"), (onehot, "onehot"), (counts, "counts")]
        SMALL = [(selJ, "selJ"), (sel_d, "sel_d"), (sel_w, "sel_w"), (mask_d, "mask_d"), (mask_w, "mask_w"),
                 (lconst, "lconst"), (ident[:], "ident"), (params[:, :, 0:128], "ln")]
        CONSTS = [(decay[:], "decay"), (decay_s[:], "decay_s"), (qdec[:], "qdec"),
                  (kmask[:], "kmask"), (kdec[:], "kdec"), (cos[:], "cos"), (sin[:], "sin"),
                  (heads_d[:], "heads_d"), (heads_w[:], "heads_w"), (token_d[:], "token_d"), (token_w[:], "token_w"),
                  (pt[:], "page_table")]

        @block.sync
        def _(sp):
            for dst, name in BIAS:
                sp.dma_start(dst, a[name]).then_inc(bias_in, 16)
            sp.dma_start(xT[:], a["x"]).then_inc(x_in, 16)
            for dst, name, n in ((lamv, "diff_lambda", L * 128), (subg, "diff_subln_g", L * 64)):
                sp.dma_start(view(dst, [[1, n]]), bass.AP(a[name].tensor, 0, [[0, P], [1, n]])).then_inc(small_in, 16)
            for dst, name in SMALL:
                sp.dma_start(dst, a[name]).then_inc(small_in, 16)
            sp.wait_ge(set_dve, 1)
            sp.dma_start(a["brow"], brow).then_inc(brow_out, 16)
            sp.wait_ge(brow_out, 16)
            sp.dma_start(hank[:, :, :], bass.AP(a["brow"].tensor, OFF - 255, [[1, P], [NU, NH], [1, 256]])).then_inc(hank_in, 16)
            for dst, h0 in ((hank_d, HX), (hank_w, 0)):
                src = bass.AP(a["brow"].tensor, h0 * NU, [[NU, HX], [1, DT], [1, 1032]])
                sp.dma_start(dst, src).then_inc(hank_in, 16)
            for dst, name in CONSTS:
                sp.dma_start(dst, a[name]).then_inc(const_in, 16)
            sp.wait_ge(const_in, 16 * len(CONSTS))
            with sp.Fori(0, L) as l:
                def page_numbers(g):
                    return [nc.values_load_multi_w_load_instructions(
                        pt[0:1, bass.ds(g * (2 * NPG) + b2 * NPG, NPG)], [mybir.EngineType.SP],
                        min_val=0, max_val=a["dk"].shape[0] - 1,
                        skip_runtime_bounds_check_because="a page table holds numbers of pages of its cache")[1]
                        for b2 in range(2)]

                def pages(numbers, what, ready, slot0):
                    for b2 in range(2):
                        for pg in range(NPG):
                            src = a[what][bass.ds(numbers[b2][pg], 1), bass.ds(l, 1)].rearrange("a b p c -> (a b p) c")
                            sp.dma_start(cache[:, slot0 + b2, 256 * pg:256 * pg + 256], src).then_inc(ready[b2].sem, 16)

                def after(kind, g):
                    return ITEMS.index((kind, g)) + 1

                def diff_keys(numbers, before):
                    if before:
                        wait_apart(sp, "sp", s_psum.sem, s_psum.upto(l, before))
                    pages(numbers, "dk", k_ready, 0)

                def diff_values(numbers, before):
                    if before:
                        wait_apart(sp, "sp", o_psum.sem, o_psum.upto(l, before))
                    pages(numbers, "dv", v_ready, 2)

                def pair(name, used, before, g, ready, slot0, n):
                    sp.wait_ge(used.sem, used.upto(l, 0) + before)
                    for b2 in range(2):
                        src = a[name][bass.ds(l, 1), bass.ds(g * 2 + b2, 1)].rearrange("a b p c -> (a b p) c")
                        sp.dma_start(cache[:, slot0 + b2, 0:n], src).then_inc(ready[b2].sem, 16)

                assert [after("diff_dec", 3)] + [after("win_dec", g) for g in range(3)] == [8, 9, 10, 11]
                assert [after("cross_dec", g) for g in (1, 2)] == [len(MIXER) + 3, len(MIXER) + 4]

                def win_keys(g):
                    pair("wk", s_psum, g + 8, g, k_ready, 0, 2 * WK)

                def win_values(g):
                    pair("wv", o_psum, g + 8, g, v_ready, 2, 2 * WK)

                def cross_keys(g, before):
                    pair("ck", s_psum, before, g, k_ready, 0, 2048)

                def cross_values(g, used, before):
                    pair("cv", used, before, g, v_ready, 2, 2048)

                def outputs_of_projections():
                    sp.wait_ge(fm_done.sem, fm_done.upto(l, 8))
                    sp.wait_ge(tm_dve.sem, tm_dve.upto(l, 9))
                    sp.dma_start(o["fm"][bass.ds(l, 1)].rearrange("a p c t -> (a p) c t"),
                                 view(fm[:, 2, 0:1], [[4 * T, 2], [1, 2 * T]])).then_inc(out_prj.sem, 16)
                    sp.dma_start(o["tm"][bass.ds(l, 1)].rearrange("a p g c -> (a p) g c"),
                                 view(tmat(0, P, 0, 1536, 1), [[2048, 3], [1, 512]])).then_inc(out_prj.sem, 16)

                numbers = [page_numbers(0)]
                wait_apart(sp, "sp", w_used.sem, w_used.upto(l, POS_FFN1 + FFN_SLOTS))
                diff_keys(numbers[0], 0)
                diff_values(numbers[0], 0)
                numbers += [page_numbers(1), page_numbers(2)]
                diff_keys(numbers[1], after("diff_dec", 0))
                outputs_of_projections()
                sp.dma_start(view(s_dec, [[1, 2048]]), layer_of(a["state"], l)).then_inc(st_in.sem, 16)
                diff_values(numbers[1], after("diff_dec", 0))
                diff_keys(numbers[2], after("diff_dec", 1))
                numbers.append(page_numbers(3))
                diff_keys(numbers[3], after("diff_dec", 2))
                diff_values(numbers[2], after("diff_dec", 1))
                win_keys(0)
                diff_values(numbers[3], after("diff_dec", 2))
                with sp.Fori(1, 4) as g:
                    win_keys(g)
                    win_values(g - 1)
                win_values(3)
                cross_keys(0, after("win_dec", 3))
                cross_values(0, o_psum, after("win_dec", 3))
                wait_apart(sp, "sp", st_act.sem, st_act.upto(l, 1))
                sp.dma_start(layer_of(o["s_pro"], l), view(s_pro, [[1, 512]])).then_inc(out_st.sem, 16)
                sp.wait_ge(st_dve.sem, st_dve.upto(l, 4))
                sp.dma_start(layer_of(o["s_dec"], l), view(s_dec, [[1, 2048]])).then_inc(out_st.sem, 16)
                sp.wait_ge(y_done.sem, y_done.upto(l, 1))
                sp.wait_ge(out_prj.sem, out_prj.upto(l, 32))
                sp.dma_start(memT, a["memT"]).then_inc(mem_in.sem, 16)
                cross_keys(1, after("cross_dec", 0))
                with sp.Fori(2, 4) as g:
                    cross_keys(g, g + (len(MIXER) + 1))
                    cross_values(g - 1, xv_psum, g - 1)
                cross_values(3, xv_psum, 3)
                sp.wait_ge(mk_act.sem, mk_act.upto(l, 8))
                sp.dma_start(layer_of(o["mk"], l), view(mkT, [[1, 2048]])).then_inc(out_mem.sem, 16)
                sp.wait_ge(mv_dve.sem, mv_dve.upto(l, 4))
                sp.dma_start(layer_of(o["mv"], l), view(mvt, [[1, 2048]])).then_inc(out_mem.sem, 16)
            sp.wait_ge(x_act.sem, x_act.upto(L - 1, 16))
            sp.wait_ge(x_dve.sem, x_dve.upto(L - 1, 16))
            sp.dma_start(o["x"], xT[:]).then_inc(out_x, 16)
            sp.wait_ge(out_prj.sem, out_prj.upto(L - 1, 32))
            sp.wait_ge(out_mem.sem, out_mem.upto(L - 1, 32))
            sp.wait_ge(out_st.sem, out_st.upto(L - 1, 32))
            sp.wait_ge(out_x, 16)

        @block.gpsimd
        def _(pool):
            pool.wait_ge(brow_out, 16)
            with pool.Fori(0, L) as l:
                def load(name, r, at, idx):
                    n = a[name].shape[2]
                    pool.wait_ge(w_used.sem, w_used.upto(l, 1 - RING) + at)
                    pool.dma_start(ring[:, r, 0:n],
                                   a[name][bass.ds(l * (a[name].shape[0] // L) + idx, 1)].rearrange("a p c -> (a p) c")
                                   ).then_inc(w_ready[r].sem, 16)

                pos, index = 0, {"w16": 0, "w11": 0}
                for name, count in SEGMENTS:
                    whole = count // RING * RING
                    with pool.Fori(0, whole // RING) as turn:
                        i = turn * RING
                        for j in range(RING):
                            load(name, (pos + j) % RING, i + (pos + j), i + (index[name] + j))
                    for j in range(whole, count):
                        load(name, (pos + j) % RING, pos + j, index[name] + j)
                    pos += count
                    index[name] += count

        @block.tensor
        def _(pe):
            mm = nc.tensor.matmul

            def tr(out, in_):
                return nc.tensor.transpose(out, in_, ident[0:in_.shape[0], 0:in_.shape[0]])

            pe.sem_inc(w_used.sem, RING)
            pe.wait_ge(bias_in, 16 * len(BIAS))
            for i in range(3):
                w = min(512, NU - 512 * i)
                last = mm(ps[0:NH, i, 0:w], rel, onehot[:, 512 * i:512 * i + w], start=True, stop=True)
            last.then_inc(set_pe, 1)
            pe.wait_ge(small_in, 16 * (len(SMALL) + 2))
            pe.wait_ge(hank_in, 16 * 3)
            for h in range(NH):
                last = mm(ps[:, 3 + h // 2, 256 * (h % 2):256 * (h % 2) + 256], selJ, hank[:, h, :],
                          start=True, stop=True)
            last.then_inc(set_pe, 1)
            mm(ps[:, 0, :], sel_d, hank_d[:, 0:512], start=True, stop=True)
            mm(ps[:, 1, :], sel_d, hank_d[:, 512:1024], start=True, stop=True)
            mm(ps[:, 2, 0:DT], sel_d, hank_d[:, 1024:1032], start=True, stop=True).then_inc(set_pe, 1)
            pe.wait_ge(set_dve, 4)
            mm(ps[0:64, 0, 0:256], sel_w, hank_w[:, 0:512].rearrange("p (a c) -> p a c", c=16)[:, :, 0:8],
               start=True, stop=True)
            mm(ps[0:64, 1, :], sel_w, hank_w[:, 512:1024], start=True, stop=True)
            mm(ps[0:64, 2, 0:DT], sel_w, hank_w[:, 1024:1032], start=True, stop=True).then_inc(set_pe, 1)
            pe.wait_ge(set_dve, 5)

            with pe.Fori(0, L) as l:
                def three(out, wh, wl, xh, xl, first, last):
                    mm(out, wh, xh, start=first, stop=False)
                    mm(out, wh, xl, start=False, stop=False)
                    return mm(out, wl, xh, start=False, stop=last)

                def split_product(out, r, tile, high, low, first, last):
                    w = slice(tile * P, (tile + 1) * P)
                    return three(out, w_high[:, r, w], w_low[:, r, w], high, low, first, last)

                def ffn_in(u):
                    wait_apart(pe, "pe", lo_x.sem, lo_x.upto(l, 12 * u + 4))

                    def chunk(j, i):
                        pe.wait_ge(lo_w.sem, lo_w.upto(l, FFN_SLOTS * u + j + 1) + i)
                        pe.wait_ge(gate_done.sem, gate_done.upto(l, NF * u + j - 1) + i)
                        for half, done in ((0, a_psum), (1, w_used)):
                            for k in range(KD):
                                last = split_product(ps[:, 2 * (j % 2) + half, 0:T], j % 2, half * KD + k,
                                                     x_high[:, k, :], x_low[:, k, :], k == 0, k == KD - 1)
                            last.then_inc(done.sem, 1)

                    whole = NF // RING * RING
                    with pe.Fori(0, whole // RING) as turn:
                        i = turn * RING
                        for j in range(RING):
                            chunk(j, i)
                    for j in range(whole, NF):
                        chunk(j, 0)
                    pe.wait_ge(gate_done.sem, gate_done.upto(l, NF * (u + 1)))

                def back_to_tokens(u, m):
                    pe.wait_ge(res_done.sem, res_done.upto(l, 8 * u + m + 1))
                    for g in range(3):
                        w = min(P, T - P * g)
                        last = tr(ps[0:w, 2 + 2 * g + m // 4, P * (m % 4):P * (m % 4) + P], yT[:, m, P * g:P * g + w])
                    if m % 4 == 3:
                        last.then_inc(tok_psum.sem, 1)

                def project_ffn(u, f):
                    for m in range(KD):
                        if m >= 2:
                            pe.wait_ge(res_done.sem, res_done.upto(l, 8 * u + m - 1))
                        for half in range(2):
                            pe.wait_ge(lo_w.sem, lo_w.upto(l, FFN_SLOTS * f + NF + 2 * m + half + 1))
                            for k in range(11):
                                last = split_product(ps[:, m % 2, 0:T], half, k, h_high[:, 11 * half + k, :],
                                                     h_low[:, 11 * half + k, :], half == 0 and k == 0,
                                                     half == 1 and k == 10)
                            last.then_inc(w_used.sem, 1)
                        if m:
                            back_to_tokens(u, m - 1)
                    back_to_tokens(u, KD - 1)

                def half_slot(q):
                    pe.wait_ge(lo_m.sem, lo_m.upto(l, q + 1))
                    place = int(q >= H_XO)
                    return m_high[place][:, q % 2, :], m_low[place][:, q % 2, :]

                def chunks(q0, high, low, n, free, even, x_at=None):
                    for m in range(KD):
                        wh, wl = half_slot(q0 + m)
                        free(m)
                        if m < 2 and x_at is not None:
                            x = x_dve if m else x_act
                            pe.wait_ge(x.sem, x.upto(l, x_at))
                        for k in range(KD):
                            c = slice(k * P, (k + 1) * P)
                            if m == 0 and k % 2 == 0 and x_at is not None:
                                pe.wait_ge(lo_x.sem, lo_x.upto(l, x_at + k // 2 + 1))
                            last = three(ps[:, m % 2, 0:n], wh[:, c], wl[:, c], high[:, k, :], low[:, k, :],
                                         k == 0, k == KD - 1)
                        last.then_inc((w_used if m % 2 else even).sem, 1)
                        yield m

                def blocks(q0, high, low, step, groups, banks_of, free, even):
                    for n, bank0 in enumerate(banks_of):
                        for j in range(4):
                            wh, wl = half_slot(q0 + 4 * n + j)
                            if j == 0:
                                free(n)
                            for i in range(2):
                                c = slice(512 * i, 512 * i + 512)
                                for g in range(groups):
                                    at = (2 * j + i) * step + P * g
                                    xh, xl = high[:, at:at + P], low[:, at:at + P]
                                    out, first, end = ps[:, bank0 + g, :], j == 0 and i == 0, j == 3 and i == 1
                                    mm(out, xh, wh[:, c], start=first, stop=False)
                                    mm(out, xh, wl[:, c], start=False, stop=False)
                                    last = mm(out, xl, wh[:, c], start=False, stop=end)
                            last.then_inc((w_used if j % 2 else even).sem, 1)

                def project(u, q0):
                    def free(m):
                        if m >= 2:
                            pe.wait_ge(res_done.sem, res_done.upto(l, 8 * u + m - 1))
                    for m in chunks(q0, x_high, x_low, T, free, out_psum):
                        if m:
                            back_to_tokens(u, m - 1)
                    back_to_tokens(u, KD - 1)

                def back_to_features(u):
                    for m in range(KD):
                        if m % 4 == 0:
                            pe.wait_ge(norm_dve.sem, norm_dve.upto(l, 2 * u + m // 4 + 1))
                            pe.wait_ge(norm_act.sem, norm_act.upto(l, 2 * u + m // 4 + 1))
                        if m == 3:
                            pe.wait_ge(norm_dve.sem, norm_dve.upto(l, 2 * u + 2))
                        if m >= 4:
                            x = x_dve if m % 2 else x_act
                            pe.wait_ge(x.sem, x.upto(l, 4 * u + m // 2 - 1))
                        for g in range(3):
                            w = min(P, T - P * g)
                            last = tr(ps[:, m % 4, P * g:P * g + w], tok[0:w, g, P * m:P * m + P])
                        last.then_inc(xt_psum.sem, 1)

                def projections():
                    def free(m):
                        if m >= 2:
                            pe.wait_ge(fm_done.sem, fm_done.upto(l, m - 1))
                    for _ in chunks(H_FM, x_high, x_low, T, free, fm_psum, 4):
                        pass

                    def block_read(n):
                        if n >= 2:
                            pe.wait_ge(tm_dve.sem, tm_dve.upto(l, 3 * (n - 1)))
                    blocks(H_TM, xh_pad, xl_pad, T, 3, (2, 5, 2, 5), block_read, tm_psum)

                def memory():
                    pe.wait_ge(lo_mem.sem, lo_mem.upto(l, 2))
                    def free(m):
                        if m >= 2:
                            pe.wait_ge(mk_act.sem, mk_act.upto(l, m - 1))
                    for _ in chunks(H_MK, mem_high, mem_low, 256, free, mk_psum):
                        pass

                    def block_read(n):
                        read = mv_dve if n else mk_act
                        pe.wait_ge(read.sem, read.upto(l, 2 if n else 8))
                    flat = [t[:, :, :].rearrange("p k t -> p (k t)") for t in (mem_high, mem_low)]
                    blocks(H_MV, flat[0], flat[1], 256, 2, (0, 0), block_read, mv_psum)
                    pe.wait_ge(mv_dve.sem, mv_dve.upto(l, 4))

                def cache_in(ready, s, b2):
                    r = ready[b2]
                    pe.wait_ge(r.sem, r.upto(l, 16 * (NPG * min(s + 1, 4) + max(s - 3, 0))))

                def scores(i, first):
                    kind, n = ITEMS[i]
                    b0 = 3 * (i % 2)
                    if i - 2 >= first:
                        s = m_done if kind[:5] != "cross" else e_done
                        pe.wait_ge(s.sem, s.upto(l, i - 1))
                    if kind == "diff_dec":
                        for b2 in range(2):
                            cache_in(k_ready, n, b2)
                            r = 64 * b2
                            for c in range(3):
                                for hp in range(2):
                                    rhs = (view(cache[:, b2, 1024 * c + 128 * hp:1024 * c + 128 * hp + 1], [[256, 4], [1, 128]])
                                           if c < 2 else fm[:, 6 + hp, SEQ:T])
                                    last = mm(ps[r:r + 64, b0 + c, 0:(512 if c < 2 else NS)], qd[:, hp, 2 * n + b2, :], rhs,
                                              start=(hp == 0), stop=(hp == 1))
                    elif kind == "win_dec":
                        for b2 in range(2):
                            cache_in(k_ready, 4 + n, b2)
                            r = 32 * b2
                            for c, (at, w, bank, col) in enumerate(((0, 512, 0, 0), (512, 256, 1, 0), (0, NS, 1, 256))):
                                for hp in range(2):
                                    rhs = cache[:, b2, WK * hp + at:WK * hp + at + w] if c < 2 else fm[:, 2 + hp, SEQ:T]
                                    last = mm(ps[r:r + 32, b0 + bank, col:col + w], qw[:, hp, 2 * n + b2, :], rhs,
                                              start=(hp == 0), stop=(hp == 1))
                    elif kind in ("win_pro", "diff_pro"):
                        maps = 1 if kind == "win_pro" else 2
                        for m in range(maps):
                            r, w = 64 * (n % 2) + 32 * m, 64 // maps
                            q0, k0 = (0, 2) if kind == "win_pro" else (4, 6)
                            q, k = fm[r:r + w, q0 + n // 2, :], fm[r:r + w, k0 + n // 2, :]
                            mm(ps[:, b0 + m, 0:128], q[:, 0:128], k[:, 0:128], start=True, stop=True)
                            last = mm(ps[:, b0 + m, 128:384], q[:, 128:256], k[:, 0:256], start=True, stop=True)
                    elif kind == "cross_dec":
                        for b2 in range(2):
                            cache_in(k_ready, 8 + n, b2)
                            r = 32 * b2
                            for c in range(KD):
                                last = mm(ps[r:r + 32, b0, 0:256], qc[:, c, 2 * n + b2, :],
                                          cache[:, b2, 256 * c:256 * c + 256], start=(c == 0), stop=(c == KD - 1))
                    else:
                        for qb in range(2):
                            for c in (2 * n, 2 * n + 1):
                                last = mm(ps[:, b0, 256 * qb:256 * qb + 256], qxT[:, c, P * qb:P * qb + P], mkT[:, c, :],
                                          start=(c == 2 * n), stop=(c == 2 * n + 1))
                    last.then_inc(s_psum.sem, 1)

                def transposes(i, first):
                    kind, n = ITEMS[i]
                    p = prob[i % 2]
                    wait_apart(pe, "pe", p_done.sem, p_done.upto(l, i + 1))
                    for b in range(BATCHES[i]):
                        if i > first or b:
                            wait_apart(pe, "pe", t_done.sem, t_done.upto(l, BEFORE[i] + b))
                        if kind == "diff_dec":
                            if b < 2:
                                for c in range(4):
                                    last = tr(ps[:, 6, P * c:P * c + P], p[:, 512 * b + P * c:512 * b + P * c + P])
                            else:
                                last = tr(ps[0:NS, 6, 0:P], p[:, PAST:PAST + NS])
                        elif kind == "win_dec":
                            for c in range(6):
                                tr(ps[:, 6, 64 * c:64 * c + 64], p[0:64, P * c:P * c + P])
                            last = tr(ps[0:NS, 6, 384:448], p[0:64, WK:WK + NS])
                        elif kind == "cross_dec":
                            for c in range(2):
                                last = tr(ps[:, 6, 64 * c:64 * c + 64], p[0:64, P * c:P * c + P])
                        elif kind == "cross_pro":
                            for qb in range(2):
                                for kb in range(2):
                                    last = tr(ps[:, 6, 256 * kb + P * qb:256 * kb + P * qb + P],
                                              p[:, 256 * qb + P * kb:256 * qb + P * kb + P])
                        else:
                            for c in range(3):
                                last = tr(ps[:, 6, P * c:P * c + P], p[:, P * c:P * c + P])
                        last.then_inc(t_psum.sem, 1)

                def values(i, first):
                    kind, n = ITEMS[i]
                    t = pT[i % 2]
                    pe.wait_ge(t_done.sem, t_done.upto(l, BEFORE[i] + BATCHES[i]))
                    if i > first and kind != "cross_dec":
                        pe.wait_ge(o_done.sem, o_done.upto(l, i))
                    if kind in ("diff_dec", "win_dec"):
                        nk, w, v0 = (8, 64, 256) if kind == "diff_dec" else (6, 32, 0)
                        for b2 in range(2):
                            cache_in(v_ready, n if kind == "diff_dec" else 4 + n, b2)
                            for k in range(nk + 1):
                                at = 2 * w * k + w * b2
                                if k == nk:
                                    lhs, rhs = t[0:NS, at:at + w], tmat(0, NS, 2, 1536 + v0, 256)
                                else:
                                    lhs, rhs = t[:, at:at + w], cache[:, 2 + b2, 256 * k:256 * k + 256]
                                last = mm(ps[w * b2:w * b2 + w, 7, 0:256], lhs, rhs, start=(k == 0), stop=(k == nk))
                    elif kind == "win_pro":
                        r = 64 * (n % 2)
                        mm(ps[r:r + 64, 7, 0:256], tmat(0, P, 0, 1536 + 64 * n, 64), t[:, 0:256], start=True, stop=False)
                        last = mm(ps[r:r + 64, 7, 128:256], tmat(0, P, 1, 1536 + 64 * n, 64), t[:, 256:384],
                                  start=False, stop=True)
                    elif kind == "diff_pro":
                        v = [tmat(0, P, kb, 1792 + 64 * n, 64) for kb in range(2)]
                        mm(ps[:, 7, 0:64], t[:, 0:128], v[0], start=True, stop=True)
                        mm(ps[:, 7, 64:128], t[:, 128:256], v[0], start=True, stop=False)
                        last = mm(ps[:, 7, 64:128], t[:, 256:384], v[1], start=False, stop=True)
                    elif kind == "cross_dec":
                        bank = 1 + 3 * (i % 2)
                        if n >= 2:
                            pe.wait_ge(xv_done.sem, xv_done.upto(l, n - 1))
                        for b2 in range(2):
                            cache_in(v_ready, 8 + n, b2)
                            r = 32 * b2
                            for c in range(2):
                                for kb in range(2):
                                    last = mm(ps[r:r + 32, bank + c, :], t[:, 64 * kb + r:64 * kb + r + 32],
                                              cache[:, 2 + b2, 1024 * kb + 512 * c:1024 * kb + 512 * c + 512],
                                              start=(kb == 0), stop=(kb == 1))
                        last.then_inc(xv_psum.sem, 1)
                        return
                    else:
                        for cc in range(2):
                            for kb in range(2):
                                last = mm(ps[:, 7, 256 * cc:256 * cc + 256],
                                          mvt[:, kb, 256 * n + P * cc:256 * n + P * cc + P],
                                          t[:, 256 * kb:256 * kb + 256], start=(kb == 0), stop=(kb == 1))
                    last.then_inc(o_psum.sem, 1)

                def own_heads(i, first):
                    pe.wait_ge(xv_done.sem, xv_done.upto(l, ITEMS[i][1] + 1))
                    if i > first:
                        pe.wait_ge(o_done.sem, o_done.upto(l, i))
                    for c in range(KD):
                        last = mm(ps[:, 7, 16 * c:16 * c + 16], own_x[i % 2][:, P * c:P * c + P], token_w[:, 0, 0:16],
                                  start=True, stop=True)
                    last.then_inc(o_psum.sem, 1)

                def attention(first, end):
                    scores(first, first)
                    for i in range(first, end):
                        if i + 1 < end:
                            scores(i + 1, first)
                        transposes(i, first)
                        if i > first and ITEMS[i - 1][0] == "cross_dec":
                            own_heads(i - 1, first)
                        values(i, first)

                def retention():
                    pe.wait_ge(o_done.sem, o_done.upto(l, len(MIXER)))
                    for b, at in ((0, 0), (1, 256)):
                        for c in range(2):
                            for g in range(2):
                                last = tr(ps[:, b, 256 * c + P * g:256 * c + P * g + P], tmat(0, P, g, at + P * c, P))
                        last.then_inc(rt_psum.sem, 1)
                    for h in range(HX):
                        for r in (0, 64):
                            last = mm(ps[r:r + 64, 2, 64 * h:64 * h + 64], tmat(0, NS, 2, 64 * h, 64), ident[0:NS, 0:NS],
                                      start=True, stop=True)
                    last.then_inc(rt_psum.sem, 1)
                    for h in range(HX):
                        last = mm(ps[0:64, 3, 64 * h:64 * h + 64], tmat(0, NS, 2, 256 + 64 * h, 64), ident[0:NS, 0:NS],
                                  start=True, stop=True)
                    last.then_inc(rt_psum.sem, 1)
                    pe.wait_ge(rt_act.sem, rt_act.upto(l, 2))

                    def head_scores(h):
                        r = 64 * (h % 2)
                        q, k = qTp[r:r + 64, h // 2, :], kTp[r:r + 64, h // 2, :]
                        if h >= 2:
                            pe.wait_ge(ra_done.sem, ra_done.upto(l, h - 1))
                        mm(ps[:, 4 + h % 2, 0:256], k[:, 0:128], q, start=True, stop=True)
                        mm(ps[:, 4 + h % 2, 256:384], k[:, 128:256], q[:, 128:256], start=True, stop=True)\
                            .then_inc(ra_psum.sem, 1)

                    head_scores(0)
                    for h in range(HX):
                        if h + 1 < HX:
                            head_scores(h + 1)
                        pe.wait_ge(ra_done.sem, ra_done.upto(l, h + 1))
                        t, at = aT[h % 2], P * h
                        v = [tmat(0, P, g, 512 + P * h, P) for g in range(2)]
                        mm(ps[:, 6, at:at + P], t[:, 0:128], v[0], start=True, stop=True)
                        mm(ps[:, 7, at:at + P], t[:, 128:256], v[0], start=True, stop=False)
                        last = mm(ps[:, 7, at:at + P], t[:, 256:384], v[1], start=False, stop=True)
                    last.then_inc(ro_psum.sem, 1)
                    wait_apart(pe, "pe", rt_dve.sem, rt_dve.upto(l, 2))
                    for h in range(HX):
                        last = mm(ps[0:NS, 2, 64 * h:64 * h + 64], kTs[:, h, :], qTs[:, h, :], start=True, stop=True)
                    last.then_inc(ra_psum.sem, 1)
                    pe.wait_ge(ra_done.sem, ra_done.upto(l, 5))
                    wait_apart(pe, "pe", st_in.sem, st_in.upto(l, 16))
                    for h in range(HX):
                        at = P * h
                        mm(ps[0:NS, 3, at:at + P], aTs[:, h, :], tmat(0, NS, 2, 512 + P * h, P), start=True, stop=False)
                        for g in range(4):
                            last = mm(ps[0:NS, 3, at:at + P], qx[:, h, g, :], s_dec[:, g, h, :], start=False, stop=(g == 3))
                    last.then_inc(ro_psum.sem, 1)
                    pe.wait_ge(k_decayed.sem, k_decayed.upto(l, 1))
                    for h in range(HX):
                        for g in range(2):
                            last = mm(ps[0:64, 0, P * h:P * h + P], kd[:, g, h, :], tmat(0, P, g, 512 + P * h, P),
                                      start=(g == 0), stop=(g == 1))
                    last.then_inc(st_psum.sem, 1)
                    for g, bank in enumerate((1, 4, 5, 2)):
                        for h in range(HX):
                            last = mm(ps[:, bank, P * h:P * h + P],
                                      view(kx[:, h, 2 * g, 0:1], [[1, P]]), tmat(0, NS, 2, 512 + P * h, P),
                                      start=True, stop=True)
                        last.then_inc(st_psum.sem, 1)
                    wait_apart(pe, "pe", st_act.sem, st_act.upto(l, 1))
                    for n in range(4):
                        mm(ps[0:NS, 0, 0:256], token_d[:, n, :], own_d[n], start=(n == 0), stop=(n == 3))
                    for c in range(2):
                        for n in range(4):
                            last = mm(ps[:, 0, 256 + NS * c:256 + NS * c + NS], own_w[n][:, P * c:P * c + P], token_w[:, n, :],
                                      start=(n == 0), stop=(n == 3))
                    last.then_inc(oc_psum.sem, 1)
                    pe.wait_ge(ya_done.sem, ya_done.upto(l, 1))
                    for i, c in enumerate((0, 1, 2, 3, 6, 7)):
                        if i == 4:
                            pe.wait_ge(y_done.sem, y_done.upto(l, 1))
                        if i >= 2:
                            pe.wait_ge(y_low.sem, y_low.upto(l, i - 1))
                        for g in range(3):
                            w = min(P, T - P * g)
                            col = P * min(i, 5)
                            last = tr(ps[:, 6 + i % 2, P * g:P * g + w], ytok[0:w, g, col:col + P])
                        last.then_inc(y_psum.sem, 1)
                    pe.wait_ge(y_low.sem, y_low.upto(l, 7))

                ffn_in(0)
                project_ffn(0, 0)
                back_to_features(0)
                projections()
                pe.wait_ge(fm_done.sem, fm_done.upto(l, 8))
                pe.wait_ge(tm_act.sem, tm_act.upto(l, 3))
                pe.wait_ge(tm_dve.sem, tm_dve.upto(l, 9))
                pe.wait_ge(q_built.sem, q_built.upto(l, 1))
                attention(0, len(MIXER))
                retention()
                project(1, H_OUT)
                memory()
                back_to_features(1)
                def free(m):
                    if m >= 2:
                        pe.wait_ge(qx_act.sem, qx_act.upto(l, m - 1))
                for _ in chunks(H_XQ, x_high, x_low, T, free, qx_psum, 8):
                    pass
                pe.wait_ge(qx_act.sem, qx_act.upto(l, 8))
                attention(len(MIXER), NI)
                pe.wait_ge(o_done.sem, o_done.upto(l, NI))
                project(2, H_XO)
                back_to_features(2)
                ffn_in(1)
                project_ffn(3, 1)
                back_to_features(3)

        @block.scalar
        def _(act):
            fn = nc.scalar.activation

            act.sem_inc(x_act.sem, 1)
            act.wait_ge(x_in, 16)
            fn(x_high, xT, ACT.Copy).then_inc(hi_x.sem, 4)
            act.wait_ge(set_dve, 2)
            fn(small[:, 4:8], small[:, 0:4], ACT.Exp).then_inc(set_act, 1)

            with act.Fori(0, L) as l:
                def high_weights(f, s, add=0):
                    pos = (POS_FFN1, POS_FFN2)[f] + s
                    n = 2048 if s < NF else 11 * P
                    r = w_ready[pos % RING]
                    act.wait_ge(r.sem, r.upto(l, 16 * (pos // RING + 1)) + 4 * add)
                    if s >= 2:
                        act.wait_ge(w_used.sem, w_used.upto(l, pos - 1) + add)
                    fn(w_high[:, pos % 2, 0:n], ring[:, pos % RING, 0:n], ACT.Copy).then_inc(hi_w.sem, 1)

                high_weights(0, 0)
                high_weights(0, 1)
                act.wait_ge(cur_done.sem, cur_done.upto(l, 1))

                def ffn_gate(u):
                    def chunk(j, i):
                        act.wait_ge(a_psum.sem, a_psum.upto(l, NF * u + j + 1) + i)
                        fn(gate[:, j % 2, :], ps[:, 2 * (j % 2), 0:T], ACT.Silu).then_inc(silu_done.sem, 1)
                        high_weights(u, j + 2, i)

                    whole = NF // RING * RING
                    with act.Fori(0, whole // RING) as turn:
                        i = turn * RING
                        for j in range(RING):
                            chunk(j, i)
                    for j in range(whole, NF):
                        chunk(j, 0)
                    for s in range(NF + 2, FFN_SLOTS):
                        high_weights(u, s)

                def high_x(u, pair):
                    act.wait_ge(x_act.sem, x_act.upto(l, 4 * u + pair + 1))
                    act.wait_ge(x_dve.sem, x_dve.upto(l, 4 * u + pair + 1))
                    c = slice(2 * pair, 2 * pair + 2)
                    if pair % 2 == 0:
                        fn(yT[:, c, :], xT[:, c, :], ACT.Copy, scale=ALPHA)
                    fn(x_high[:, c, :], xT[:, c, :], ACT.Copy).then_inc(hi_x.sem, 1)

                def high_half(q):
                    pos, place = POS_MIX + q // 2, int(q >= H_XO)
                    if q % 2 == 0:
                        r = w_ready[pos % RING]
                        act.wait_ge(r.sem, r.upto(l, 16 * (pos // RING + 1)))
                    if q in (H_FM, H_FM + 1):
                        act.wait_ge(w_used.sem, w_used.upto(l, POS_FFN1 + FFN_SLOTS))
                    elif q in (H_OUT, H_OUT + 1):
                        act.wait_ge(st_psum.sem, st_psum.upto(l, 5))
                    elif q not in (H_XO, H_XO + 1):
                        half_done(act, l, q - 2)
                    fn(m_high[place][:, q % 2, :], ring[:, pos % RING, 1024 * (q % 2):1024 * (q % 2) + 1024], ACT.Copy)\
                        .then_inc(hi_m.sem, 1)

                def norm(u, fill=None, before=()):
                    for q in before:
                        high_half(q)
                    if u == 2:
                        high_weights(1, 0)
                        high_weights(1, 1)
                    act.wait_ge(var_done.sem, var_done.upto(l, u + 1))
                    fn(lnst[:, :, 1], lnst[:, :, 0], ACT.Sqrt).then_inc(sd_done.sem, 1)
                    act.wait_ge(par_done.sem, par_done.upto(l, u + 1))
                    for i in range(2):
                        fn(tok[:, 1, 512 * i:512 * i + 512], ps[:, 4 + i, :], ACT.Identity, bias=lnst[:, 1, 2:3],
                           scale=lnst[:, 1, 1:2]).then_inc(norm_act.sem, 1)
                    if fill:
                        fill()
                    for m in range(0, KD, 2):
                        act.wait_ge(xt_psum.sem, xt_psum.upto(l, 8 * u + m + 1))
                        fn(xT[:, m, :], ps[:, m % 4, 0:T], ACT.Identity, bias=cur[:, 64 + 8 * u + m:65 + 8 * u + m], scale=cur[:, 8 * u + m:8 * u + m + 1]
                           ).then_inc(x_act.sem, 1)
                        if m:
                            high_x(u, m // 2 - 1)
                    high_x(u, 3)

                def memory():
                    for m in range(KD):
                        if m:
                            high_half(H_MK + m + 2)
                        half_done(act, l, H_MK + m)
                        fn(mkT[:, m, :], ps[:, m % 2, 0:256], ACT.Copy).then_inc(mk_act.sem, 1)
                    for q in range(H_MV + 2, H_XQ + 2):
                        high_half(q)

                def exponentials(i):
                    kind, n = ITEMS[i]
                    p, st, b0 = prob[i % 2], stat[:, i % 2, :], 3 * (i % 2)
                    act.wait_ge(m_done.sem, m_done.upto(l, i + 1))
                    parts = {"diff_dec": [(0, P, 0, PAST + NS)], "win_dec": [(0, 64, 0, WK + NS)],
                             "win_pro": [(0, P, 0, 128), (0, P, 128, 256)],
                             "diff_pro": [(0, P, 0, 128), (0, P, 128, 256), (0, P, 384, 128), (0, P, 512, 256)],
                             "cross_dec": [(0, 64, 0, 256)], "cross_pro": [(0, P, 0, 256), (0, P, 256, 256)]}[kind]
                    for j, (r0, r1, at, w) in enumerate(parts):
                        cross = kind[:5] == "cross"
                        src = banks(b0, r0, r1, 512)[:, at:at + w] if cross else p[r0:r1, at:at + w]
                        last = fn(p[r0:r1, at:at + w], src, ACT.Exp, bias=st[r0:r1, 4 + j:5 + j],
                                  scale=XSCALE if cross else 1.0, accum_out=st[r0:r1, 8 + j:9 + j])
                    last.then_inc(e_done.sem, 1)

                def copies(i):
                    kind, n = ITEMS[i]
                    t = pT[i % 2]
                    for b in range(BATCHES[i]):
                        act.wait_ge(t_psum.sem, t_psum.upto(l, BEFORE[i] + b + 1))
                        if kind == "diff_dec":
                            last = (fn(t[:, 512 * b:512 * b + 512], ps[:, 6, :], ACT.Copy) if b < 2 else
                                    fn(t[0:NS, 1024:1152], ps[0:NS, 6, 0:P], ACT.Copy))
                        elif kind == "win_dec":
                            fn(t[:, 0:384], ps[:, 6, 0:384], ACT.Copy)
                            last = fn(t[0:NS, 384:448], ps[0:NS, 6, 384:448], ACT.Copy)
                        else:
                            w = {"cross_dec": 128, "cross_pro": 512}.get(kind, 384)
                            last = fn(t[:, 0:w], ps[:, 6, 0:w], ACT.Copy)
                        last.then_inc(t_done.sem, 1)

                def attention(first, end):
                    exponentials(first)
                    for i in range(first, end):
                        copies(i)
                        if i + 1 < end:
                            exponentials(i + 1)

                ffn_gate(0)
                norm(0, before=(H_FM, H_FM + 1))
                for m in range(8):
                    high_half(H_FM + m + 2)
                    half_done(act, l, H_FM + m)
                    scale = {0: 64 ** -0.5, 2: 32 ** -0.5}.get(m // 2, 1.0)
                    fn(fm[:, m, :], ps[:, m % 2, 0:T], ACT.Copy, scale=scale).then_inc(fm_done.sem, 1)
                for q in range(H_TM + 2, H_OUT):
                    high_half(q)
                half_done(act, l, H_TM + 11)
                for g in range(3):
                    w = min(P, T - P * g)
                    fn(tmat(0, w, g, 1024, 512), ps[0:w, 2 + g, :], ACT.Silu).then_inc(tm_act.sem, 1)
                attention(0, len(MIXER))
                for b, dst, scale in ((0, qTp, 1.0), (1, kTp, 0.125)):
                    act.wait_ge(rt_psum.sem, rt_psum.upto(l, b + 1))
                    fn(view(dst, [[1, 512]]), ps[:, b, :], ACT.Copy, scale=scale).then_inc(rt_act.sem, 1)
                for g, bank in ((0, 6), (1, 7), (2, 3)):
                    act.wait_ge(ro_psum.sem, ro_psum.upto(l, 1 if g < 2 else 2))
                    w = min(P, T - P * g)
                    for h in range(HX):
                        last = fn(ytok[0:w, g, P * h:P * h + P], ps[0:w, bank, P * h:P * h + P], ACT.Square,
                                  accum_out=small[0:w, 12 + 4 * g + h:13 + 4 * g + h])
                last.then_inc(rsq_done.sem, 1)
                act.wait_ge(st_psum.sem, st_psum.upto(l, 1))
                fn(view(s_pro, [[1, 512]]), ps[0:64, 0, :], ACT.Copy).then_inc(st_act.sem, 1)
                act.wait_ge(rss_done.sem, rss_done.upto(l, 1))
                fn(small[:, 24:48], small[:, 0:24], ACT.Sqrt).then_inc(rsd_done.sem, 1)
                high_half(H_OUT)
                high_half(H_OUT + 1)
                act.wait_ge(rss_done.sem, rss_done.upto(l, 2))
                fn(small[0:NS, 32:36], small[0:NS, 8:12], ACT.Sqrt).then_inc(rsd_done.sem, 1)
                act.wait_ge(out_st.sem, out_st.upto(l, 32))
                for i, c in enumerate((0, 1, 2, 3, 6, 7)):
                    act.wait_ge(y_psum.sem, y_psum.upto(l, i + 1))
                    fn(x_high[:, c, :], ps[:, 6 + i % 2, 0:T], ACT.Copy).then_inc(y_high.sem, 1)
                act.wait_ge(y_done.sem, y_done.upto(l, 1))
                fn(x_high[:, 4:6, :], xT[:, 4:6, :], ACT.Copy).then_inc(y_high.sem, 1)
                for q in range(H_OUT + 2, H_OUT + 6):
                    high_half(q)
                act.wait_ge(mem_in.sem, mem_in.upto(l, 16))
                for i in range(2):
                    fn(mem_high[:, 4 * i:4 * i + 4, :], memT[:, 4 * i:4 * i + 4, :], ACT.Copy).then_inc(hi_mem.sem, 1)
                    high_half(H_OUT + 6 + i)
                norm(1, memory, before=range(H_MK, H_MK + 3))
                act.wait_ge(qc_zero.sem, qc_zero.upto(l, 1))
                for m in range(KD):
                    if m + 2 < KD:
                        high_half(H_XQ + m + 2)
                    half_done(act, l, H_XQ + m)
                    fn(qxT[:, m, :], ps[:, m % 2, 0:SEQ], ACT.Copy)
                    fn(qc[:, m, :, DT * (m // 2):DT * (m // 2) + DT],
                       ps[:, m % 2, SEQ:T].rearrange("p (b t) -> p b t", b=DB), ACT.Copy).then_inc(qx_act.sem, 1)
                attention(len(MIXER), NI)
                norm(2, before=range(H_XO, HALVES))
                ffn_gate(1)
                norm(3)

        @block.vector
        def _(dve):
            V = nc.vector
            dve.sem_inc(x_dve.sem, 1)
            dve.sem_inc(gate_done.sem, 2)
            own = [0]

            def own_step(ins):
                own[0] += 1
                ins.then_inc(own_set, 1)
                dve.wait_ge(own_set, own[0])

            V.memset(xh_pad[:, KD * T:KD * T + 64].bitcast(F32), 0.0)
            V.memset(xl_pad[:, KD * T:KD * T + 64].bitcast(F32), 0.0)
            V.memset(qd[:], 0.0)
            V.memset(qw[:], 0.0)
            V.memset(small[:], 1.0)
            V.memset(lnst[:], 1.0)
            V.memset(tok[:, 2, :], 0.0)
            V.memset(mean_var[:], 1.0)
            dve.wait_ge(bias_in, 16 * len(BIAS))
            dve.wait_ge(set_pe, 1)
            V.tensor_tensor(brow, banks(0, 0, NH, NU), counts, ALU.add).then_inc(set_dve, 1)
            dve.wait_ge(x_in, 16)
            V.tensor_scalar(yT[:], xT[:], ALPHA, None, ALU.mult)
            dve.wait_ge(small_in, 16 * (len(SMALL) + 2))
            lv = lamv[:, :, :, :]
            own_step(V.tensor_tensor(lamt.rearrange("p (l v d) -> p l v d", l=L, v=2), lv[:, :, 0::2, :], lv[:, :, 1::2, :],
                                     ALU.mult))
            V.tensor_reduce(small[:, 0:4], lamt.rearrange("p (a d) -> p a d", d=32), AX.X, ALU.add).then_inc(set_dve, 1)
            dve.wait_ge(set_act, 1)
            for i in range(L):
                own_step(V.tensor_tensor(params[:, i, 128:129], small[:, 5 + 2 * i:6 + 2 * i], small[:, 4 + 2 * i:5 + 2 * i],
                                         ALU.subtract))
                own_step(V.tensor_tensor(params[:, i, 128:129], params[:, i, 128:129], lconst[:, i:i + 1], ALU.subtract))
                V.scalar_tensor_tensor(params[:, i, 129:130], lconst[:, 5:6], params[:, i, 128:129], lconst[:, 4:5],
                                       ALU.mult, ALU.add)
                own_step(V.tensor_scalar(subg[:, i, :], subg[:, i, :], lconst[:, 2 + i:3 + i], None, ALU.mult))

            dve.wait_ge(set_pe, 2)
            V.tensor_copy(view(bias_pro[:, 0, 0:1], [[1, 2048]]), banks(3, 0, P, 2048)).then_inc(set_dve, 1)
            dve.wait_ge(set_pe, 3)
            V.tensor_copy(bias_dd[:], banks(0, 0, P, PAST))
            V.tensor_tensor(view(bias_dn[:, 0, 0:1], [[DT, 32], [1, DT]]), view(ps[:, 2, 0:1], [[0, 32], [1, DT]]),
                            view(mask_d[:, 0, 0:1], [[1, 32], [0, DT]]), ALU.add).then_inc(set_dve, 1)
            dve.wait_ge(set_pe, 4)
            V.tensor_copy(bias_wd[:, 0:256], ps[0:64, 0, 0:256])
            V.tensor_copy(bias_wd[:, 256:768], ps[0:64, 1, :])
            V.tensor_tensor(view(bias_wn[:, 0, 0:1], [[DT, 32], [1, DT]]), view(ps[0:64, 2, 0:1], [[0, 32], [1, DT]]),
                            view(mask_w[:, 0, 0:1], [[1, 32], [0, DT]]), ALU.add).then_inc(set_dve, 1)
            dve.wait_ge(const_in, 16 * len(CONSTS))
            with dve.Fori(0, L) as l:
                step = [0]

                def link(ins, alone=False):
                    step[0] += 1
                    ins.then_inc(dve_step.sem, 1)
                    if alone:
                        wait_apart(dve, "dve", dve_step.sem, dve_step.upto(l, step[0]))
                    else:
                        dve.wait_ge(dve_step.sem, dve_step.upto(l, step[0]))

                neglam, sign = cur[:, 128:129], cur[:, 129:130]

                def low_weights(f, s, add=0):
                    pos = (POS_FFN1, POS_FFN2)[f] + s
                    n = 2048 if s < NF else 11 * P
                    dve.wait_ge(hi_w.sem, hi_w.upto(l, FFN_SLOTS * f + s + 1) + add)
                    V.tensor_tensor(w_low[:, pos % 2, 0:n], ring[:, pos % RING, 0:n],
                                    w_high[:, pos % 2, 0:n].bitcast(F32), ALU.subtract).then_inc(lo_w.sem, 1)

                def low_half(q):
                    pos, place = POS_MIX + q // 2, int(q >= H_XO)
                    dve.wait_ge(hi_m.sem, hi_m.upto(l, q + 1))
                    V.tensor_tensor(m_low[place][:, q % 2, :], ring[:, pos % RING, 1024 * (q % 2):1024 * (q % 2) + 1024],
                                    m_high[place][:, q % 2, :].bitcast(F32), ALU.subtract).then_inc(lo_m.sem, 1)

                def low_x(u, pair):
                    dve.wait_ge(hi_x.sem, hi_x.upto(l, 4 * u + pair + 1))
                    c = slice(2 * pair, 2 * pair + 2)
                    V.tensor_tensor(x_low[:, c, :], xT[:, c, :], x_high[:, c, :].bitcast(F32), ALU.subtract)\
                        .then_inc(lo_x.sem, 1)

                def ffn_gate(u, pos0):
                    def chunk(j, i):
                        dve.wait_ge(silu_done.sem, silu_done.upto(l, NF * u + j + 1) + i)
                        dve.wait_ge(w_used.sem, w_used.upto(l, pos0 + j + 1) + i)
                        h, c = gate[:, j % 2:j % 2 + 1, :], bass.ds(i + j, 1)
                        V.tensor_tensor(h, h, ps[:, 2 * (j % 2) + 1:2 * (j % 2) + 2, 0:T], ALU.mult).then_inc(prod_done.sem, 1)
                        dve.wait_ge(prod_done.sem, prod_done.upto(l, NF * u + j + 1) + i)
                        V.tensor_copy(h_high[:, c, :], h).then_inc(hi_h.sem, 1)
                        dve.wait_ge(hi_h.sem, hi_h.upto(l, NF * u + j + 1) + i)
                        V.tensor_tensor(h_low[:, c, :], h, h_high[:, c, :].bitcast(F32), ALU.subtract)\
                            .then_inc(gate_done.sem, 1)
                        low_weights(u, j + 2, i)
                    whole = NF // RING * RING
                    with dve.Fori(0, whole // RING) as turn:
                        i = turn * RING
                        for j in range(RING):
                            chunk(j, i)
                    for j in range(whole, NF):
                        chunk(j, 0)

                def statistics(half):
                    for g in range(3):
                        w = min(P, T - P * g)
                        last = V.bn_stats(bn[0:w, g, half, :], ps[0:w, 2 + 2 * g + half, :])
                    return last

                def norm(u, scale, ready, fill=None, after=None, between=None):
                    for m in range(KD):
                        ready(m)
                        V.scalar_tensor_tensor(yT[:, m, :], ps[:, m % 2, 0:T], scale, yT[:, m, :], ALU.mult, ALU.add)\
                            .then_inc(res_done.sem, 1)
                        if after:
                            after(m)
                        if m == 6:
                            dve.wait_ge(tok_psum.sem, tok_psum.upto(l, 2 * u + 1))
                            statistics(0)
                    dve.wait_ge(tok_psum.sem, tok_psum.upto(l, 2 * u + 2))
                    link(statistics(1), alone=True)
                    for g in range(3):
                        w = min(P, T - P * g)
                        last = V.bn_aggr(mean_var[0:w, g, :], bn[0:w, g, :, :].rearrange("p a b -> p (a b)"))
                    link(last)
                    V.tensor_scalar(lnst[:, :, 0], mean_var[:, :, 1], LN_EPS, None, ALU.add).then_inc(var_done.sem, 1)
                    dve.wait_ge(sd_done.sem, sd_done.upto(l, u + 1))
                    link(V.reciprocal(lnst[:, :, 1], lnst[:, :, 1]))
                    V.scalar_tensor_tensor(lnst[:, :, 2], mean_var[:, :, 0], -1.0, lnst[:, :, 1], ALU.mult, ALU.mult)\
                        .then_inc(par_done.sem, 1)
                    for i in range(2):
                        for g in (0, 2):
                            w = min(P, T - P * g)
                            last = V.tensor_scalar(tok[0:w, g, 512 * i:512 * i + 512], ps[0:w, 2 + 2 * g + i, :],
                                                   mean_var[0:w, g, 0:1], lnst[0:w, g, 1:2], ALU.subtract, ALU.mult)
                        last.then_inc(norm_dve.sem, 1)
                    if fill:
                        fill()
                    for m in range(1, KD, 2):
                        dve.wait_ge(xt_psum.sem, xt_psum.upto(l, 8 * u + m + 1))
                        V.tensor_scalar(xT[:, m, :], ps[:, m % 4, 0:T], cur[:, 8 * u + m:8 * u + m + 1],
                                        cur[:, 64 + 8 * u + m:65 + 8 * u + m], ALU.mult, ALU.add).then_inc(x_dve.sem, 1)
                        if m == 3 and between:
                            between()
                        if m > 1:
                            behind(u, m // 2 - 1)
                    behind(u, 3)

                def behind(u, pair):
                    if pair % 2:
                        dve.wait_ge(x_dve.sem, x_dve.upto(l, 4 * u + pair + 1))
                        dve.wait_ge(x_act.sem, x_act.upto(l, 4 * u + pair + 1))
                        c = slice(2 * pair, 2 * pair + 2)
                        V.tensor_scalar(yT[:, c, :], xT[:, c, :], ALPHA, None, ALU.mult)
                    if u < 3:
                        low_x(u, pair)

                def ffn_out(f):
                    def ready(m):
                        if m < KD - 1:
                            low_weights(f, NF + 2 * m + 2)
                        dve.wait_ge(w_used.sem, w_used.upto(l, (POS_FFN1, POS_FFN2)[f] + NF + 2 * m + 2))

                    def after(m):
                        if m < KD - 1:
                            low_weights(f, NF + 2 * m + 3)
                    return ready, after

                def square_out(q0):
                    return lambda m: half_done(dve, l, q0 + m)

                def token_major(n, g):
                    half_done(dve, l, H_TM + 4 * n + 3)
                    w = min(P, T - P * g)
                    V.tensor_copy(tmat(0, w, g, 512 * n, 512), ps[0:w, 2 + 3 * (n % 2) + g, :]).then_inc(tm_dve.sem, 1)

                def rotate(g):
                    dve.wait_ge(tm_dve.sem, tm_dve.upto(l, 3))
                    def bc(t):
                        return view(t[:, g, 0:1], [[0, 8], [1, 32]])
                    def half(i):
                        return view(tmat(0, P, g, 32 * i, 1), [[64, 8], [1, 32]])
                    for i, (x, t) in enumerate(((0, cos), (1, sin), (0, sin), (1, cos))):
                        last = V.tensor_tensor(rp[i][:, g, :, :], half(x), bc(t), ALU.mult)
                    link(last)
                    V.tensor_tensor(half(0), rp[0][:, g, :, :], rp[1][:, g, :, :], ALU.subtract)
                    link(V.tensor_tensor(half(1), rp[2][:, g, :, :], rp[3][:, g, :, :], ALU.add))

                def spread_queries():
                    dve.wait_ge(fm_done.sem, fm_done.upto(l, 8))
                    for hp in range(2):
                        for m in range(2):
                            r = 64 * hp + 32 * m
                            V.tensor_copy(view(qd[r:r + 32, 0, 0, 16 * hp + 8 * m:16 * hp + 8 * m + 1],
                                               [[DB * 64 + 32, 2], [64, DB], [1, DT]]),
                                          view(fm[r:r + 32, 4, SEQ:SEQ + 1], [[T, 2], [DT, DB], [1, DT]]))
                    for hp in range(2):
                        r = 64 * hp
                        last = V.tensor_copy(view(qw[r:r + 64, 0, 0, DT * hp:DT * hp + 1],
                                                  [[DB * 32 + 2 * DT, 2], [32, DB], [1, DT]]),
                                             view(fm[r:r + 64, 0, SEQ:SEQ + 1], [[T, 2], [DT, DB], [1, DT]]))
                    last.then_inc(q_built.sem, 1)

                def maxima(i):
                    kind, n = ITEMS[i]
                    p, st, b0 = prob[i % 2], stat[:, i % 2, :], 3 * (i % 2)
                    if kind[:5] != "cross":
                        wait_apart(dve, "dve", s_psum.sem, s_psum.upto(l, i + 1))
                    else:
                        dve.wait_ge(s_psum.sem, s_psum.upto(l, i + 1))

                    def add_max(r1, at, w, src, bias, j):
                        return V.tensor_tensor_reduce(out=p[0:r1, at:at + w], in0=src, in1=bias, scale=1.0, scalar=LOW,
                                                      op0=ALU.add, op1=ALU.max, accum_out=st[0:r1, j:j + 1])
                    if kind in ("diff_dec", "win_dec"):
                        r1, w, past, new = (P, PAST, bias_dd, bias_dn) if kind == "diff_dec" else (64, WK, bias_wd, bias_wn)
                        add_max(r1, 0, w, banks(b0, 0, r1, w), past[:], 0)
                        link(add_max(r1, w, NS, banks(b0, 0, r1, w + NS)[:, w:w + NS], new[:, n, :], 1))
                        V.tensor_reduce(st[0:r1, 4:5], st[0:r1, 0:2], AX.X, ALU.max, negate=True).then_inc(m_done.sem, 1)
                    elif kind in ("win_pro", "diff_pro"):
                        h = n if kind == "win_pro" else HX + n
                        maps = 1 if kind == "win_pro" else 2
                        for m in range(maps):
                            add_max(P, 384 * m, 128, ps[:, b0 + m, 0:128], bias_pro[:, h, 128:256], 2 * m)
                            last = add_max(P, 384 * m + 128, 256, ps[:, b0 + m, 128:384], bias_pro[:, h, :], 2 * m + 1)
                        link(last)
                        V.tensor_scalar(st[:, 4:4 + 2 * maps], st[:, 0:2 * maps], -1.0, None, ALU.mult)\
                            .then_inc(m_done.sem, 1)
                    else:
                        r1, k = (64, 1) if kind == "cross_dec" else (P, 2)
                        link(V.tensor_reduce(st[0:r1, 0:k], ps[0:r1, b0, 0:256 * k].rearrange("p (a b) -> p a b", a=k),
                                             AX.X, ALU.max))
                        V.tensor_scalar(st[0:r1, 4:4 + k], st[0:r1, 0:k], -XSCALE, None, ALU.mult).then_inc(m_done.sem, 1)

                def normalise(i):
                    kind, n = ITEMS[i]
                    p, st = prob[i % 2], stat[:, i % 2, :]
                    dve.wait_ge(e_done.sem, e_done.upto(l, i + 1))
                    r1, k = {"diff_dec": (P, 1), "win_dec": (64, 1), "win_pro": (P, 2), "diff_pro": (P, 4),
                             "cross_dec": (64, 1), "cross_pro": (P, 2)}[kind]
                    link(V.reciprocal(st[0:r1, 12:12 + k], st[0:r1, 8:8 + k]))
                    if kind == "diff_dec":
                        link(V.tensor_tensor(st[:, 12:13], st[:, 12:13], sign, ALU.mult))
                    if kind == "diff_pro":
                        link(V.tensor_scalar(st[:, 14:16], st[:, 14:16], neglam, None, ALU.mult))
                    parts = {"diff_dec": [(0, PAST + NS)], "win_dec": [(0, WK + NS)], "win_pro": [(0, 128), (128, 256)],
                             "diff_pro": [(0, 128), (128, 256)], "cross_dec": [(0, 256)],
                             "cross_pro": [(0, 256), (256, 256)]}[kind]
                    for j, (at, w) in enumerate(parts):
                        last = V.tensor_scalar(p[0:r1, at:at + w], p[0:r1, at:at + w], st[0:r1, 12 + j:13 + j], None, ALU.mult)
                    if kind == "diff_pro":
                        link(last)
                        for j, (at, w) in enumerate(parts):
                            last = V.scalar_tensor_tensor(p[:, at:at + w], p[:, 384 + at:384 + at + w], st[:, 14 + j:15 + j],
                                                          p[:, at:at + w], ALU.mult, ALU.add)
                    last.then_inc(p_done.sem, 1)

                def outputs(i):
                    kind, n = ITEMS[i]
                    dve.wait_ge(o_psum.sem, o_psum.upto(l, i + 1))
                    if kind == "diff_dec":
                        last = V.tensor_tensor(own_d[n], ps[:, 7, 0:256], heads_d[:], ALU.mult)
                    elif kind == "win_dec":
                        last = V.tensor_tensor(own_w[n], ps[0:64, 7, 0:256], heads_w[:], ALU.mult)
                    elif kind == "win_pro":
                        r = 64 * (n % 2)
                        last = V.tensor_copy(xT[r:r + 64, 4 + n // 2, 0:256], ps[r:r + 64, 7, 0:256])
                    elif kind == "diff_pro":
                        last = V.tensor_copy(ytok[:, 0:2, 512 + 64 * n:576 + 64 * n],
                                             ps[:, 7, 0:128].rearrange("p (g e) -> p g e", g=2))
                    else:
                        if kind == "cross_dec":
                            c, t, w = slice(0, KD), slice(SEQ + 16 * n, SEQ + 16 * n + 16), 128
                        else:
                            c, t, w = slice(2 * n, 2 * n + 2), slice(0, SEQ), 512
                        out = ps[:, 7, 0:w].rearrange("p (c t) -> p c t", c=c.stop - c.start)
                        link(V.tensor_copy(x_high[:, c, t], out))
                        last = V.tensor_tensor(x_low[:, c, t], out, x_high[:, c, t].bitcast(F32), ALU.subtract)
                    last.then_inc(o_done.sem, 1)

                def own_heads(i):
                    n = ITEMS[i][1]
                    dve.wait_ge(xv_psum.sem, xv_psum.upto(l, n + 1))
                    for c in range(2):
                        last = V.tensor_tensor(own_x[i % 2][:, 512 * c:512 * c + 512], ps[0:64, 1 + 3 * (i % 2) + c, :],
                                               view(heads_w[:, 128 * c:128 * c + 1], [[64, 2], [0, 256]]), ALU.mult)
                    last.then_inc(xv_done.sem, 1)

                def attention(first, end):
                    maxima(first)
                    normalise(first)
                    for i in range(first, end):
                        if i + 1 < end:
                            maxima(i + 1)
                        elif end == NI:
                            low_half(H_XO)
                            low_half(H_XO + 1)
                        if i > first and ITEMS[i - 1][0] == "cross_dec":
                            outputs(i - 1)
                        if ITEMS[i][0] == "cross_dec":
                            own_heads(i)
                        else:
                            outputs(i)
                        if i + 1 < end:
                            normalise(i + 1)

                def retention():
                    dve.wait_ge(out_prj.sem, out_prj.upto(l, 32))
                    for g in range(2):
                        V.tensor_tensor(kd[:, g, :, :], view(tmat(0, P, g, 256, 1), [[64, HX], [1, 64]]),
                                        view(kdec[:, g, 0:1], [[1, HX], [0, 64]]), ALU.mult)
                    V.tensor_tensor(kx[:, :, :, :], view(tmat(0, NS, 2, 256, 1), [[64, HX], [0, DB], [1, 64]]),
                                    view(kmask[:, 0, 0:1], [[DB, HX], [1, DB], [0, 64]]), ALU.mult).then_inc(k_decayed.sem, 1)
                    dve.wait_ge(rt_psum.sem, rt_psum.upto(l, 3))
                    V.tensor_copy(view(qTs, [[1, 256]]), ps[0:64, 2, 0:256])
                    V.tensor_tensor(qx[:, :, :, :], view(ps[:, 2, 0:1], [[64, HX], [0, 4], [1, NS]]), qdec[:], ALU.mult)\
                        .then_inc(rt_dve.sem, 1)
                    dve.wait_ge(rt_psum.sem, rt_psum.upto(l, 4))
                    V.tensor_scalar(view(kTs, [[1, 256]]), ps[0:64, 3, 0:256], 0.125, None, ALU.mult).then_inc(rt_dve.sem, 1)
                    for h in range(HX):
                        dve.wait_ge(ra_psum.sem, ra_psum.upto(l, h + 1))
                        V.tensor_tensor(aT[h % 2][:, 0:256], ps[:, 4 + h % 2, 0:256], decay[:, h, :], ALU.mult)
                        V.tensor_tensor(aT[h % 2][:, 256:384], ps[:, 4 + h % 2, 256:384], decay[:, h, 0:128], ALU.mult)\
                            .then_inc(ra_done.sem, 1)
                    dve.wait_ge(ra_psum.sem, ra_psum.upto(l, 5))
                    V.tensor_tensor(view(aTs, [[1, 256]]), ps[0:NS, 2, 0:256], view(decay_s[:, 0, 0:1], [[1, 256]]), ALU.mult)\
                        .then_inc(ra_done.sem, 1)
                    dve.wait_ge(rsq_done.sem, rsq_done.upto(l, 1))
                    c, squares = ytok[:, 0:2, 512:768], ytok[:, 0:2, 0:256]
                    link(V.tensor_tensor(squares, c, c, ALU.mult))
                    link(V.tensor_reduce(small[:, 0:8].rearrange("p (g h) -> p g h", g=2),
                                         squares.rearrange("p g (h e) -> p g h e", e=64), AX.X, ALU.add))
                    V.tensor_scalar(small[:, 0:8], small[:, 0:8], 1.0 / 64, RMS_EPS, ALU.mult, ALU.add)
                    V.tensor_scalar(small[:, 12:24], small[:, 12:24], 1.0 / P, RMS_EPS, ALU.mult, ALU.add)\
                        .then_inc(rss_done.sem, 1)
                    dve.wait_ge(ro_psum.sem, ro_psum.upto(l, 2))
                    for g, bank in enumerate((1, 4, 5, 2)):
                        dve.wait_ge(st_psum.sem, st_psum.upto(l, g + 2))
                        for h in range(HX):
                            last = V.scalar_tensor_tensor(s_dec[:, g, h, :], s_dec[:, g, h, :], CHUNK_DECAY[h],
                                                          ps[:, bank, P * h:P * h + P], ALU.mult, ALU.add)
                        last.then_inc(st_dve.sem, 1)
                    dve.wait_ge(rsd_done.sem, rsd_done.upto(l, 1))
                    link(V.reciprocal(small[:, 24:48], small[:, 24:48]))
                    for g, bank in ((0, 6), (1, 7), (2, 3)):
                        w = min(P, T - P * g)
                        for h in range(HX):
                            last = V.scalar_tensor_tensor(ytok[0:w, g, P * h:P * h + P], ps[0:w, bank, P * h:P * h + P],
                                                          small[0:w, 36 + 4 * g + h:37 + 4 * g + h],
                                                          tmat(0, w, g, 1024 + P * h, P), ALU.mult, ALU.mult)
                    last.then_inc(ya_done.sem, 1)
                    dve.wait_ge(oc_psum.sem, oc_psum.upto(l, 1))
                    V.tensor_copy(xT[:, 4:6, SEQ:T], ps[:, 0, 256:384].rearrange("p (c t) -> p c t", c=2))
                    link(V.tensor_copy(ytok[0:NS, 2, 512:768], ps[0:NS, 0, 0:256]))
                    c = ytok[0:NS, 2, 512:768]
                    link(V.tensor_tensor(sq[0:NS, 0:256], c, c, ALU.mult))
                    link(V.tensor_reduce(small[0:NS, 8:12], sq[0:NS, 0:256].rearrange("p (a e) -> p a e", e=64), AX.X, ALU.add))
                    V.tensor_scalar(small[0:NS, 8:12], small[0:NS, 8:12], 1.0 / 64, RMS_EPS, ALU.mult, ALU.add)\
                        .then_inc(rss_done.sem, 1)
                    heads = view(ytok[:, 0, 512:513], [[768, 2], [64, HX], [1, 64]])
                    link(V.tensor_tensor(heads, heads, view(small[:, 24:25], [[HX, 2], [1, HX], [0, 64]]), ALU.mult))
                    V.tensor_tensor(heads, heads, view(curg[:, 0:1], [[0, 2], [0, HX], [1, 64]]), ALU.mult)
                    dve.wait_ge(rsd_done.sem, rsd_done.upto(l, 2))
                    link(V.reciprocal(small[0:NS, 32:36], small[0:NS, 32:36]))
                    heads = view(ytok[0:NS, 2, 512:513], [[64, HX], [1, 64]])
                    link(V.tensor_tensor(heads, heads, view(small[0:NS, 32:33], [[1, HX], [0, 64]]), ALU.mult))
                    V.tensor_tensor(heads, heads, view(curg[0:NS, 0:1], [[0, HX], [1, 64]]), ALU.mult)\
                        .then_inc(y_done.sem, 1)

                def y_low_parts():
                    low_half(H_OUT)
                    for i, c in enumerate((0, 1, 2, 3, 6, 7)):
                        dve.wait_ge(y_high.sem, y_high.upto(l, i + 1))
                        V.tensor_tensor(x_low[:, c, :], ps[:, 6 + i % 2, 0:T], x_high[:, c, :].bitcast(F32), ALU.subtract)\
                            .then_inc(y_low.sem, 1)
                    dve.wait_ge(y_high.sem, y_high.upto(l, 7))
                    V.tensor_tensor(x_low[:, 4:6, :], xT[:, 4:6, :], x_high[:, 4:6, :].bitcast(F32), ALU.subtract)\
                        .then_inc(y_low.sem, 1)
                    low_half(H_OUT + 1)

                def between_out(m):
                    low_half(H_OUT + m + 2)
                    if m in (4, 5):
                        i = m - 4
                        dve.wait_ge(hi_mem.sem, hi_mem.upto(l, i + 1))
                        V.tensor_tensor(mem_low[:, 4 * i:4 * i + 4, :], memT[:, 4 * i:4 * i + 4, :],
                                        mem_high[:, 4 * i:4 * i + 4, :].bitcast(F32), ALU.subtract).then_inc(lo_mem.sem, 1)

                def memory():
                    for q in range(H_MK + 2, H_MV + 6):
                        low_half(q)
                    for n in range(2):
                        half_done(dve, l, H_MV + 4 * n + 3)
                        for g in range(2):
                            V.tensor_copy(mvt[:, g, 512 * n:512 * n + 512], ps[:, g, :]).then_inc(mv_dve.sem, 1)
                        if n == 0:
                            for q in range(H_MV + 6, H_XQ + 2):
                                low_half(q)

                def between_xo(m):
                    if m < 6:
                        low_half(H_XO + m + 2)
                    else:
                        low_weights(1, m - 6)

                for pair in range(4):
                    low_x(-1, pair)
                low_weights(0, 0)
                low_weights(0, 1)
                dve.wait_ge(x_act.sem, x_act.upto(l, 0))
                V.tensor_copy(cur[:], params[:, bass.ds(l, 1), :].rearrange("p a c -> p (a c)"))
                V.tensor_copy(curg[:], subg[:, bass.ds(l, 1), :].rearrange("p a c -> p (a c)")).then_inc(cur_done.sem, 1)
                wait_apart(dve, "dve", cur_done.sem, cur_done.upto(l, 1))
                ffn_gate(0, POS_FFN1)
                ready, after = ffn_out(0)
                norm(0, 0.5, ready, None, after, lambda: low_half(H_FM))
                low_half(H_FM + 1)
                V.memset(tmat(64, P, 2, 0, 2048), 0.0)
                for q in range(H_FM + 2, H_TM + 2):
                    low_half(q)
                for j in range(4):
                    low_half(H_TM + j + 2)
                spread_queries()
                for n in range(3):
                    for g in range(3):
                        if n < 2:
                            token_major(n, g)
                        else:
                            rotate(g)
                        if H_TM + 4 * n + 6 + g < H_OUT:
                            low_half(H_TM + 4 * n + 6 + g)
                    if H_TM + 4 * n + 9 < H_OUT:
                        low_half(H_TM + 4 * n + 9)
                for g in range(3):
                    token_major(3, g)
                attention(0, len(MIXER))
                retention()
                y_low_parts()
                norm(1, 1.0, square_out(H_OUT), memory, between_out)
                V.memset(view(tok[:, 0, 0:1], [[1, 2048]]), 0.0).then_inc(qc_zero.sem, 1)
                for q in range(H_XQ + 2, H_XO):
                    low_half(q)
                attention(len(MIXER), NI)
                norm(2, 1.0, square_out(H_XO), after=between_xo)
                wait_apart(dve, "dve", out_mem.sem, out_mem.upto(l, 32))
                ffn_gate(1, POS_FFN2)
                ready, after = ffn_out(1)
                norm(3, 0.5, ready, after=after)
                assert step[0] == DVE_STEPS, step[0]


def constants():
    f = np.float32
    c = {}
    c["ident"] = np.eye(P, dtype=f)
    c["selJ"] = np.eye(P, dtype=f)[::-1].copy()
    sel_d, sel_w = np.zeros((32, P), f), np.zeros((32, 64), f)
    for h in range(HX):
        for t in range(DT):
            for b2 in range(2):
                for m in range(2):
                    sel_d[DT * h + DT - 1 - t, 64 * b2 + 16 * h + 8 * m + t] = 1
                sel_w[DT * h + DT - 1 - t, 32 * b2 + DT * h + t] = 1
    c["sel_d"], c["sel_w"] = sel_d, sel_w
    dist = OFF - np.arange(NU)
    n = np.maximum(dist, 0)
    half = NBUCKET // 2
    large = half + (np.log(np.maximum(n, 1).astype(f) / half) / math.log(128 / half) * half).astype(np.int32)
    bucket = np.where(n < half, n, np.minimum(large, NBUCKET - 1))
    c["onehot"] = (np.arange(NBUCKET)[:, None] == bucket[None]).astype(f)
    times = ((dist >= 0) & (dist <= 128)) * 1 + ((dist >= 0) & (dist <= 512) & (dist % 4 == 0)) \
        + ((dist >= 0) & (dist <= 2048) & (dist % 16 == 0))
    window = np.where(times > 0, np.log(np.maximum(times, 1)), NEG)
    causal = np.where(dist >= 0, 0.0, NEG)
    c["counts"] = np.stack([window] * HX + [causal] * HX).astype(f)
    for kind, rows, maps in (("d", 64, 2), ("w", 32, 1)):
        r = np.arange(2 * rows)
        head, b2 = r % rows // (DT * maps), r // rows
        c["heads_" + kind] = (head[:, None] == np.arange(256)[None] // 64).astype(f)
        token = DT * (2 * np.arange(4)[None] + b2[:, None]) + (r % DT)[:, None]
        c["token_" + kind] = (token[:, :, None] == np.arange(NS)).astype(f)
    for name, rows in (("mask_d", 64), ("mask_w", 32)):
        m = np.full((2 * rows, 4, DB), NEG, f)
        for g in range(4):
            for b2 in range(2):
                m[rows * b2:rows * b2 + rows, g, 2 * g + b2] = 0
        c[name] = m
    lg = np.log1p(-np.exp2(-5.0 - np.arange(HX)))
    i, j = np.arange(256), np.arange(P)
    rel = i[None] - j[:, None]
    c["decay"] = np.where(rel[:, None] >= 0, np.exp(lg[None, :, None] * np.maximum(rel, 0)[:, None]), 0).astype(f)
    s = np.arange(NS)
    rel = s[None] - s[:, None]
    same = (s[None] // DT == s[:, None] // DT) & (rel >= 0)
    c["decay_s"] = np.where(same[:, None], np.exp(lg[None, :, None] * np.maximum(rel, 0)[:, None]), 0).astype(f)
    part = np.arange(P) // 64
    pair = np.arange(4)
    own = (s // DT)[None, None, None, :] == (2 * pair[None, None, :, None] + part[:, None, None, None])
    c["qdec"] = (own * np.exp(lg[None, :, None, None] * (s % DT + 1.0)[None, None, None, :])).astype(f)
    c["kmask"] = ((s // DT)[:, None, None] == np.arange(DB)[None, None]) * \
        np.exp(lg[None, :, None] * (DT - 1.0 - s % DT)[:, None, None]) * 0.125
    c["kmask"] = c["kmask"].astype(f)
    tokn = np.arange(P)[:, None, None] + P * np.arange(2)[None, :, None]
    c["kdec"] = (np.exp(lg[None, None] * (SEQ - 1.0 - tokn)) * 0.125).astype(f)
    pos = np.zeros((3, P), f)
    pos[0], pos[1] = np.arange(P), P + np.arange(P)
    pos[2, :NS] = PAST + s % DT
    inv = (f(10000.0) ** (-np.arange(32, dtype=f) / f(32))).astype(f)
    ang = (pos.T[:, :, None] * inv[None, None]).astype(f)
    c["cos"], c["sin"] = np.cos(ang.astype(np.float64)).astype(f), np.sin(ang.astype(np.float64)).astype(f)
    lam = [0.8 - 0.6 * math.exp(-0.3 * i) for i in range(L)]
    row = np.zeros((P, 8), f)
    row[:, 0:2], row[:, 2:4] = lam, [1 - x for x in lam]
    m = (np.arange(P) // DT) % 2
    row[:, 4], row[:, 5] = m == 0, m == 1
    c["lconst"] = row
    return c


def kernel(**inputs):
    import concourse.bacc as _bacc
    from concourse.bass_utils import run_bass_kernel_spmd as _run

    x = {k: np.asarray(v) for k, v in inputs.items()}
    a = constants()

    def rows_of_features(t):
        return t.T.reshape(KD, P, -1).transpose(1, 0, 2)

    a["x"] = rows_of_features(np.concatenate([x["x_prompt"][0], x["x_sample"].reshape(NS, D)]))
    a["memT"] = rows_of_features(x["mem_prompt"][0])
    a["rel_bias"] = x["rel_bias"]
    a["diff_lambda"], a["diff_subln_g"] = x["diff_lambda"], x["diff_subln_g"]
    a["page_table"] = x["page_table"].reshape(1, -1)
    ln = [x[k].reshape(L, 4, KD, P).transpose(3, 0, 1, 2).reshape(P, L, 32) for k in ("ln_g", "ln_b")]
    a["ln"] = np.concatenate([ln[0], np.zeros_like(ln[0]), ln[1], np.zeros_like(ln[1])], 2)

    def stationary(w, cols):
        w = w[:, cols]
        n = w.shape[1] // P
        return w.reshape(KD, P, n, P).transpose(1, 2, 0, 3).reshape(P, n // 2, 2048).transpose(1, 0, 2)

    def moving(w, cols):
        w = w[:, cols]
        n = w.shape[1] // 512
        return w.reshape(2, 4, P, n, 512).transpose(3, 0, 2, 1, 4).reshape(2 * n, P, 2048)

    def gate_value(w):
        return w.reshape(KD, P, 2, NF, P).transpose(3, 1, 2, 0, 4).reshape(NF, P, 2048)

    def down(w):
        return w.reshape(2, 11, P, KD, P).transpose(3, 0, 2, 1, 4).reshape(16, P, 1408)

    every = np.arange(D)
    fcols = np.r_[1536:2048, 2304:2816]
    tcols = np.r_[0:1536, 2048:2304, 2816:3072]
    w16, w11 = [], []
    for l in range(L):
        w16 += [gate_value(x["ffn1_in"][l]), stationary(x["w_in"][l], fcols), moving(x["w_in"][l], tcols),
                stationary(x["w_out"][l], every), stationary(x["w_xk"][l], every), moving(x["w_xv"][l], every),
                stationary(x["w_xq"][l], every), stationary(x["w_xo"][l], every), gate_value(x["ffn2_in"][l])]
        w11 += [down(x["ffn1_out"][l]), down(x["ffn2_out"][l])]
    a["w16"], a["w11"] = np.concatenate(w16), np.concatenate(w11)

    n = x["cache_diff_k"].shape[0]
    a["dk"] = x["cache_diff_k"].reshape(n, L, PAGE, 2, P).transpose(0, 1, 4, 3, 2).reshape(n, L, P, 256)
    a["dv"] = x["cache_diff_v"].reshape(n, L, PAGE, 256)
    reach = np.r_[[i for i in range(512) if i % 16 < 8], 512:PAST].astype(int)
    a["wk"] = x["cache_win_k"][:, :, reach].reshape(DB, L, WK, 2, P).transpose(1, 0, 4, 3, 2).reshape(L, DB, P, 2 * WK)
    a["wv"] = x["cache_win_v"][:, :, reach].reshape(DB, L, WK // P, P, 256).transpose(1, 0, 3, 2, 4).reshape(L, DB, P, 2 * WK)
    a["ck"] = x["cache_mem_k"].reshape(DB, L, 256, KD, P).transpose(1, 0, 4, 3, 2).reshape(L, DB, P, 2048)
    a["cv"] = x["cache_mem_v"].reshape(DB, L, 2, P, D).transpose(1, 0, 3, 2, 4).reshape(L, DB, P, 2048)
    a["state"] = x["state_ret"].reshape(4, 2, L, HX, 64, P).transpose(2, 1, 4, 0, 3, 5).reshape(L, P, 2048)

    nc = _bacc.Bacc("TRN2", target_bir_lowering=False, num_devices=1)
    a = {k: np.ascontiguousarray(v) for k, v in a.items()}
    ins = {k: nc.dram_tensor(f"in_{k}", v.shape, mybir.dt.from_np(v.dtype), kind="ExternalInput").ap()
           for k, v in a.items()}
    ins["brow"] = nc.dram_tensor("bias_rows", [NH, NU], F32, kind="Internal").ap()
    shapes = {"x": [P, KD, T], "fm": [L, P, 2, 2 * T], "tm": [L, P, 3, 512], "s_pro": [L, 64, 512],
              "s_dec": [L, P, 2048], "mk": [L, P, 2048], "mv": [L, P, 2048]}
    outs = {k: nc.dram_tensor(f"out_{k}", s, F32, kind="ExternalOutput").ap() for k, s in shapes.items()}
    build(nc, ins, outs)
    r = _run(nc, [{f"in_{k}": v for k, v in a.items()}], core_ids=[0]).results[0]
    r = {k: np.asarray(r[f"out_{k}"]) for k in shapes}

    y = r["x"].transpose(2, 1, 0).reshape(T, D)
    fm = r["fm"].reshape(L, P, 2, 2, T).transpose(2, 0, 4, 3, 1).reshape(2, L, T, 256)
    tm = r["tm"].transpose(0, 2, 1, 3).reshape(L, 384, 512)[:, :T]
    bk, ck, bv, cv = fm[0], fm[1], tm[:, :, 0:256], tm[:, :, 256:512]

    def prompt(t):
        return t[None, :, :SEQ].reshape(1, L, SEQ, HX, 64)

    def decode(t):
        return t[:, SEQ:].reshape(L, DB, DT, HX, 64).transpose(1, 0, 2, 3, 4)

    p_ret = r["s_pro"].reshape(L, 64, HX, P).transpose(0, 2, 1, 3)[None]
    s_ret = r["s_dec"].reshape(L, 2, 64, 4, HX, P).transpose(3, 1, 0, 4, 2, 5).reshape(DB, L, HX, 64, P)
    mk = r["mk"].reshape(L, P, KD, 256).transpose(0, 3, 2, 1).reshape(1, L, 256, HX, 256)
    mv = r["mv"].reshape(L, P, 2, D).transpose(0, 2, 1, 3).reshape(1, L, 256, HX, 256)
    got = (y[None, :SEQ], y[SEQ:].reshape(DB, DT, D), prompt(ck), prompt(cv), prompt(bk), prompt(bv), p_ret, mk, mv,
           decode(ck), decode(cv), decode(bk), decode(bv), s_ret)
    return tuple(np.ascontiguousarray(t) for t in got)
```
